# Optimizing a Trainium2 kernel written in Bass

```python
import math
import jax
import jax.numpy as jnp
from jax import lax
import numpy as np

D_MODEL = 1024
BATCH = 1
SEQ = 2048
DEPTH = 1

MIX_WIDTH = D_MODEL
RWKV_WIDTH = MIX_WIDTH // 2
POOL_WIDTH = MIX_WIDTH - RWKV_WIDTH
HEAD_DIM = 64
RWKV_HEADS = RWKV_WIDTH // HEAD_DIM
DECAY_LORA = 64
AAA_LORA = 64
GATE_LORA = 128
POOL_WINDOWS = (2, 4, 8, 16)
POOL_GROUPS = len(POOL_WINDOWS)
POOL_GROUP_DIM = POOL_WIDTH // POOL_GROUPS
RWKV_COLS = 3 * RWKV_WIDTH + DECAY_LORA + AAA_LORA + GATE_LORA
IN_COLS = RWKV_COLS + POOL_WIDTH
RWKV_SPLITS = (RWKV_WIDTH, 2 * RWKV_WIDTH, 3 * RWKV_WIDTH,
               3 * RWKV_WIDTH + DECAY_LORA, 3 * RWKV_WIDTH + DECAY_LORA + AAA_LORA)
D_FF = 2816
CONV_WIDTH = 3
NORM_EPS = 1e-6
GN_EPS = 64e-5

kernel_name = 'hymba_rwkv7_pool_convffn'

def rms_norm(x, gain):
    xf = x.astype(jnp.float32)
    y = xf * lax.rsqrt(jnp.mean(xf * xf, axis=-1, keepdims=True) + NORM_EPS)
    return (y * gain.astype(jnp.float32)).astype(x.dtype)

def token_shift(u):
    return jnp.pad(u, ((0, 0), (1, 0), (0, 0)))[:, :-1]

def rwkv7_recurrence(r, w, k, v, a, b):
    bsz, _, n_heads, n = r.shape

    def step(state, inp):
        r_t, w_t, k_t, v_t, a_t, b_t = inp
        sa = jnp.einsum('bhvk,bhk->bhv', state, a_t)
        state = (state * w_t[:, :, None, :] + sa[..., None] * b_t[:, :, None, :]
                 + v_t[..., None] * k_t[:, :, None, :])
        y_t = jnp.einsum('bhvk,bhk->bhv', state, r_t)
        return state, y_t

    seq = (jnp.moveaxis(r, 1, 0), jnp.moveaxis(w, 1, 0), jnp.moveaxis(k, 1, 0),
           jnp.moveaxis(v, 1, 0), jnp.moveaxis(a, 1, 0), jnp.moveaxis(b, 1, 0))
    s0 = jnp.zeros((bsz, n_heads, n, n), jnp.float32)
    _, y = lax.scan(step, s0, seq)
    return jnp.moveaxis(y, 0, 1)

def rwkv7_group(u, mu_shift, w0, w_decay_up, a0, w_aaa_up, w_gate_up, k_k, k_a, r_k, ln_x_w, ln_x_b):
    bsz, t_len, _ = u.shape
    f = lambda p: p.astype(jnp.float32)
    u = u + f(mu_shift) * (token_shift(u) - u)
    r, k, v, wl, al, gl = jnp.split(u, RWKV_SPLITS, axis=-1)
    w_log = -jax.nn.softplus(-(f(w0) + jnp.tanh(wl) @ f(w_decay_up))) - 0.5
    decay = jnp.exp(-jnp.exp(w_log))
    alpha = jax.nn.sigmoid(f(a0) + al @ f(w_aaa_up))
    g = jax.nn.sigmoid(gl) @ f(w_gate_up)
    hs = lambda z: z.reshape(bsz, t_len, RWKV_HEADS, HEAD_DIM)
    kk = hs(k * f(k_k))
    kk = kk * lax.rsqrt(jnp.maximum(jnp.sum(kk * kk, axis=-1, keepdims=True), 1e-24))
    alpha_h = hs(alpha)
    k_mod = hs(k * (1.0 + (alpha - 1.0) * f(k_a)))
    r_h, v_h = hs(r), hs(v)
    y = rwkv7_recurrence(r_h, hs(decay), k_mod, v_h, -kk, kk * alpha_h)
    mean = jnp.mean(y, axis=-1, keepdims=True)
    var = jnp.mean(jnp.square(y - mean), axis=-1, keepdims=True)
    y = ((y - mean) * lax.rsqrt(var + GN_EPS) * f(ln_x_w).reshape(RWKV_HEADS, HEAD_DIM)
         + f(ln_x_b).reshape(RWKV_HEADS, HEAD_DIM))
    bonus = jnp.sum(r_h * k_mod * f(r_k), axis=-1, keepdims=True) * v_h
    return (y + bonus).reshape(bsz, t_len, RWKV_WIDTH) * g

def multiscale_pool(u, w_pool, pool_scale):
    bsz, t_len, _ = u.shape
    ug = u.reshape(bsz, t_len, POOL_GROUPS, POOL_GROUP_DIM)
    cs = lax.cumsum(ug, axis=1)
    pos = jnp.arange(t_len)
    outs = []
    for gi, win in enumerate(POOL_WINDOWS):
        c = cs[:, :, gi]
        lag = jnp.pad(c, ((0, 0), (win, 0), (0, 0)))[:, :t_len]
        cnt = jnp.minimum(pos + 1, win).astype(jnp.float32)[None, :, None]
        outs.append((c - lag) / cnt - ug[:, :, gi])
    pooled = jnp.stack(outs, axis=2)
    mixed = jnp.einsum('btgc,gcd->btgd', pooled, w_pool.astype(jnp.float32))
    return mixed.reshape(bsz, t_len, POOL_WIDTH) * pool_scale.astype(jnp.float32)

def conv_ffn(h, w_up, conv_w, conv_b, w_down):
    up = h @ w_up
    up = lax.conv_general_dilated(up, conv_w[:, None, :], window_strides=(1,),
                                  padding=((CONV_WIDTH - 1, 0),),
                                  dimension_numbers=('NWC', 'WIO', 'NWC'),
                                  feature_group_count=2 * D_FF) + conv_b
    gate, val = jnp.split(up, 2, axis=-1)
    return (jax.nn.gelu(gate, approximate=True) * val) @ w_down

def setup_inputs(seed: int = 0) -> dict:
    key = jax.random.key(seed)
    ks = jax.random.split(key, 24)
    n = lambda k, s: jax.random.normal(k, s, jnp.float32)
    L = DEPTH
    return {
        'x': n(ks[0], (BATCH, SEQ, D_MODEL)),
        'pre_mix_norm': 1.0 + 0.05 * n(ks[1], (L, D_MODEL)),
        'w_in': n(ks[2], (L, D_MODEL, IN_COLS)) * D_MODEL ** -0.5,
        'mu_shift': jax.random.uniform(ks[3], (L, RWKV_COLS), jnp.float32),
        'w0': -1.0 + 0.5 * n(ks[4], (L, RWKV_WIDTH)),
        'w_decay_up': n(ks[5], (L, DECAY_LORA, RWKV_WIDTH)) * 0.5 * DECAY_LORA ** -0.5,
        'a0': 0.1 * n(ks[6], (L, RWKV_WIDTH)),
        'w_aaa_up': n(ks[7], (L, AAA_LORA, RWKV_WIDTH)) * 0.5 * AAA_LORA ** -0.5,
        'w_gate_up': n(ks[8], (L, GATE_LORA, RWKV_WIDTH)) * GATE_LORA ** -0.5,
        'k_k': 0.85 + 0.05 * n(ks[9], (L, RWKV_WIDTH)),
        'k_a': 1.0 + 0.05 * n(ks[10], (L, RWKV_WIDTH)),
        'r_k': 0.1 * n(ks[11], (L, RWKV_HEADS, HEAD_DIM)),
        'ln_x_w': 1.0 + 0.05 * n(ks[12], (L, RWKV_WIDTH)),
        'ln_x_b': 0.01 * n(ks[13], (L, RWKV_WIDTH)),
        'w_pool': n(ks[14], (L, POOL_GROUPS, POOL_GROUP_DIM, POOL_GROUP_DIM)) * POOL_GROUP_DIM ** -0.5,
        'pool_scale': 1.0 + 0.05 * n(ks[15], (L, POOL_WIDTH)),
        'w_out': n(ks[16], (L, MIX_WIDTH, D_MODEL)) * MIX_WIDTH ** -0.5,
        'post_mix_norm': 1.0 + 0.05 * n(ks[17], (L, D_MODEL)),
        'pre_ffn_norm': 1.0 + 0.05 * n(ks[18], (L, D_MODEL)),
        'w_up': n(ks[19], (L, D_MODEL, 2 * D_FF)) * D_MODEL ** -0.5,
        'conv_w': n(ks[20], (L, CONV_WIDTH, 2 * D_FF)) * CONV_WIDTH ** -0.5,
        'conv_b': 0.01 * n(ks[21], (L, 2 * D_FF)),
        'w_down': n(ks[22], (L, D_FF, D_MODEL)) * D_FF ** -0.5,
        'post_ffn_norm': 1.0 + 0.05 * n(ks[23], (L, D_MODEL)),
    }

def reference(x, pre_mix_norm, w_in, mu_shift, w0, w_decay_up, a0, w_aaa_up, w_gate_up,
              k_k, k_a, r_k, ln_x_w, ln_x_b, w_pool, pool_scale, w_out, post_mix_norm,
              pre_ffn_norm, w_up, conv_w, conv_b, w_down, post_ffn_norm):
    for layer in range(DEPTH):
        h = rms_norm(x, pre_mix_norm[layer])
        proj = (h @ w_in[layer]).astype(jnp.float32)
        y_rwkv = rwkv7_group(proj[..., :RWKV_COLS], mu_shift[layer], w0[layer], w_decay_up[layer],
                             a0[layer], w_aaa_up[layer], w_gate_up[layer], k_k[layer], k_a[layer],
                             r_k[layer], ln_x_w[layer], ln_x_b[layer])
        y_pool = multiscale_pool(proj[..., RWKV_COLS:], w_pool[layer], pool_scale[layer])
        mixed = jnp.concatenate([y_rwkv, y_pool], axis=-1).astype(x.dtype) @ w_out[layer]
        x = x + rms_norm(mixed, post_mix_norm[layer])
        h = rms_norm(x, pre_ffn_norm[layer])
        f = conv_ffn(h, w_up[layer], conv_w[layer], conv_b[layer], w_down[layer])
        x = x + rms_norm(f, post_ffn_norm[layer])
    return x


_drawn_inputs = setup_inputs


def setup_inputs(seed=0):
    import zlib

    import numpy as np

    out = dict(_drawn_inputs(seed))
    spreads = {}
    factors = {'k_k': 8.0, 'ln_x_b': 8.0, 'conv_b': 6.668}
    for name, (base, spread) in spreads.items():
        noise = np.random.default_rng([zlib.crc32(name.encode()), seed]).standard_normal(out[name].shape)
        drawn = base * np.exp(spread * noise) if base else spread * noise
        out[name] = jnp.asarray(drawn.astype(out[name].dtype))
    for name, factor in factors.items():
        out[name] = (out[name] * factor).astype(out[name].dtype)
    return out
```

```python
import math
from contextlib import ExitStack

import numpy as np

import concourse.bass as bass
from concourse import mybir

F32 = mybir.dt.float32
F32R = mybir.dt.float32r
ALU = mybir.AluOpType
ACT = mybir.ActivationFunctionType
AX = mybir.AxisListType

P = 128
D_MODEL, SEQ = 1024, 2048
RWKV_WIDTH, POOL_WIDTH, HEAD_DIM = 512, 512, 64
DECAY_LORA = AAA_LORA = 64
GATE_LORA = 128
IN_COLS = 3 * RWKV_WIDTH + DECAY_LORA + AAA_LORA + GATE_LORA + POOL_WIDTH
D_FF = 2816
CONV_WIDTH = 3
NORM_EPS, GN_EPS = 1e-6, 64e-5

TB = 512
BLOCKS = SEQ // TB
TT = TB // P
KT = D_MODEL // P
FT = IN_COLS // P
PAIRS = RWKV_WIDTH // P
SHIFTED = 14
LORA, GATE, POOL0 = 12, 13, 14
HALO = 16
C = 32
SC = P
CH = SC // C
UNITS = PAIRS * CH
DBL = UNITS // 2
FF = D_FF // P
GROUP = 2
GROUPS = FF // GROUP


CONSTS = {}


def _layout():
    at = 0
    for name, shape in (("ident", (P,)), ("head_ones", (P,)), ("reset", (TB,)), ("cinv", (PAIRS, HALO)),
                        ("ident2", (HEAD_DIM,)), ("ident4", (C,)), ("strict", (C,)), ("causal", (C,)),
                        ("levels", (5, C)), ("rows_to_tokens", (2 * C,)), ("head_rows", (2,))):
        size = math.prod(shape)
        CONSTS[name] = (at, size, shape)
        at += size
    return at


CONST_COLS = _layout()


def constants():
    p = np.arange(P)[:, None]
    t = np.arange(C)[None, :]
    s = p % C
    parts = {
        "ident": p == np.arange(P)[None, :],
        "head_ones": p // HEAD_DIM == np.arange(P)[None, :] // HEAD_DIM,
        "reset": np.broadcast_to(np.arange(TB)[None, :] % C != 0, (P, TB)),
        "cinv": np.broadcast_to(1.0 / np.minimum(np.arange(HALO)[None, :] + 1, 2.0 ** np.arange(1, PAIRS + 1)[:, None]).reshape(1, -1),
                                (P, PAIRS * HALO)),
        "ident2": p % HEAD_DIM == np.arange(HEAD_DIM)[None, :],
        "ident4": s == t,
        "strict": s < t,
        "causal": s <= t,
        "levels": np.concatenate([(s >> (l + 1) == t >> (l + 1)) & ((s >> l) % 2 == 1) & ((t >> l) % 2 == 0)
                                  for l in range(5)], axis=1),
        "rows_to_tokens": (1 - p // HEAD_DIM) * C + s == np.arange(2 * C)[None, :],
        "head_rows": (p // C) % 2 == np.arange(2)[None, :],
    }
    return np.concatenate([np.asarray(parts[k], np.float32) for k in CONSTS], axis=1)


def const_view(a, name):
    at, size, shape = CONSTS[name]
    v = a["consts"][:, at:at + size]
    return v.rearrange("p (a b) -> p a b", b=shape[1]) if len(shape) == 2 else v


class Steps:

    def __init__(self, eng, sem, base=0):
        self.eng, self.sem, self.base, self.n = eng, sem, base, 0

    def do(self, ins):
        ins.then_inc(self.sem, 1)
        self.n += 1
        return self.n

    def wait(self, n=None):
        self.eng.wait_ge(self.sem, ONE + self.base + (self.n if n is None else n))

    def link(self, ins):
        self.do(ins)
        self.wait()


ONE = 1


def credit(nc, sems):
    with nc.Block() as block:
        @block.sync
        def _(sp):
            for s in sems:
                sp.sem_inc(s, ONE)


def split_matmul(nc, out, lhs_hi, lhs_lo, rhs_hi, rhs_lo, start, stop):
    nc.tensor.matmul(out, lhs_hi, rhs_hi, start=start, stop=False)
    nc.tensor.matmul(out, lhs_hi, rhs_lo, start=False, stop=False)
    return nc.tensor.matmul(out, lhs_lo, rhs_hi, start=False, stop=stop)


def phase_project(nc, a, scr):
    ctx, sems = ExitStack(), []
    with ctx:
        def sb(name, shape, dt=F32):
            return ctx.enter_context(nc.sbuf_tensor("p1_" + name, shape, dt))

        def sem(name):
            sems.append(ctx.enter_context(nc.semaphore("p1_" + name)))
            return sems[-1]

        xin = sb("xin", [P, TT, D_MODEL])
        hT_hi = sb("hT_hi", [P, KT, TB], F32R)
        hT_lo = sb("hT_lo", [P, KT, TB], F32R)
        w_raw = [sb(f"w_raw{i}", [P, KT, P]) for i in range(2)]
        w_hi = [sb(f"w_hi{i}", [P, KT, P], F32R) for i in range(2)]
        w_lo = [sb(f"w_lo{i}", [P, KT, P], F32R) for i in range(2)]
        proj = sb("proj", [P, FT, HALO + TB])
        um = sb("um", [P, SHIFTED, TB])
        dec = sb("dec", [P, PAIRS, TB])
        alpha = sb("alpha", [P, PAIRS, TB])
        cum = sb("cum", [P, PAIRS, TB])
        einv = sb("einv", [P, PAIRS, TB])
        kk = sb("kk", [P, PAIRS, TB])
        tmp = sb("tmp", [P, PAIRS, TB])
        gate = sb("gate", [P, PAIRS, TB])
        ident = sb("ident", [P, P])
        head_ones = sb("head_ones", [P, P])
        reset = sb("reset", [P, TB])
        cinv = sb("cinv", [P, PAIRS, HALO])
        wlora = sb("wlora", [P, RWKV_WIDTH])
        wgate = sb("wgate", [P, RWKV_WIDTH])
        wpool = sb("wpool", [P, PAIRS, P])
        gain = sb("gain", [P, KT])
        mu = sb("mu", [P, SHIFTED])
        par = sb("par", [P, 7, PAIRS])
        W0, A0, KKW, KA, RK, PSC, ONE_KA = range(7)
        ss = sb("ss", [P, TT])
        rstd = sb("rstd", [P, TT])
        eps = sb("eps", [P, 1])
        sA = tmp[:, 0:2, :].rearrange("p a t -> p (a t)")[:, 0:HALO + TB]
        sB = tmp[:, 2:4, :].rearrange("p a t -> p (a t)")[:, 0:HALO + TB]

        ptr = [ctx.enter_context(nc.psum_tensor(f"p1_ptr{i}", [P, TB], F32)) for i in range(2)]
        ppr = [ctx.enter_context(nc.psum_tensor(f"p1_ppr{i}", [P, TB], F32)) for i in range(2)]
        pm = ctx.enter_context(nc.psum_tensor("p1_pm", [P, 4, TB], F32))

        s_par = sem("params_loaded")
        s_const = sem("constants_built")
        s_x = [sem(f"x_loaded{t}") for t in range(TT)]
        s_xs = sem("x_scaled")
        s_ss = sem("sum_squares")
        s_sq = sem("rms_root")
        s_rs = sem("rms_recip")
        s_tr = sem("transposed")
        s_ht = sem("hT_ready")
        s_w = [sem(f"w_loaded{i}") for i in range(2)]
        s_wh = sem("w_hi_ready")
        s_wl = sem("w_lo_ready")
        s_pr = sem("proj_done")
        s_prf = sem("proj_read")
        s_halo = sem("halo_moved")
        s_diff = sem("shift_diff")
        s_um = sem("shifted")
        s_lora = sem("lora_act")
        s_mm = sem("small_matmul")
        s_mmr = sem("small_matmul_read")
        s_kkr = sem("kk_raw")
        s_sqk = sem("kk_squared")
        s_nmax = sem("kk_norm_max")
        s_nrt = sem("kk_norm_root")
        s_km = sem("k_modified")
        s_cum = sem("decay_sums")
        s_exp = sem("exps_ready")
        s_bon = sem("bonus_terms")
        s_out = sem("outputs_ready")
        s_store = sem("stored")
        s_poolin = sem("pool_in")
        s_pout = sem("pool_out_ready")
        s_pstore = sem("pool_stored")
        s_dve = sem("dve_step")

        xv = a["x"][0].rearrange("(t p) d -> p t d", p=P)
        wv = a["w_in"][0].rearrange("(k p) n -> p k n", p=P)
        NPAR = 12 + 4
        STORES = 7

        credit(nc, sems)
        with nc.Block() as block:
            @block.sync
            def _(sp):
                with nc.allow_non_contiguous_dma(reason="per-feature parameters, once"):
                    for dst, name in ((gain, "pre_mix_norm"), (mu, "mu_shift")):
                        sp.dma_start(dst[:, :], a[name][0].rearrange("(t p) -> p t", p=P)).then_inc(s_par, 16)
                    for i, name in ((W0, "w0"), (A0, "a0"), (KKW, "k_k"), (KA, "k_a"), (PSC, "pool_scale")):
                        sp.dma_start(par[:, i, :], a[name][0].rearrange("(t p) -> p t", p=P)).then_inc(s_par, 16)
                    sp.dma_start(par[:, RK, :], a["r_k"][0].rearrange("h d -> (h d)").rearrange("(t p) -> p t", p=P)
                                 ).then_inc(s_par, 16)
                    for dst, key in ((ident[:, :], "ident"), (head_ones[:, :], "head_ones"), (reset[:, :], "reset"),
                                     (cinv[:, :, :], "cinv")):
                        sp.dma_start(dst, const_view(a, key)).then_inc(s_par, 16)
                    sp.dma_start(wlora[0:DECAY_LORA, :], a["w_decay_up"][0]).then_inc(s_par, 16)
                    sp.dma_start(wlora[DECAY_LORA:P, :], a["w_aaa_up"][0]).then_inc(s_par, 16)
                    sp.dma_start(wgate[:, :], a["w_gate_up"][0]).then_inc(s_par, 16)
                    sp.dma_start(wpool[:, :, :], a["w_pool"][0].rearrange("g c d -> c g d")).then_inc(s_par, 16)
                with nc.sync.Fori(0, BLOCKS) as b:
                    for t in range(TT):
                        sp.wait_ge(s_tr, ONE + b * KT)
                        sp.dma_start(xin[:, t, :], xv[:, b * TT + t, :]).then_inc(s_x[t], 16)
                    with nc.sync.Fori(0, FT // 2) as f2:
                        for i in range(2):
                            sp.wait_ge(s_wh, ONE + b * FT + f2 * 2)
                            sp.wait_ge(s_wl, ONE + b * FT + f2 * 2)
                            sp.dma_start(w_raw[i][:, :, :], wv[:, :, bass.ds(f2 * (2 * P) + i * P, P)]).then_inc(s_w[i], 16)
                sp.wait_ge(s_store, ONE + 16 * STORES * BLOCKS)
                sp.wait_ge(s_pstore, ONE + 16 * BLOCKS)

            @block.gpsimd
            def _(gp):
                nc.gpsimd.memset(eps[:, :], NORM_EPS)
                nc.gpsimd.memset(proj[:, :, TB:TB + HALO], 0.0).then_inc(s_const, 1)
                gp.wait_ge(s_const, ONE + 1)
                with nc.gpsimd.Fori(0, BLOCKS) as b:
                    with nc.gpsimd.Fori(0, FT // 2) as f2:
                        for i in range(2):
                            n = b * FT + f2 * 2 + i
                            gp.wait_ge(s_w[i], ONE + (b * (FT // 2) + f2) * 16 + 16)
                            gp.wait_ge(s_wh, ONE + n + 1)
                            nc.gpsimd.tensor_tensor(w_lo[i][:, :, :], w_raw[i][:, :, :], w_hi[i][:, :, :].bitcast(F32),
                                                    ALU.subtract).then_inc(s_wl, 1)
                    gp.wait_ge(s_prf, ONE + (b + 1) * FT)
                    gp.wait_ge(s_store, ONE + b * (16 * STORES))
                    for f in (LORA, GATE, *range(LORA)):
                        nc.gpsimd.tensor_tensor(um[:, f, :], proj[:, f, HALO - 1:HALO - 1 + TB],
                                                proj[:, f, HALO:HALO + TB], ALU.subtract).then_inc(s_diff, 1)

            @block.scalar
            def _(act):
                act.wait_ge(s_const, ONE + 1)
                with nc.scalar.Fori(0, BLOCKS) as b:
                    for t in range(TT):
                        act.wait_ge(s_x[t], ONE + b * 16 + 16)
                        if t == 0:
                            act.wait_ge(s_store, ONE + b * (16 * STORES))
                        dump = (tmp if t < 2 else einv)[:, t % 2 * 2:t % 2 * 2 + 2, :].rearrange("p a t -> p (a t)")
                        nc.scalar.activation(dump, xin[:, t, :], ACT.Square,
                                             accum_out=ss[:, t:t + 1]).then_inc(s_ss, 1)
                    act.wait_ge(s_ss, ONE + b * TT + TT)
                    nc.scalar.activation(rstd[:, :], ss[:, :], ACT.Sqrt, scale=1.0 / D_MODEL, bias=eps[:, 0:1]).then_inc(s_sq, 1)
                    act.wait_ge(s_rs, ONE + b + 1)
                    for t in range(TT):
                        nc.scalar.activation(xin[:, t, :], xin[:, t, :], ACT.Copy, scale=rstd[:, t:t + 1]).then_inc(s_xs, 1)
                    def w_high(f2, i):
                        n = b * FT + f2 * 2 + i
                        act.wait_ge(s_w[i], ONE + (b * (FT // 2) + f2) * 16 + 16)
                        nc.scalar.activation(w_hi[i][:, :, :], w_raw[i][:, :, :], ACT.Copy).then_inc(s_wh, 1)

                    def read_proj(f2, i):
                        act.wait_ge(s_pr, ONE + b * FT + f2 * 2 + i + 1)
                        nc.scalar.activation(proj[:, bass.ds(f2 * 2 + i, 1), HALO:HALO + TB],
                                             ppr[i][:, :].rearrange("p (a t) -> p a t", a=1), ACT.Copy).then_inc(s_prf, 1)

                    w_high(0, 0)
                    act.wait_ge(s_poolin, ONE + b * PAIRS)
                    act.wait_ge(s_um, ONE + b * SHIFTED)
                    nc.scalar.activation(proj[:, :, 0:HALO], proj[:, :, TB:TB + HALO], ACT.Copy).then_inc(s_halo, 1)
                    act.wait_ge(s_halo, ONE + b + 1)
                    with nc.scalar.Fori(0, FT // 2 - 1) as f2:
                        w_high(f2, 1)
                        read_proj(f2, 0)
                        w_high(f2 + 1, 0)
                        read_proj(f2, 1)
                    w_high(FT // 2 - 1, 1)
                    read_proj(FT // 2 - 1, 0)
                    read_proj(FT // 2 - 1, 1)
                    act.wait_ge(s_um, ONE + b * SHIFTED + 1)
                    nc.scalar.activation(um[0:DECAY_LORA, LORA, :], um[0:DECAY_LORA, LORA, :], ACT.Tanh).then_inc(s_lora, 1)
                    act.wait_ge(s_um, ONE + b * SHIFTED + 2)
                    nc.scalar.activation(um[:, GATE, :], um[:, GATE, :], ACT.Sigmoid).then_inc(s_lora, 1)
                    for j in range(PAIRS):
                        act.wait_ge(s_mm, ONE + b * 6 + 1)
                        last = nc.scalar.activation(dec[:, j, :], pm[:, j, :], ACT.Sigmoid, bias=par[:, W0, j:j + 1])
                    last.then_inc(s_mmr, 1)
                    act.wait_ge(s_mm, ONE + b * 6 + 2)
                    for j in range(PAIRS):
                        last = nc.scalar.activation(alpha[:, j, :], pm[:, j, :], ACT.Sigmoid, bias=par[:, A0, j:j + 1])
                    last.then_inc(s_mmr, 1)
                    act.wait_ge(s_mm, ONE + b * 6 + 3)
                    act.wait_ge(s_pstore, ONE + b * 16)
                    nc.scalar.activation(gate[:, :, :], pm[:, :, :], ACT.Copy).then_inc(s_mmr, 1)
                    act.wait_ge(s_um, ONE + b * SHIFTED + 10)
                    for j in range(PAIRS):
                        last = nc.scalar.activation(kk[:, j, :], um[:, 4 + j, :], ACT.Copy, scale=par[:, KKW, j:j + 1])
                    last.then_inc(s_kkr, 1)
                    act.wait_ge(s_kkr, ONE + b + 1)
                    nc.scalar.activation(tmp[:, :, :], kk[:, :, :], ACT.Square).then_inc(s_sqk, 1)
                    act.wait_ge(s_nmax, ONE + b + 1)
                    nc.scalar.activation(tmp[:, :, :], tmp[:, :, :], ACT.Sqrt).then_inc(s_nrt, 1)
                    act.wait_ge(s_cum, ONE + b + 1)
                    act.wait_ge(s_km, ONE + b + 1)
                    nc.scalar.activation(einv[:, :, :], cum[:, :, :], ACT.Exp, scale=-1.0).then_inc(s_exp, 1)
                    nc.scalar.activation(dec[:, :, :], dec[:, :, :], ACT.Exp).then_inc(s_exp, 1)
                    act.wait_ge(s_exp, ONE + b * 3 + 1)
                    nc.scalar.activation(cum[:, :, :], cum[:, :, :], ACT.Exp).then_inc(s_exp, 1)
                    tok = bass.ds(b * TB, TB)
                    act.wait_ge(s_um, ONE + (b + 1) * SHIFTED)
                    act.dma_start(scr["v"][:, :, tok], um[:, 8:12, :]).then_inc(s_store, 16)
                    act.wait_ge(s_mmr, ONE + b * 3 + 3)
                    act.dma_start(scr["g"][:, :, tok], gate[:, :, :]).then_inc(s_store, 16)
                    for n, (src, dst) in enumerate(((um[:, 0:4, :], scr["rt"]), (dec[:, :, :], scr["at"]),
                                                    (alpha[:, :, :], scr["bt"]), (um[:, 4:8, :], scr["kt"]),
                                                    (tmp[:, :, :], scr["bonus"]))):
                        act.wait_ge(s_out, ONE + b * 5 + n + 1)
                        act.dma_start(dst[:, :, tok], src).then_inc(s_store, 16)
                    act.wait_ge(s_mm, ONE + b * 6 + 6)
                    act.wait_ge(s_store, ONE + (b + 1) * (16 * STORES))
                    for g in range(PAIRS):
                        last = nc.scalar.activation(gate[:, g, :], pm[:, g, :], ACT.Copy, scale=par[:, PSC, g:g + 1])
                    last.then_inc(s_pout, 1)
                    last = None
                    act.wait_ge(s_pout, ONE + b + 1)
                    act.dma_start(scr["mix"][:, PAIRS:2 * PAIRS, tok], gate[:, :, :]).then_inc(s_pstore, 16)

            @block.vector
            def _(dve):
                dve.wait_ge(s_par, ONE + 16 * NPAR)
                nc.vector.tensor_scalar(par[:, ONE_KA, :], par[:, KA, :], -1.0, 1.0, ALU.mult, ALU.add).then_inc(s_dve, 1)
                dve.wait_ge(s_dve, ONE + 1)
                K = 42
                with nc.vector.Fori(0, BLOCKS) as b:
                    st = Steps(dve, s_dve, b * K + 1)
                    dve.wait_ge(s_sq, ONE + b + 1)
                    nc.vector.reciprocal(rstd[:, :], rstd[:, :]).then_inc(s_rs, 1)
                    for k in range(KT):
                        dve.wait_ge(s_tr, ONE + b * KT + k + 1)
                        st.link(nc.vector.tensor_scalar(hT_hi[:, k, :], ptr[k % 2][:, :], gain[:, k:k + 1], None, ALU.mult))
                        nc.vector.scalar_tensor_tensor(hT_lo[:, k, :], ptr[k % 2][:, :], gain[:, k:k + 1],
                                                       hT_hi[:, k, :].bitcast(F32), ALU.mult, ALU.subtract
                                                       ).then_inc(s_ht, 1)
                    for n, f in enumerate((LORA, GATE, *range(LORA))):
                        dve.wait_ge(s_diff, ONE + b * SHIFTED + n + 1)
                        nc.vector.scalar_tensor_tensor(um[:, f, :], um[:, f, :], mu[:, f:f + 1],
                                                       proj[:, f, HALO:HALO + TB], ALU.mult, ALU.add).then_inc(s_um, 1)
                    dve.wait_ge(s_mmr, ONE + b * 3 + 1)
                    st.link(nc.vector.tensor_scalar(dec[:, :, :], dec[:, :, :], -math.exp(-0.5), None, ALU.mult))
                    for j in range(PAIRS):
                        st.do(nc.vector.tensor_tensor_scan(cum[:, j, :], reset[:, :], dec[:, j, :], 0.0, ALU.mult, ALU.add))
                    st.wait()
                    nc.vector.tensor_tensor(dec[:, :, :], cum[:, :, :], dec[:, :, :], ALU.subtract).then_inc(s_cum, 1)
                    dve.wait_ge(s_mmr, ONE + b * 3 + 2)
                    for j in range(PAIRS):
                        st.do(nc.vector.tensor_scalar(einv[:, j, :], alpha[:, j, :], par[:, KA, j:j + 1],
                                                      par[:, ONE_KA, j:j + 1], ALU.mult, ALU.add))
                    st.wait()
                    dve.wait_ge(s_um, ONE + b * SHIFTED + SHIFTED)
                    dve.wait_ge(s_kkr, ONE + b + 1)
                    nc.vector.tensor_tensor(um[:, 4:8, :], um[:, 4:8, :], einv[:, :, :], ALU.mult).then_inc(s_km, 1)
                    dve.wait_ge(s_km, ONE + b + 1)
                    dve.wait_ge(s_mm, ONE + b * 6 + 4)
                    nc.vector.tensor_scalar(tmp[:, :, :], pm[:, :, :], 1e-24, None, ALU.max).then_inc(s_nmax, 1)
                    dve.wait_ge(s_nrt, ONE + b + 1)
                    st.link(nc.vector.reciprocal(tmp[:, :, :], tmp[:, :, :]))
                    st.link(nc.vector.tensor_tensor(kk[:, :, :], kk[:, :, :], tmp[:, :, :], ALU.mult))
                    for j in range(PAIRS):
                        last = nc.vector.scalar_tensor_tensor(tmp[:, j, :], um[:, j, :], par[:, RK, j:j + 1],
                                                              um[:, 4 + j, :], ALU.mult, ALU.mult)
                    last.then_inc(s_bon, 1)
                    dve.wait_ge(s_exp, ONE + b * 3 + 3)
                    dve.wait_ge(s_bon, ONE + b + 1)
                    nc.vector.tensor_tensor(um[:, 0:4, :], um[:, 0:4, :], cum[:, :, :], ALU.mult).then_inc(s_out, 1)
                    nc.vector.tensor_copy(scr["pend"][:, :, bass.ds(b * (TB // C), TB // C)],
                                          cum[:, :, :].rearrange("p j (c t) -> p j c t", t=C)[:, :, :, C - 1])
                    nc.vector.scalar_tensor_tensor(dec[:, :, :].rearrange("p j t -> p (j t)"),
                                                   kk[:, :, :].rearrange("p j t -> p (j t)"), -1.0,
                                                   dec[:, :, :].rearrange("p j t -> p (j t)"),
                                                   ALU.mult, ALU.mult).then_inc(s_out, 1)
                    st.link(nc.vector.tensor_tensor(alpha[:, :, :], alpha[:, :, :], kk[:, :, :], ALU.mult))
                    nc.vector.tensor_tensor(alpha[:, :, :], alpha[:, :, :], einv[:, :, :], ALU.mult).then_inc(s_out, 1)
                    nc.vector.tensor_tensor(um[:, 4:8, :], um[:, 4:8, :], einv[:, :, :], ALU.mult).then_inc(s_out, 1)
                    dve.wait_ge(s_mm, ONE + b * 6 + 5)
                    nc.vector.tensor_tensor(tmp[:, :, :], pm[:, :, :], um[:, 8:12, :], ALU.mult).then_inc(s_out, 1)
                    dve.wait_ge(s_store, ONE + (b + 1) * (16 * STORES))
                    for g in range(PAIRS):
                        dve.wait_ge(s_poolin, ONE + b * PAIRS + g)
                        u = proj[:, POOL0 + g, :]
                        src, dst, other = u, sA, sB
                        for l in range(g + 1):
                            w = 1 << l
                            lo = 2 * w - 1
                            st.link(nc.vector.tensor_tensor(dst[:, lo:HALO + TB], src[:, lo:HALO + TB],
                                                            src[:, lo - w:HALO + TB - w], ALU.add))
                            src, dst, other = dst, other, dst
                        s = src[:, HALO:HALO + TB]
                        st.do(nc.vector.scalar_tensor_tensor(kk[:, g, HALO:TB], s[:, HALO:TB], 1.0 / 2 ** (g + 1),
                                                             u[:, 2 * HALO:HALO + TB], ALU.mult, ALU.subtract))
                        st.link(nc.vector.tensor_tensor(s[:, 0:HALO], s[:, 0:HALO], cinv[:, g, :], ALU.mult))
                        nc.vector.tensor_tensor(kk[:, g, 0:HALO], s[:, 0:HALO], u[:, HALO:2 * HALO],
                                                ALU.subtract).then_inc(s_poolin, 1)
                    dve.wait_ge(s_poolin, ONE + (b + 1) * PAIRS)
                    for g in range(PAIRS):
                        st.do(nc.vector.memset(cinv[:, g, :], 1.0 / 2 ** (g + 1)))
                    st.wait()
                    assert st.n == K, st.n

            @block.tensor
            def _(pe):
                pe.wait_ge(s_const, ONE + 1)
                pe.wait_ge(s_par, ONE + 16 * NPAR)
                with nc.tensor.Fori(0, BLOCKS) as b:
                    for k in range(KT):
                        if k == 0:
                            pe.wait_ge(s_xs, ONE + b * TT + TT)
                        if k >= 2:
                            pe.wait_ge(s_ht, ONE + b * KT + k - 1)
                        for t in range(TT):
                            last = nc.tensor.transpose(ptr[k % 2][:, t * P:(t + 1) * P], xin[:, t, k * P:(k + 1) * P], ident[:, :])
                        last.then_inc(s_tr, 1)
                    with nc.tensor.Fori(0, FT // 2) as f2:
                        for i in range(2):
                            pe.wait_ge(s_ht, ONE + b * KT + KT)
                            n = b * FT + f2 * 2 + i
                            pe.wait_ge(s_wh, ONE + n + 1)
                            pe.wait_ge(s_wl, ONE + n + 1)
                            pe.wait_ge(s_prf, ONE + b * FT + f2 * 2)
                            for k in range(KT):
                                last = split_matmul(nc, ppr[i][:, :], w_hi[i][:, k, :], w_lo[i][:, k, :],
                                                    hT_hi[:, k, :], hT_lo[:, k, :], k == 0, k == KT - 1)
                            last.then_inc(s_pr, 1)
                    pe.wait_ge(s_lora, ONE + b * 2 + 1)
                    for j in range(PAIRS):
                        last = nc.tensor.matmul(pm[:, j, :], wlora[0:64, j * P:(j + 1) * P], um[0:64, LORA, :], start=True, stop=True)
                    last.then_inc(s_mm, 1)
                    pe.wait_ge(s_mmr, ONE + b * 3 + 1)
                    for j in range(PAIRS):
                        last = nc.tensor.matmul(pm[:, j, :], wlora[64:128, j * P:(j + 1) * P], um[64:128, LORA, :], start=True, stop=True)
                    last.then_inc(s_mm, 1)
                    pe.wait_ge(s_lora, ONE + b * 2 + 2)
                    pe.wait_ge(s_mmr, ONE + b * 3 + 2)
                    for j in range(PAIRS):
                        last = nc.tensor.matmul(pm[:, j, :], wgate[:, j * P:(j + 1) * P], um[:, GATE, :], start=True, stop=True)
                    last.then_inc(s_mm, 1)
                    pe.wait_ge(s_sqk, ONE + b + 1)
                    pe.wait_ge(s_mmr, ONE + b * 3 + 3)
                    for j in range(PAIRS):
                        last = nc.tensor.matmul(pm[:, j, :], head_ones[:, :], tmp[:, j, :], start=True, stop=True)
                    last.then_inc(s_mm, 1)
                    pe.wait_ge(s_bon, ONE + b + 1)
                    for j in range(PAIRS):
                        last = nc.tensor.matmul(pm[:, j, :], head_ones[:, :], tmp[:, j, :], start=True, stop=True)
                    last.then_inc(s_mm, 1)
                    pe.wait_ge(s_out, ONE + b * 5 + 5)
                    pe.wait_ge(s_poolin, ONE + b * PAIRS + PAIRS)
                    for g in range(PAIRS):
                        last = nc.tensor.matmul(pm[:, g, :], wpool[:, g, :], kk[:, g, :], start=True, stop=True)
                    last.then_inc(s_mm, 1)


def phase_recur(nc, a, scr):
    ctx, sems = ExitStack(), []
    with ctx:
        def sb(name, shape, dt=F32):
            return ctx.enter_context(nc.sbuf_tensor("p2_" + name, shape, dt))

        def sem(name):
            sems.append(ctx.enter_context(nc.semaphore("p2_" + name)))
            return sems[-1]

        H = HEAD_DIM
        LEVELS = 5
        ar = sb("ar", [P, 2, PAIRS, SC])
        bt = sb("bt", [P, PAIRS, SC])
        kt = sb("kt", [P, PAIRS, SC])
        vt = sb("vt", [P, PAIRS, SC])
        bonus = sb("bonus", [P, PAIRS, SC])
        gate = sb("gate", [P, PAIRS, SC])
        bk = sb("bk", [P, PAIRS, CH, P])
        wr = sb("wr", [P, PAIRS, CH, P])
        ab = sb("ab", [P, PAIRS, CH // 2, P])
        vb = sb("vb", [P, PAIRS, CH // 2, P])
        aab = sb("aab", [P, DBL, P])
        aak = sb("aak", [P, DBL, P])
        ark = sb("ark", [P, UNITS, 2 * C])
        x = sb("x", [P, DBL, C])
        xm = sb("xm", [P, DBL, C])
        xt = sb("xt", [P, DBL, P])
        t1 = sb("t1", [P, DBL, C])
        atm = sb("atm", [P, DBL, P])
        bkt = sb("bkt", [P, UNITS, P])
        vd = sb("vd", [P, DBL, H])
        uv = sb("uv", [P, PAIRS, CH, H])
        z0 = sb("z0", [P, DBL, H])
        z = sb("z", [P, PAIRS, CH // 2, H])
        state = sb("state", [P, PAIRS, H])
        sumst = sb("sumst", [P, PAIRS, H])
        pq = sb("pq", [P, PAIRS, CH])
        y = sb("y", [P, PAIRS, CH // 2, H])
        y2 = sb("y2", [P, DBL, H])
        yb = sb("yb", [P, DBL, 2, H])
        stat = sb("stat", [P, 3, DBL])
        mo = sb("mo", [P, PAIRS, SC])
        geps = sb("geps", [P, 1])
        ident = sb("ident", [P, P])
        ident2 = sb("ident2", [P, H])
        ident4 = sb("ident4", [P, C])
        strict = sb("strict", [P, C])
        causal = sb("causal", [P, C])
        levels = sb("levels", [P, LEVELS, C])
        rows = sb("rows", [P, 2 * C])
        hrow = sb("hrow", [P, 2])
        lnw = sb("lnw", [P, PAIRS])
        lnb = sb("lnb", [P, PAIRS])
        bank = ctx.enter_context(nc.psum_tensor("p2_bank", [P, 8, 512], F32))

        s_par = sem("params_loaded")
        s_const = sem("zeros_written")
        s_in = sem("inputs_loaded")
        s_in2 = sem("bonus_gate_loaded")
        s_bk = sem("bk_built")
        s_rb = sem("r_built")
        s_av = sem("a_v_built")
        s_gram = sem("gram_done")
        s_aab = sem("aab_masked")
        s_gr = sem("gram_read")
        s_vst = sem("v_stacked")
        s_vr = sem("v_read")
        s_bkt = sem("bk_transposed")
        s_bktr = sem("bkt_read")
        s_at = sem("a_transposed")
        s_atr = sem("atm_read")
        s_t1 = sem("t1_done")
        s_t1r = sem("t1_read")
        s_x2 = sem("x_product")
        s_xc = sem("x_updated")
        s_xt = sem("x_transposed")
        s_z0 = sem("z0_done")
        s_z0r = sem("z0_read")
        s_z = sem("z_done")
        s_zr = sem("z_read")
        s_w = sem("w_done")
        s_wr = sem("w_read")
        s_p1 = sem("state_products")
        s_u = sem("u_ready")
        s_s = sem("state_update")
        s_sn = sem("state_ready")
        s_y = sem("y_done")
        s_yr = sem("y_read")
        s_sq = sem("y_squared")
        s_var = sem("y_var")
        s_sd = sem("y_deviation")
        s_yb = sem("y_blocks")
        s_yt = sem("y_back")
        s_aff = sem("y_affine")
        s_mo = sem("mix_ready")
        s_mix = sem("mix_stored")
        s_dve = sem("dve_step")
        s_yc = sem("y_centred")
        s_go = sem("gpsimd_started")

        def vrows(e):
            return slice(0, 64) if e else slice(64, 128)

        def urows(e):
            return slice(64, 128) if e else slice(0, 64)

        credit(nc, sems)
        with nc.Block() as block:
            @block.sync
            def _(sp):
                with nc.allow_non_contiguous_dma(reason="per-feature parameters, once"):
                    for dst, name in ((lnw, "ln_x_w"), (lnb, "ln_x_b")):
                        sp.dma_start(dst[:, :], a[name][0].rearrange("(t p) -> p t", p=P)).then_inc(s_par, 16)
                    for dst, key in ((ident[:, :], "ident"), (ident2[:, :], "ident2"), (ident4[:, :], "ident4"),
                                     (strict[:, :], "strict"), (causal[:, :], "causal"), (levels[:, :, :], "levels"),
                                     (rows[:, :], "rows_to_tokens"), (hrow[:, :], "head_rows")):
                        sp.dma_start(dst, const_view(a, key)).then_inc(s_par, 16)
                with nc.sync.Fori(0, SEQ // SC) as q:
                    tok = bass.ds(q * SC, SC)
                    sp.wait_ge(s_gram, ONE + q)
                    sp.wait_ge(s_bk, ONE + q * 8)
                    sp.wait_ge(s_av, ONE + q * 8)
                    sp.wait_ge(s_rb, ONE + q * 4)
                    for dst, key in ((bt[:, :, :], "bt"), (kt[:, :, :], "kt"), (ar[:, 0, :, :], "at"),
                                     (ar[:, 1, :, :], "rt"), (vt[:, :, :], "v")):
                        sp.dma_start(dst, scr[key][:, :, tok]).then_inc(s_in, 16)
                    sp.wait_ge(s_mo, ONE + q)
                    for dst, key in ((bonus[:, :, :], "bonus"), (gate[:, :, :], "g")):
                        sp.dma_start(dst, scr[key][:, :, tok]).then_inc(s_in2, 16)
                    sp.wait_ge(s_mo, ONE + q + 1)
                    sp.dma_start(scr["mix"][:, 0:PAIRS, tok], mo[:, :, :]).then_inc(s_mix, 16)
                sp.wait_ge(s_mix, ONE + 16 * (SEQ // SC))

            @block.gpsimd
            def _(gp):
                for m in (bk, wr, ab, vb, aab, aak, ark, xt):
                    nc.gpsimd.memset(m[:], 0.0)
                nc.gpsimd.memset(geps[:, :], GN_EPS)
                nc.gpsimd.memset(state[:, :, :], 0.0).then_inc(s_const, 1)
                gp.wait_ge(s_const, ONE + 1)
                with nc.gpsimd.Fori(0, SEQ // SC) as q:
                    gp.wait_ge(s_in, ONE + q * 80 + 80)
                    gp.wait_ge(s_bkt, ONE + q)
                    gp.sem_inc(s_go, 1)
                    for e in range(2):
                        for kind, src in ((e, bt), (1 - e, kt)):
                            for h in range(2):
                                off = 64 * kind + 32 * h
                                nc.gpsimd.tensor_copy(
                                    bk[64 * h:64 * h + 64, :, :, off:off + C].rearrange("p j (c e) t -> p j c e t", e=2)[:, :, :, e, :],
                                    src[64 * h:64 * h + 64, :, :].rearrange("p j (c e t) -> p j c e t", e=2, t=C)[:, :, :, e, :]
                                ).then_inc(s_bk, 1)
                    gp.wait_ge(s_yc, ONE + q + 1)
                    nc.gpsimd.tensor_tensor(y2[:, :, :], y[:].rearrange("p j c v -> p (j c) v"),
                                            y[:].rearrange("p j c v -> p (j c) v"), ALU.mult).then_inc(s_sq, 1)
                    gp.wait_ge(s_in2, ONE + q * 32 + 32)
                    gp.wait_ge(s_aff, ONE + q + 1)
                    nc.gpsimd.tensor_tensor(mo[:, :, :], mo[:, :, :], bonus[:, :, :], ALU.add).then_inc(s_const, 1)
                    gp.wait_ge(s_const, ONE + q + 2)
                    nc.gpsimd.tensor_tensor(mo[:, :, :], mo[:, :, :], gate[:, :, :], ALU.mult).then_inc(s_mo, 1)

            @block.scalar
            def _(act):
                act.wait_ge(s_const, ONE + 1)
                act.wait_ge(s_par, ONE + 160)
                with nc.scalar.Fori(0, SEQ // SC) as q:
                    act.wait_ge(s_in, ONE + q * 80 + 80)
                    for e in range(2):
                        for h in range(2):
                            off = 64 * e + 32 * h
                            nc.scalar.activation(
                                ab[64 * h:64 * h + 64, :, :, off:off + C],
                                ar[64 * h:64 * h + 64, 0, :, :].rearrange("p j (c e t) -> p j c e t", e=2, t=C)[:, :, :, e, :],
                                ACT.Copy).then_inc(s_av, 1)
                    for e in range(2):
                        for h in range(2):
                            off = 64 * (1 - e) + 32 * h
                            nc.scalar.activation(
                                vb[64 * h:64 * h + 64, :, :, off:off + C],
                                vt[64 * h:64 * h + 64, :, :].rearrange("p j (c e t) -> p j c e t", e=2, t=C)[:, :, :, e, :],
                                ACT.Copy).then_inc(s_av, 1)
                    act.wait_ge(s_vst, ONE + q + 1)
                    nc.scalar.activation(vd[:, :, :], bank[:, 5, :].rearrange("p (d v) -> p d v", v=H), ACT.Copy)
                    for e in range(2):
                        last = nc.scalar.activation(
                            uv[:].rearrange("p j (c e) v -> p j c e v", e=2)[vrows(e), :, :, e, :],
                            bank[vrows(e), 5, :].rearrange("p (j c v) -> p j c v", j=PAIRS, v=H), ACT.Copy)
                    last.then_inc(s_vr, 1)
                    act.wait_ge(s_bkt, ONE + q + 1)
                    nc.scalar.activation(bkt[:, :, :], bank[:, 0:4, :].rearrange("p b (u k) -> p (b u) k", k=P), ACT.Copy).then_inc(s_bktr, 1)
                    act.wait_ge(s_at, ONE + q + 1)
                    nc.scalar.activation(atm[:, :, :], bank[:, 4:6, :].rearrange("p b (u k) -> p (b u) k", k=P), ACT.Copy).then_inc(s_atr, 1)
                    for l in range(1, LEVELS):
                        act.wait_ge(s_t1, ONE + q * 4 + l)
                        nc.scalar.activation(t1[:, :, :], bank[:, 7, 0:DBL * C].rearrange("p (d s) -> p d s", s=C), ACT.Copy).then_inc(s_t1r, 1)
                    act.wait_ge(s_z0, ONE + q + 1)
                    nc.scalar.activation(z0[:, :, :], bank[:, 5, :].rearrange("p (d v) -> p d v", v=H), ACT.Copy).then_inc(s_z0r, 1)
                    act.wait_ge(s_w, ONE + q + 1)
                    for e in range(2):
                        last = nc.scalar.activation(
                            wr[:].rearrange("p j (c e) n -> p j c e n", e=2)[:, :, :, e, 64 * e:64 * e + 64],
                            bank[:, 6:8, :].rearrange("p b (j c n) -> p (b j) c n", j=2, n=P)[:, :, :, 64 * e:64 * e + 64], ACT.Copy)
                    last.then_inc(s_wr, 1)
                    act.wait_ge(s_z, ONE + q + 1)
                    nc.scalar.activation(z[:, :, :, :], bank[:, 4, :].rearrange("p (j c v) -> p j c v", j=PAIRS, v=H), ACT.Copy).then_inc(s_zr, 1)
                    act.wait_ge(s_y, ONE + q * CH + CH)
                    for e in range(2):
                        last = nc.scalar.activation(
                            y[vrows(e), :, :, :],
                            bank[vrows(e), 0:4, 0:256].rearrange("p j (c e v) -> p j c e v", e=2, v=H)[:, :, :, e, :], ACT.Copy)
                    last.then_inc(s_yr, 1)
                    act.wait_ge(s_var, ONE + q + 1)
                    nc.scalar.activation(stat[:, 1, :], stat[:, 1, :], ACT.Sqrt, scale=1.0 / H, bias=geps[:, 0:1]).then_inc(s_sd, 1)
                    act.wait_ge(s_yt, ONE + q + 1)
                    act.wait_ge(s_mix, ONE + q * 16)
                    for j in range(PAIRS):
                        last = nc.scalar.activation(mo[:, j, :], bank[:, 5, j * SC:(j + 1) * SC], ACT.Identity,
                                                    scale=lnw[:, j:j + 1], bias=lnb[:, j:j + 1])
                    last.then_inc(s_aff, 1)

            @block.vector
            def _(dve):
                dve.wait_ge(s_par, ONE + 160)
                dve.wait_ge(s_const, ONE + 1)
                K = 14
                with nc.vector.Fori(0, SEQ // SC) as q:
                    st = Steps(dve, s_dve, q * K)
                    st.do(nc.vector.tensor_copy(pq[:, :, :], scr["pend"][:, :, bass.ds(q * CH, CH)]))
                    dve.wait_ge(s_in, ONE + q * 80 + 80)
                    for e in range(2):
                        for h in range(2):
                            off = 64 * (1 - e) + 32 * h
                            nc.vector.tensor_copy(
                                wr[:].rearrange("p j (c e) n -> p j c e n", e=2)[64 * h:64 * h + 64, :, :, e, off:off + C],
                                ar[64 * h:64 * h + 64, 1, :, :].rearrange("p j (c e t) -> p j c e t", e=2, t=C)[:, :, :, e, :]
                            ).then_inc(s_rb, 1)
                    dve.wait_ge(s_gram, ONE + q + 1)
                    g = bank[:, 6:8, :].rearrange("p b (j c n) -> p (b j) c n", j=2, n=2 * C)
                    g = g.rearrange("p j (c e) n -> p j c e n", e=2)
                    for p in range(4):
                        e, r = p // 2, slice(32 * p, 32 * p + 32)
                        m = strict[r, :].unsqueeze(1).unsqueeze(1).to_broadcast([32, PAIRS, CH // 2, C])
                        last = nc.vector.tensor_tensor(
                            aab[r, :, 32 * p:32 * p + 32].rearrange("p (j c) t -> p j c t", c=CH // 2), g[r, :, :, e, 0:C], m, ALU.mult)
                    last.then_inc(s_aab, 1)
                    for p in range(4):
                        e, r, col = 1 - p // 2, slice(32 * p, 32 * p + 32), 32 * ((p + 2) % 4)
                        m = strict[r, :].unsqueeze(1).unsqueeze(1).to_broadcast([32, PAIRS, CH // 2, C])
                        nc.vector.tensor_tensor(
                            aak[r, :, col:col + 32].rearrange("p (j c) t -> p j c t", c=CH // 2), g[r, :, :, e, 0:C], m, ALU.mult)
                    g2 = bank[:, 6:8, :].rearrange("p b (u n) -> p (b u) n", n=2 * C)
                    for p in range(4):
                        r = slice(32 * p, 32 * p + 32)
                        m = causal[r, :].unsqueeze(1).to_broadcast([32, UNITS, C])
                        last = nc.vector.tensor_tensor(ark[r, :, 32 * (p % 2):32 * (p % 2) + 32], g2[r, :, C:2 * C], m, ALU.mult)
                    last.then_inc(s_gr, 1)
                    for l in range(LEVELS):
                        dve.wait_ge(s_x2, ONE + q * LEVELS + l + 1)
                        m = levels[:, l, :].unsqueeze(1).to_broadcast([P, DBL, C])
                        st.link(nc.vector.tensor_tensor(xm[:, :, :], bank[:, 6, 0:DBL * C].rearrange("p (d s) -> p d s", s=C), m, ALU.mult))
                        base = x[:, :, :] if l else ident4[:, :].unsqueeze(1).to_broadcast([P, DBL, C])
                        nc.vector.tensor_tensor(x[:, :, :], xm[:, :, :], base, ALU.add).then_inc(s_xc, 1)
                        dve.wait_ge(s_xc, ONE + q * LEVELS + l + 1)
                        for p in range(4):
                            r = slice(32 * p, 32 * p + 32)
                            last = nc.vector.transpose(xt[r, :, 32 * p:32 * p + 32], x[r, :, :])
                        last.then_inc(s_xt, 1)
                    dve.wait_ge(s_zr, ONE + q + 1)
                    for c in range(CH):
                        e = c % 2
                        dve.wait_ge(s_p1, ONE + q * CH + c + 1)
                        nc.vector.tensor_tensor(uv[urows(e), :, c, :], bank[urows(e), 0:4, c * H:(c + 1) * H],
                                                z[urows(e), :, c // 2, :], ALU.add).then_inc(s_u, 1)
                        dve.wait_ge(s_s, ONE + q * CH + c + 1)
                        st.link(nc.vector.tensor_tensor(sumst[:, :, :], bank[:, 4, 0:PAIRS * H].rearrange("p (j v) -> p j v", v=H),
                                                        state[:, :, :], ALU.add))
                        nc.vector.tensor_tensor(state[:, :, :], sumst[:, :, :],
                                                pq[:, :, c:c + 1].to_broadcast([P, PAIRS, H]), ALU.mult).then_inc(s_sn, 1)
                        dve.wait_ge(s_sn, ONE + q * CH + c + 1)
                    yv = y[:].rearrange("p j c v -> p (j c) v")
                    dve.wait_ge(s_yr, ONE + q + 1)
                    st.link(nc.vector.tensor_reduce(stat[:, 0, :], yv, AX.X, ALU.add))
                    st.link(nc.vector.tensor_scalar(stat[:, 0, :], stat[:, 0, :], -1.0 / H, None, ALU.mult))
                    nc.vector.tensor_tensor(yv, yv, stat[:, 0, :].unsqueeze(2).to_broadcast([P, DBL, H]), ALU.add).then_inc(s_yc, 1)
                    dve.wait_ge(s_sq, ONE + q + 1)
                    nc.vector.tensor_reduce(stat[:, 1, :], y2[:, :, :], AX.X, ALU.add).then_inc(s_var, 1)
                    dve.wait_ge(s_sd, ONE + q + 1)
                    st.link(nc.vector.reciprocal(stat[:, 2, :], stat[:, 1, :]))
                    st.link(nc.vector.tensor_tensor(y2[:, :, :], yv, stat[:, 2, :].unsqueeze(2).to_broadcast([P, DBL, H]), ALU.mult))
                    for h in range(2):
                        last = nc.vector.tensor_scalar(yb[:, :, h, :], y2[:, :, :], hrow[:, h:h + 1], None, ALU.mult)
                    last.then_inc(s_yb, 1)
                    assert st.n == K, st.n

            @block.tensor
            def _(pe):
                pe.wait_ge(s_const, ONE + 1)
                pe.wait_ge(s_par, ONE + 160)
                with nc.tensor.Fori(0, SEQ // SC) as q:
                    pe.wait_ge(s_bk, ONE + q * 8 + 8)
                    for j in range(PAIRS):
                        for c in range(CH):
                            u = j * CH + c
                            last = nc.tensor.matmul(bank[:, 6 + u // 8, (u % 8) * 64:(u % 8) * 64 + 64], bk[:, j, c, :],
                                                    ar[:, :, j, c * C:(c + 1) * C], start=True, stop=True)
                    last.then_inc(s_gram, 1)
                    pe.wait_ge(s_av, ONE + q * 8 + 8)
                    pe.wait_ge(s_aff, ONE + q)
                    for d in range(DBL):
                        last = nc.tensor.matmul(bank[:, 5, d * H:(d + 1) * H], vb[:, d // 2, d % 2, :], ident2[:, :], start=True, stop=True)
                    last.then_inc(s_vst, 1)
                    pe.wait_ge(s_yr, ONE + q)
                    for u in range(UNITS):
                        last = nc.tensor.transpose(bank[:, u // 4, (u % 4) * P:(u % 4 + 1) * P], bk[:, u // CH, u % CH, :], ident[:, :])
                    last.then_inc(s_bkt, 1)
                    pe.wait_ge(s_vr, ONE + q + 1)
                    for d in range(DBL):
                        last = nc.tensor.transpose(bank[:, 4 + d // 4, (d % 4) * P:(d % 4 + 1) * P], ab[:, d // 2, d % 2, :], ident[:, :])
                    last.then_inc(s_at, 1)
                    pe.wait_ge(s_aab, ONE + q + 1)
                    pe.wait_ge(s_gr, ONE + q + 1)
                    for d in range(DBL):
                        last = nc.tensor.matmul(bank[:, 6, d * C:(d + 1) * C], aab[:, d, :], ident4[:, :], start=True, stop=True)
                    last.then_inc(s_x2, 1)
                    for l in range(1, LEVELS):
                        pe.wait_ge(s_xc, ONE + q * LEVELS + l)
                        for d in range(DBL):
                            last = nc.tensor.matmul(bank[:, 7, d * C:(d + 1) * C], aab[:, d, :], x[:, d, :], start=True, stop=True)
                        last.then_inc(s_t1, 1)
                        pe.wait_ge(s_t1r, ONE + q * 4 + l)
                        pe.wait_ge(s_xt, ONE + q * LEVELS + l)
                        for d in range(DBL):
                            last = nc.tensor.matmul(bank[:, 6, d * C:(d + 1) * C], xt[:, d, :], t1[:, d, :], start=True, stop=True)
                        last.then_inc(s_x2, 1)
                        if l == 1:
                            pe.wait_ge(s_atr, ONE + q + 1)
                            for d in range(DBL):
                                last = nc.tensor.matmul(bank[:, 5, d * H:(d + 1) * H], aak[:, d, :], vd[:, d, :], start=True, stop=True)
                            last.then_inc(s_z0, 1)
                    pe.wait_ge(s_xt, ONE + q * LEVELS + LEVELS)
                    for d in range(DBL):
                        last = nc.tensor.matmul(bank[:, 6 + d // 4, (d % 4) * P:(d % 4 + 1) * P], atm[:, d, :], xt[:, d, :], start=True, stop=True)
                    last.then_inc(s_w, 1)
                    pe.wait_ge(s_z0r, ONE + q + 1)
                    for d in range(DBL):
                        last = nc.tensor.matmul(bank[:, 4, d * H:(d + 1) * H], xt[:, d, :], z0[:, d, :], start=True, stop=True)
                    last.then_inc(s_z, 1)
                    pe.wait_ge(s_wr, ONE + q + 1)
                    pe.wait_ge(s_zr, ONE + q + 1)
                    pe.wait_ge(s_rb, ONE + q * 4 + 4)
                    pe.wait_ge(s_bktr, ONE + q + 1)
                    for c in range(CH):
                        if c == 0:
                            pe.wait_ge(s_sn, ONE + q * CH)
                        else:
                            pe.wait_ge(s_sn, ONE + q * CH + c)
                        for j in range(PAIRS):
                            last = nc.tensor.matmul(bank[:, j, c * H:(c + 1) * H], wr[:, j, c, :], state[:, j, :], start=True, stop=True)
                        last.then_inc(s_p1, 1)
                        pe.wait_ge(s_u, ONE + q * CH + c + 1)
                        for j in range(PAIRS):
                            last = nc.tensor.matmul(bank[:, 4, j * H:(j + 1) * H], bkt[:, j * CH + c, :], uv[:, j, c, :], start=True, stop=True)
                        last.then_inc(s_s, 1)
                        for j in range(PAIRS):
                            last = nc.tensor.matmul(bank[vrows(c % 2), j, c * H:(c + 1) * H], ark[:, j * CH + c, :], uv[:, j, c, :],
                                                    start=False, stop=True, skip_group_check=True)
                        last.then_inc(s_y, 1)
                    pe.wait_ge(s_yb, ONE + q + 1)
                    for d in range(DBL):
                        last = nc.tensor.matmul(bank[:, 5, d * 2 * C:(d + 1) * 2 * C], yb[:, d, :, :].rearrange("p h v -> p (h v)"), rows[:, :],
                                                start=True, stop=True)
                    last.then_inc(s_yt, 1)


def phase_ffn(nc, a, scr, out):
    ctx, sems = ExitStack(), []
    with ctx:
        def sb(name, shape, dt=F32):
            return ctx.enter_context(nc.sbuf_tensor("p3_" + name, shape, dt))

        def sem(name):
            sems.append(ctx.enter_context(nc.semaphore("p3_" + name)))
            return sems[-1]

        KO = KT
        NDN = KO + FF
        HALF = D_MODEL // TB
        mraw = sb("mraw", [P, KO, TB])
        hT_hi = sb("hT_hi", [P, KT, TB], F32R)
        hT_lo = sb("hT_lo", [P, KT, TB], F32R)
        x = sb("x", [P, TT, D_MODEL])
        acc = sb("acc", [P, TT, D_MODEL])
        hs = sb("hs", [P, 2, D_MODEL])
        up_raw = [sb(f"up_raw{i}", [P, 2, KT, P]) for i in range(2)]
        up_hi = [sb(f"up_hi{i}", [P, 2, KT, P], F32R) for i in range(2)]
        up_lo = [sb(f"up_lo{i}", [P, 2, KT, P], F32R) for i in range(2)]
        dn_raw = [sb(f"dn_raw{i}", [P, D_MODEL]) for i in range(2)]
        dn_hi = [sb(f"dn_hi{i}", [P, D_MODEL], F32R) for i in range(2)]
        dn_lo = [sb(f"dn_lo{i}", [P, D_MODEL], F32R) for i in range(2)]
        ub = [sb(f"ub{i}", [P, 2, 2 + TB]) for i in range(2)]
        cv = [sb(f"cv{i}", [P, 2, TB]) for i in range(2)]
        ah = [sb(f"ah{i}", [P, TB]) for i in range(2)]
        a_hi = [sb(f"a_hi{i}", [P, TB], F32R) for i in range(2)]
        a_lo = [sb(f"a_lo{i}", [P, TB], F32R) for i in range(2)]
        cpar = [sb(f"cpar{i}", [P, 2, 4]) for i in range(2)]
        cw = sb("cw", [P, 2, FF, 4])
        tail = sb("tail", [P, 2, FF, 2])
        gpost = sb("gpost", [P, D_MODEL])
        gffn = sb("gffn", [P, D_MODEL])
        gain = sb("gain", [P, KT])
        ss = sb("ss", [P, 3, TT])
        rstd = sb("rstd", [P, 3, TT])
        eps = sb("eps", [P, 1])
        ident = sb("ident", [P, P])
        bank = ctx.enter_context(nc.psum_tensor("p3_bank", [P, 8, 512], F32))

        s_par = sem("params_loaded")
        s_const = sem("zeros_written")
        s_mix = sem("mix_loaded")
        s_x = sem("x_loaded")
        s_up = [sem(f"up_loaded{i}") for i in range(2)]
        s_dn = [sem(f"dn_loaded{i}") for i in range(2)]
        s_mh = sem("mix_hi_ready")
        s_ml = sem("mix_lo_ready")
        s_uh = sem("up_hi_ready")
        s_ul = sem("up_lo_ready")
        s_dh = sem("dn_hi_ready")
        s_dl = sem("dn_lo_ready")
        s_op = sem("out_proj_tile")
        s_sq = sem("squares_summed")
        s_rt = sem("rms_root")
        s_rc = sem("rms_recip")
        s_x2 = sem("x_updated")
        s_xs = sem("x_scaled")
        s_tr = sem("transposed")
        s_ht = sem("hT_ready")
        s_zero = sem("acc_zeroed")
        s_upd = sem("up_done")
        s_tl = sem("tail_used")
        s_ub = sem("up_read")
        s_tap = sem("tap_bias")
        s_cv = sem("conv_done")
        s_gl = sem("gelu_done")
        s_a = sem("hidden_ready")
        s_ah = sem("hidden_hi_ready")
        s_al = sem("hidden_lo_ready")
        s_db = sem("down_bank_done")
        s_acc = sem("down_bank_added")
        s_fin = sem("block_ready")
        s_out = sem("block_stored")
        s_dve = sem("dve_step")
        s_go = sem("gpsimd_started")

        upv = a["w_up"][0].rearrange("(k p) (s n) -> p s k n", p=P, s=2)
        xv = a["x"][0].rearrange("(t p) d -> p t d", p=P)
        ov = out[0].rearrange("(t p) d -> p t d", p=P)
        NPAR = 1 + 2 + 1 + 2 * (CONV_WIDTH + 1)

        with ExitStack():
            credit(nc, sems)
        with nc.Block() as block:
            @block.sync
            def _(sp):
                with nc.allow_non_contiguous_dma(reason="per-feature parameters, once"):
                    sp.dma_start(gain[:, :], a["pre_ffn_norm"][0].rearrange("(t p) -> p t", p=P)).then_inc(s_par, 16)
                    sp.dma_start(gpost[:, :], a["post_mix_norm"][0].partition_broadcast(P)).then_inc(s_par, 16)
                    sp.dma_start(gffn[:, :], a["post_ffn_norm"][0].partition_broadcast(P)).then_inc(s_par, 16)
                    sp.dma_start(ident[:, :], const_view(a, "ident")).then_inc(s_par, 16)
                    for s in range(2):
                        for tap in range(CONV_WIDTH):
                            sp.dma_start(cw[:, s, :, tap], a["conv_w"][0, tap, s * D_FF:(s + 1) * D_FF].rearrange("(f p) -> p f", p=P)
                                         ).then_inc(s_par, 16)
                        sp.dma_start(cw[:, s, :, CONV_WIDTH], a["conv_b"][0, s * D_FF:(s + 1) * D_FF].rearrange("(f p) -> p f", p=P)
                                     ).then_inc(s_par, 16)

                def load_up(b, g, s):
                    n = b * FF + g * GROUP + (0 if s == 0 else s - 1)
                    sp.wait_ge(s_uh, ONE + n)
                    sp.wait_ge(s_ul, ONE + n)
                    sp.dma_start(up_raw[s][:, 0, :, :], upv[:, 0, :, bass.ds((g * GROUP + s) * P, P)]).then_inc(s_up[s], 16)
                    sp.dma_start(up_raw[s][:, 1, :, :], upv[:, 1, :, bass.ds((g * GROUP + s) * P, P)]).then_inc(s_up[s], 16)

                def load_dn(b, n, s, src):
                    w = b * NDN + n - (0 if s == 0 else 1)
                    sp.wait_ge(s_dh, ONE + w)
                    sp.wait_ge(s_dl, ONE + w)
                    sp.dma_start(dn_raw[s][:, :], src).then_inc(s_dn[s], 16)

                with nc.sync.Fori(0, BLOCKS) as b:
                    sp.wait_ge(s_mh, ONE + b)
                    sp.wait_ge(s_ml, ONE + b)
                    sp.dma_start(mraw[:, :, :], scr["mix"][:, :, bass.ds(b * TB, TB)]).then_inc(s_mix, 16)
                    for s in range(GROUP):
                        load_up(b, 0, s)
                    for k in range(KO):
                        load_dn(b, k, k % 2, a["w_out"][0, k * P:(k + 1) * P, :])
                        if k == 1:
                            sp.wait_ge(s_out, ONE + b * 16)
                            sp.dma_start(x[:, :, :], xv[:, bass.ds(b * TT, TT), :]).then_inc(s_x, 16)
                    with nc.sync.Fori(0, GROUPS - 1) as g:
                        load_up(b, g + 1, 0)
                        for s in range(GROUP):
                            load_dn(b, KO + g * GROUP + s, s, a["w_down"][0, bass.ds((g * GROUP + s) * P, P), :])
                        load_up(b, g + 1, 1)
                    for s in range(GROUP):
                        f = (GROUPS - 1) * GROUP + s
                        load_dn(b, KO + f, s, a["w_down"][0, f * P:(f + 1) * P, :])
                    sp.wait_ge(s_fin, ONE + b * TT + TT)
                    sp.dma_start(ov[:, bass.ds(b * TT, TT), :], x[:, :, :]).then_inc(s_out, 16)
                sp.wait_ge(s_out, ONE + 16 * BLOCKS)

            @block.gpsimd
            def _(gp):
                nc.gpsimd.memset(eps[:, :], NORM_EPS)
                nc.gpsimd.memset(tail[:, :, :, :], 0.0).then_inc(s_const, 1)

                def low_up(b, g, s):
                    n = b * FF + g * GROUP + s
                    gp.wait_ge(s_uh, ONE + n + 1)
                    nc.gpsimd.tensor_tensor(up_lo[s][:, :, :, :], up_raw[s][:, :, :, :], up_hi[s][:, :, :, :].bitcast(F32),
                                            ALU.subtract).then_inc(s_ul, 1)

                def low_dn(b, n, s):
                    gp.wait_ge(s_dh, ONE + b * NDN + n + 1)
                    nc.gpsimd.tensor_tensor(dn_lo[s][:, :], dn_raw[s][:, :], dn_hi[s][:, :].bitcast(F32),
                                            ALU.subtract).then_inc(s_dl, 1)

                with nc.gpsimd.Fori(0, BLOCKS) as b:
                    for s in range(GROUP):
                        low_up(b, 0, s)
                    gp.wait_ge(s_mh, ONE + b + 1)
                    nc.gpsimd.tensor_tensor(hT_lo[:, :, :], mraw[:, :, :], hT_hi[:, :, :].bitcast(F32), ALU.subtract).then_inc(s_ml, 1)
                    for k in range(KO):
                        low_dn(b, k, k % 2)
                    gp.wait_ge(s_tr, ONE + b * KT + KT)
                    gp.sem_inc(s_go, 1)
                    nc.gpsimd.memset(acc[:, :, :], 0.0).then_inc(s_zero, 1)
                    with nc.gpsimd.Fori(0, GROUPS - 1) as g:
                        low_up(b, g + 1, 0)
                        for s in range(GROUP):
                            low_dn(b, KO + g * GROUP + s, s)
                        low_up(b, g + 1, 1)
                    for s in range(GROUP):
                        low_dn(b, KO + (GROUPS - 1) * GROUP + s, s)

            @block.scalar
            def _(act):
                act.wait_ge(s_const, ONE + 1)
                act.wait_ge(s_par, ONE + 16 * NPAR)

                def high_up(b, g, s):
                    act.wait_ge(s_up[s], ONE + (b * GROUPS + g) * 32 + 32)
                    nc.scalar.activation(up_hi[s][:, :, :, :], up_raw[s][:, :, :, :], ACT.Copy).then_inc(s_uh, 1)

                def high_dn(b, n, s):
                    act.wait_ge(s_dn[s], ONE + (b * (NDN // 2)) * 16 + (n - s) * 8 + 16)
                    nc.scalar.activation(dn_hi[s][:, :], dn_raw[s][:, :], ACT.Copy).then_inc(s_dh, 1)

                def read_up(b, g, s):
                    n = b * FF + g * GROUP + s
                    act.wait_ge(s_upd, ONE + n + 1)
                    act.wait_ge(s_a, ONE + b * FF + g * GROUP + (0 if s == 0 else s - 1))
                    nc.scalar.activation(ub[s][:, :, 2:2 + TB], bank[:, 2 * s:2 * s + 2, :], ACT.Copy).then_inc(s_ub, 1)
                    nc.scalar.activation(ub[s][:, :, 0:2], tail[:, :, bass.ds(g * GROUP + s, 1), :].rearrange("p s f t -> p s (f t)"),
                                         ACT.Copy)
                    nc.scalar.activation(cpar[s][:, :, :], cw[:, :, bass.ds(g * GROUP + s, 1), :].rearrange("p s f t -> p s (f t)"),
                                         ACT.Copy).then_inc(s_tl, 1)

                def taps(b, g, s):
                    n = b * FF + g * GROUP + s
                    act.wait_ge(s_ub, ONE + n + 1)
                    act.wait_ge(s_tl, ONE + n + 1)
                    for i in range(2):
                        last = nc.scalar.activation(cv[s][:, i, :], ub[s][:, i, 2:2 + TB], ACT.Identity,
                                                    scale=cpar[s][:, i, 2:3], bias=cpar[s][:, i, 3:4])
                    last.then_inc(s_tap, 1)
                    nc.scalar.activation(tail[:, :, bass.ds(g * GROUP + s, 1), :].rearrange("p s f t -> p s (f t)"),
                                         ub[s][:, :, TB:TB + 2], ACT.Copy)

                def gelu(b, g, s):
                    n = b * FF + g * GROUP + s
                    act.wait_ge(s_cv, ONE + n + 1)
                    nc.scalar.activation(cv[s][:, 0, :], cv[s][:, 0, :], ACT.Gelu_apprx_tanh).then_inc(s_gl, 1)

                def high_a(b, g, s):
                    n = b * FF + g * GROUP + s
                    act.wait_ge(s_a, ONE + n + 1)
                    nc.scalar.activation(a_hi[s][:, :], ah[s][:, :], ACT.Copy).then_inc(s_ah, 1)

                def group(b, g, last):
                    read_up(b, g, 0)
                    if not last:
                        high_up(b, g + 1, 0)
                    taps(b, g, 0)
                    gelu(b, g, 0)
                    act.wait_ge(s_db, ONE + (b * GROUPS + g) * 8)
                    for s in range(GROUP):
                        high_dn(b, KO + g * GROUP + s, s)
                    high_a(b, g, 0)
                    read_up(b, g, 1)
                    if not last:
                        high_up(b, g + 1, 1)
                    taps(b, g, 1)
                    gelu(b, g, 1)
                    high_a(b, g, 1)

                def root(b, i):
                    act.wait_ge(s_sq, ONE + (b * 3 + i) * TT + TT)
                    nc.scalar.activation(rstd[:, i, :], ss[:, i, :], ACT.Sqrt, scale=1.0 / D_MODEL, bias=eps[:, 0:1]).then_inc(s_rt, 1)

                with nc.scalar.Fori(0, BLOCKS) as b:
                    act.wait_ge(s_upd, ONE + b * FF)
                    for s in range(GROUP):
                        high_up(b, 0, s)
                    act.wait_ge(s_mix, ONE + b * 16 + 16)
                    nc.scalar.activation(hT_hi[:, :, :], mraw[:, :, :], ACT.Copy).then_inc(s_mh, 1)
                    act.wait_ge(s_db, ONE + b * (GROUPS * 8))
                    for k in range(KO):
                        if k >= 2:
                            act.wait_ge(s_op, ONE + b * KO + k - 1)
                        high_dn(b, k, k % 2)
                    act.wait_ge(s_op, ONE + b * KO + KO)
                    for t in range(TT):
                        if t >= 2 or True:
                            act.wait_ge(s_sq, ONE + (b * 3) * TT + (t - 1 if t else 0))
                        nc.scalar.activation(hs[:, t % 2, :], bank[:, 2 * t:2 * t + 2, :].rearrange("p h d -> p (h d)"), ACT.Square,
                                             accum_out=ss[:, 0, t:t + 1]).then_inc(s_sq, 1)
                    root(b, 0)
                    for t in range(TT):
                        act.wait_ge(s_x2, ONE + b * TT + t + 1)
                        nc.scalar.activation(acc[:, t, :], x[:, t, :], ACT.Square, accum_out=ss[:, 1, t:t + 1]).then_inc(s_sq, 1)
                    root(b, 1)
                    act.wait_ge(s_rc, ONE + b * 3 + 2)
                    for t in range(TT):
                        nc.scalar.activation(acc[:, t, :], x[:, t, :], ACT.Copy, scale=rstd[:, 1, t:t + 1]).then_inc(s_xs, 1)
                    with nc.scalar.Fori(0, GROUPS - 1) as g:
                        group(b, g, False)
                    group(b, GROUPS - 1, True)
                    act.wait_ge(s_acc, ONE + (b + 1) * (GROUPS * 8))
                    for t in range(TT):
                        act.wait_ge(s_sq, ONE + (b * 3 + 2) * TT + (t - 1 if t else 0))
                        nc.scalar.activation(hs[:, t % 2, :], acc[:, t, :], ACT.Square, accum_out=ss[:, 2, t:t + 1]).then_inc(s_sq, 1)
                    root(b, 2)

            @block.vector
            def _(dve):
                dve.wait_ge(s_par, ONE + 16 * NPAR)

                def conv(st, b, g, s):
                    n = b * FF + g * GROUP + s
                    dve.wait_ge(s_tap, ONE + n + 1)
                    for i in range(2):
                        st.do(nc.vector.scalar_tensor_tensor(cv[s][:, i, :], ub[s][:, i, 1:1 + TB], cpar[s][:, i, 1:2],
                                                             cv[s][:, i, :], ALU.mult, ALU.add))
                    st.wait()
                    for i in range(2):
                        last = nc.vector.scalar_tensor_tensor(cv[s][:, i, :], ub[s][:, i, 0:TB], cpar[s][:, i, 0:1],
                                                              cv[s][:, i, :], ALU.mult, ALU.add)
                    last.then_inc(s_cv, 1)
                    dve.wait_ge(s_gl, ONE + n + 1)
                    dve.wait_ge(s_ah, ONE + b * FF + g * GROUP + (0 if s == 0 else s - 1))
                    nc.vector.tensor_tensor(ah[s][:, :], cv[s][:, 0, :], cv[s][:, 1, :], ALU.mult).then_inc(s_a, 1)

                def low_a(b, g, s):
                    dve.wait_ge(s_ah, ONE + b * FF + g * GROUP + s + 1)
                    nc.vector.tensor_tensor(a_lo[s][:, :], ah[s][:, :], a_hi[s][:, :].bitcast(F32), ALU.subtract).then_inc(s_al, 1)

                def add_down(b, g):
                    for n in range(TT * HALF):
                        dve.wait_ge(s_db, ONE + (b * GROUPS + g) * 8 + n + 1)
                        dst = acc[:, n // HALF, (n % HALF) * TB:(n % HALF + 1) * TB]
                        nc.vector.tensor_tensor(dst, bank[:, 4 + n % 4, :], dst, ALU.add).then_inc(s_acc, 1)

                def group(st, b, g, first):
                    conv(st, b, g, 0)
                    if not first:
                        dve.wait_ge(s_acc, ONE + (b * GROUPS + g - 1) * 8)
                        add_down(b, g - 1)
                    low_a(b, g, 0)
                    conv(st, b, g, 1)
                    low_a(b, g, 1)

                def residual(b, i, sem_done, src, gain_row):
                    dve.wait_ge(s_rt, ONE + b * 3 + (0 if i == 0 else 2) + 1)
                    j = 0 if i == 0 else 2
                    nc.vector.reciprocal(rstd[:, j, :], rstd[:, j, :]).then_inc(s_rc, 1)
                    dve.wait_ge(s_rc, ONE + b * 3 + j + 1)
                    for t in range(TT):
                        if t >= 2:
                            dve.wait_ge(sem_done[0], sem_done[1] + t - 1)
                        st2 = nc.vector.scalar_tensor_tensor(hs[:, t % 2, :], src(t), rstd[:, j, t:t + 1], gain_row[:, :], ALU.mult, ALU.mult)
                        yield t, st2

                K = 2 * TT + KT + FF * 2
                with nc.vector.Fori(0, BLOCKS) as b:
                    st = Steps(dve, s_dve, b * K)
                    dve.wait_ge(s_x, ONE + b * 16 + 16)
                    base = ONE + b * TT
                    for t, ins in residual(b, 0, (s_x2, base), lambda t: bank[:, 2 * t:2 * t + 2, :].rearrange("p h d -> p (h d)"), gpost):
                        st.link(ins)
                        nc.vector.tensor_tensor(x[:, t, :], x[:, t, :], hs[:, t % 2, :], ALU.add).then_inc(s_x2, 1)
                    dve.wait_ge(s_rt, ONE + b * 3 + 2)
                    nc.vector.reciprocal(rstd[:, 1, :], rstd[:, 1, :]).then_inc(s_rc, 1)
                    for k in range(KT):
                        dve.wait_ge(s_tr, ONE + b * KT + k + 1)
                        st.link(nc.vector.tensor_scalar(hT_hi[:, k, :], bank[:, k % 2, :], gain[:, k:k + 1], None, ALU.mult))
                        nc.vector.scalar_tensor_tensor(hT_lo[:, k, :], bank[:, k % 2, :], gain[:, k:k + 1],
                                                       hT_hi[:, k, :].bitcast(F32), ALU.mult, ALU.subtract).then_inc(s_ht, 1)
                    dve.wait_ge(s_zero, ONE + b + 1)
                    group(st, b, 0, True)
                    inner = st.n
                    with nc.vector.Fori(1, GROUPS) as g:
                        sg = Steps(dve, s_dve, b * K + inner + (g - 1) * 4)
                        group(sg, b, g, False)
                        assert sg.n == 4
                    st.n = inner + (GROUPS - 1) * 4
                    add_down(b, GROUPS - 1)
                    dve.wait_ge(s_acc, ONE + (b + 1) * (GROUPS * 8))
                    for t, ins in residual(b, 1, (s_fin, ONE + b * TT), lambda t: acc[:, t, :], gffn):
                        st.link(ins)
                        nc.vector.tensor_tensor(x[:, t, :], x[:, t, :], hs[:, t % 2, :], ALU.add).then_inc(s_fin, 1)
                    assert st.n == K, (st.n, K)

            @block.tensor
            def _(pe):
                pe.wait_ge(s_par, ONE + 16 * NPAR)

                def up(b, g, s):
                    n = b * FF + g * GROUP + s
                    pe.wait_ge(s_uh, ONE + n + 1)
                    pe.wait_ge(s_ul, ONE + n + 1)
                    pe.wait_ge(s_ub, ONE + b * FF + g * GROUP + (0 if s == 0 else s - 1))
                    for i in range(2):
                        for k in range(KT):
                            last = split_matmul(nc, bank[:, 2 * s + i, :], up_hi[s][:, i, k, :], up_lo[s][:, i, k, :],
                                                hT_hi[:, k, :], hT_lo[:, k, :], k == 0, k == KT - 1)
                    last.then_inc(s_upd, 1)

                def down(b, g):
                    pe.wait_ge(s_ah, ONE + b * FF + g * GROUP + GROUP)
                    pe.wait_ge(s_al, ONE + b * FF + g * GROUP + GROUP)
                    pe.wait_ge(s_dh, ONE + b * NDN + KO + g * GROUP + GROUP)
                    pe.wait_ge(s_dl, ONE + b * NDN + KO + g * GROUP + GROUP)
                    for n in range(TT * HALF):
                        t, h = n // HALF, n % HALF
                        pe.wait_ge(s_acc, ONE + (b * GROUPS + g) * 8 + (n - 3 if n >= 4 else 0))
                        for s in range(GROUP):
                            last = split_matmul(nc, bank[:, 4 + n % 4, :], a_hi[s][:, t * P:(t + 1) * P], a_lo[s][:, t * P:(t + 1) * P],
                                                dn_hi[s][:, h * TB:(h + 1) * TB], dn_lo[s][:, h * TB:(h + 1) * TB],
                                                s == 0, s == GROUP - 1)
                        last.then_inc(s_db, 1)

                with nc.tensor.Fori(0, BLOCKS) as b:
                    pe.wait_ge(s_mh, ONE + b + 1)
                    pe.wait_ge(s_ml, ONE + b + 1)
                    pe.wait_ge(s_acc, ONE + b * (GROUPS * 8))
                    for k in range(KO):
                        pe.wait_ge(s_dh, ONE + b * NDN + k + 1)
                        pe.wait_ge(s_dl, ONE + b * NDN + k + 1)
                        for t in range(TT):
                            for h in range(HALF):
                                last = split_matmul(nc, bank[:, 2 * t + h, :], hT_hi[:, k, t * P:(t + 1) * P], hT_lo[:, k, t * P:(t + 1) * P],
                                                    dn_hi[k % 2][:, h * TB:(h + 1) * TB], dn_lo[k % 2][:, h * TB:(h + 1) * TB],
                                                    k == 0, k == KO - 1)
                        last.then_inc(s_op, 1)
                    pe.wait_ge(s_xs, ONE + b * TT + TT)
                    for k in range(KT):
                        if k >= 2:
                            pe.wait_ge(s_ht, ONE + b * KT + k - 1)
                        for t in range(TT):
                            last = nc.tensor.transpose(bank[:, k % 2, t * P:(t + 1) * P], acc[:, t, k * P:(k + 1) * P], ident[:, :])
                        last.then_inc(s_tr, 1)
                    pe.wait_ge(s_ht, ONE + b * KT + KT)
                    up(b, 0, 0)
                    up(b, 0, 1)
                    with nc.tensor.Fori(1, GROUPS) as g:
                        up(b, g, 0)
                        down(b, g - 1)
                        up(b, g, 1)
                    down(b, GROUPS - 1)


_INS = ['x', 'pre_mix_norm', 'w_in', 'mu_shift', 'w0', 'w_decay_up', 'a0', 'w_aaa_up', 'w_gate_up', 'k_k', 'k_a', 'r_k',
        'ln_x_w', 'ln_x_b', 'w_pool', 'pool_scale', 'w_out', 'post_mix_norm', 'pre_ffn_norm', 'w_up', 'conv_w', 'conv_b',
        'w_down', 'post_ffn_norm']

def build(nc, a, out):
    def scratch(name, shape):
        return nc.dram_tensor("scratch_" + name, shape, F32).ap()

    with ExitStack() as ctx:
        pend = ctx.enter_context(nc.sbuf_tensor("chunk_decay", [P, PAIRS, SEQ // C], F32))
        scr = {k: scratch(k, (P, PAIRS, SEQ)) for k in ("rt", "at", "bt", "kt", "v", "bonus", "g")}
        scr["mix"] = scratch("mix", (P, 2 * PAIRS, SEQ))
        scr["pend"] = pend
        phase_project(nc, a, scr)
        phase_recur(nc, a, scr)
        phase_ffn(nc, a, scr, out)


def kernel(**inputs):
    import concourse.bacc as bacc
    from concourse.bass_utils import run_bass_kernel_spmd

    nc = bacc.Bacc("TRN2", target_bir_lowering=False, num_devices=1)
    arrays = {"in_" + k: np.ascontiguousarray(inputs[k]) for k in _INS}
    arrays["in_consts"] = constants()
    a = {k[3:]: nc.dram_tensor(k, v.shape, mybir.dt.from_np(v.dtype), kind="ExternalInput").ap() for k, v in arrays.items()}
    out = nc.dram_tensor("out", (1, SEQ, D_MODEL), F32, kind="ExternalOutput").ap()
    build(nc, a, out)
    r = run_bass_kernel_spmd(nc, [arrays], core_ids=[0])
    return r.results[0]["out"]
```

```python
import math
from contextlib import ExitStack

import numpy as np

import concourse.bass as bass
from concourse import mybir

F32 = mybir.dt.float32
F32R = mybir.dt.float32r
ALU = mybir.AluOpType
ACT = mybir.ActivationFunctionType
AX = mybir.AxisListType

P = 128
D_MODEL, SEQ = 1024, 2048
RWKV_WIDTH, POOL_WIDTH, HEAD_DIM = 512, 512, 64
DECAY_LORA = AAA_LORA = 64
GATE_LORA = 128
IN_COLS = 3 * RWKV_WIDTH + DECAY_LORA + AAA_LORA + GATE_LORA + POOL_WIDTH
D_FF = 2816
CONV_WIDTH = 3
NORM_EPS, GN_EPS = 1e-6, 64e-5

TB = 512
BLOCKS = SEQ // TB
TT = TB // P
KT = D_MODEL // P
FT = IN_COLS // P
PAIRS = RWKV_WIDTH // P
SHIFTED = 14
LORA, GATE, POOL0 = 12, 13, 14
HALO = 16
C = 32
SC = P
CH = SC // C
UNITS = PAIRS * CH
DBL = UNITS // 2
FF = D_FF // P
GROUP = 2
GROUPS = FF // GROUP


CONSTS = {}


def _layout():
    at = 0
    for name, shape in (("ident", (P,)), ("head_ones", (P,)), ("reset", (TB,)), ("cinv", (PAIRS, HALO)),
                        ("ident2", (HEAD_DIM,)), ("ident4", (C,)), ("strict", (C,)), ("causal", (C,)),
                        ("levels", (5, C)), ("rows_to_tokens", (2 * C,)), ("head_rows", (2,))):
        size = math.prod(shape)
        CONSTS[name] = (at, size, shape)
        at += size
    return at


CONST_COLS = _layout()


def constants():
    p = np.arange(P)[:, None]
    t = np.arange(C)[None, :]
    s = p % C
    parts = {
        "ident": p == np.arange(P)[None, :],
        "head_ones": p // HEAD_DIM == np.arange(P)[None, :] // HEAD_DIM,
        "reset": np.broadcast_to(np.arange(TB)[None, :] % C != 0, (P, TB)),
        "cinv": np.broadcast_to(1.0 / np.minimum(np.arange(HALO)[None, :] + 1, 2.0 ** np.arange(1, PAIRS + 1)[:, None]).reshape(1, -1),
                                (P, PAIRS * HALO)),
        "ident2": p % HEAD_DIM == np.arange(HEAD_DIM)[None, :],
        "ident4": s == t,
        "strict": s < t,
        "causal": s <= t,
        "levels": np.concatenate([(s >> (l + 1) == t >> (l + 1)) & ((s >> l) % 2 == 1) & ((t >> l) % 2 == 0)
                                  for l in range(5)], axis=1),
        "rows_to_tokens": (1 - p // HEAD_DIM) * C + s == np.arange(2 * C)[None, :],
        "head_rows": (p // C) % 2 == np.arange(2)[None, :],
    }
    return np.concatenate([np.asarray(parts[k], np.float32) for k in CONSTS], axis=1)


def const_view(a, name):
    at, size, shape = CONSTS[name]
    v = a["consts"][:, at:at + size]
    return v.rearrange("p (a b) -> p a b", b=shape[1]) if len(shape) == 2 else v


class Steps:

    def __init__(self, eng, sem, base=0):
        self.eng, self.sem, self.base, self.n = eng, sem, base, 0

    def do(self, ins):
        ins.then_inc(self.sem, 1)
        self.n += 1
        return self.n

    def wait(self, n=None):
        self.eng.wait_ge(self.sem, ONE + self.base + (self.n if n is None else n))

    def link(self, ins):
        self.do(ins)
        self.wait()


ONE = 1


def credit(nc, sems):
    with nc.Block() as block:
        @block.sync
        def _(sp):
            for s in sems:
                sp.sem_inc(s, ONE)


def split_matmul(nc, out, lhs_hi, lhs_lo, rhs_hi, rhs_lo, start, stop):
    nc.tensor.matmul(out, lhs_hi, rhs_hi, start=start, stop=False)
    nc.tensor.matmul(out, lhs_hi, rhs_lo, start=False, stop=False)
    return nc.tensor.matmul(out, lhs_lo, rhs_hi, start=False, stop=stop)


def phase_project(nc, a, scr):
    ctx, sems = ExitStack(), []
    with ctx:
        def sb(name, shape, dt=F32):
            return ctx.enter_context(nc.sbuf_tensor("p1_" + name, shape, dt))

        def sem(name):
            sems.append(ctx.enter_context(nc.semaphore("p1_" + name)))
            return sems[-1]

        xin = sb("xin", [P, TT, D_MODEL])
        hT_hi = sb("hT_hi", [P, KT, TB], F32R)
        hT_lo = sb("hT_lo", [P, KT, TB], F32R)
        w_raw = [sb(f"w_raw{i}", [P, KT, P]) for i in range(2)]
        w_hi = [sb(f"w_hi{i}", [P, KT, P], F32R) for i in range(2)]
        w_lo = [sb(f"w_lo{i}", [P, KT, P], F32R) for i in range(2)]
        proj = sb("proj", [P, FT, HALO + TB])
        um = sb("um", [P, SHIFTED, TB])
        dec = sb("dec", [P, PAIRS, TB])
        alpha = sb("alpha", [P, PAIRS, TB])
        cum = sb("cum", [P, PAIRS, TB])
        einv = sb("einv", [P, PAIRS, TB])
        kk = sb("kk", [P, PAIRS, TB])
        tmp = sb("tmp", [P, PAIRS, TB])
        gate = sb("gate", [P, PAIRS, TB])
        ident = sb("ident", [P, P])
        head_ones = sb("head_ones", [P, P])
        reset = sb("reset", [P, TB])
        cinv = sb("cinv", [P, PAIRS, HALO])
        wlora = sb("wlora", [P, RWKV_WIDTH])
        wgate = sb("wgate", [P, RWKV_WIDTH])
        wpool = sb("wpool", [P, PAIRS, P])
        gain = sb("gain", [P, KT])
        mu = sb("mu", [P, SHIFTED])
        par = sb("par", [P, 7, PAIRS])
        W0, A0, KKW, KA, RK, PSC, ONE_KA = range(7)
        ss = sb("ss", [P, TT])
        rstd = sb("rstd", [P, TT])
        eps = sb("eps", [P, 1])
        sA = tmp[:, 0:2, :].rearrange("p a t -> p (a t)")[:, 0:HALO + TB]
        sB = tmp[:, 2:4, :].rearrange("p a t -> p (a t)")[:, 0:HALO + TB]

        ptr = [ctx.enter_context(nc.psum_tensor(f"p1_ptr{i}", [P, TB], F32)) for i in range(2)]
        ppr = [ctx.enter_context(nc.psum_tensor(f"p1_ppr{i}", [P, TB], F32)) for i in range(2)]
        pm = ctx.enter_context(nc.psum_tensor("p1_pm", [P, 4, TB], F32))

        s_par = sem("params_loaded")
        s_const = sem("constants_built")
        s_x = [sem(f"x_loaded{t}") for t in range(TT)]
        s_xs = sem("x_scaled")
        s_ss = sem("sum_squares")
        s_sq = sem("rms_root")
        s_rs = sem("rms_recip")
        s_tr = sem("transposed")
        s_ht = sem("hT_ready")
        s_w = [sem(f"w_loaded{i}") for i in range(2)]
        s_wh = sem("w_hi_ready")
        s_wl = sem("w_lo_ready")
        s_pr = sem("proj_done")
        s_prf = sem("proj_read")
        s_halo = sem("halo_moved")
        s_diff = sem("shift_diff")
        s_um = sem("shifted")
        s_lora = sem("lora_act")
        s_mm = sem("small_matmul")
        s_mmr = sem("small_matmul_read")
        s_kkr = sem("kk_raw")
        s_sqk = sem("kk_squared")
        s_nmax = sem("kk_norm_max")
        s_nrt = sem("kk_norm_root")
        s_km = sem("k_modified")
        s_cum = sem("decay_sums")
        s_exp = sem("exps_ready")
        s_bon = sem("bonus_terms")
        s_out = sem("outputs_ready")
        s_store = sem("stored")
        s_poolin = sem("pool_in")
        s_pout = sem("pool_out_ready")
        s_pstore = sem("pool_stored")
        s_dve = sem("dve_step")

        xv = a["x"][0].rearrange("(t p) d -> p t d", p=P)
        wv = a["w_in"][0].rearrange("(k p) n -> p k n", p=P)
        NPAR = 12 + 4
        STORES = 7

        credit(nc, sems)
        with nc.Block() as block:
            @block.sync
            def _(sp):
                with nc.allow_non_contiguous_dma(reason="per-feature parameters, once"):
                    for dst, name in ((gain, "pre_mix_norm"), (mu, "mu_shift")):
                        sp.dma_start(dst[:, :], a[name][0].rearrange("(t p) -> p t", p=P)).then_inc(s_par, 16)
                    for i, name in ((W0, "w0"), (A0, "a0"), (KKW, "k_k"), (KA, "k_a"), (PSC, "pool_scale")):
                        sp.dma_start(par[:, i, :], a[name][0].rearrange("(t p) -> p t", p=P)).then_inc(s_par, 16)
                    sp.dma_start(par[:, RK, :], a["r_k"][0].rearrange("h d -> (h d)").rearrange("(t p) -> p t", p=P)
                                 ).then_inc(s_par, 16)
                    for dst, key in ((ident[:, :], "ident"), (head_ones[:, :], "head_ones"), (reset[:, :], "reset"),
                                     (cinv[:, :, :], "cinv")):
                        sp.dma_start(dst, const_view(a, key)).then_inc(s_par, 16)
                    sp.dma_start(wlora[0:DECAY_LORA, :], a["w_decay_up"][0]).then_inc(s_par, 16)
                    sp.dma_start(wlora[DECAY_LORA:P, :], a["w_aaa_up"][0]).then_inc(s_par, 16)
                    sp.dma_start(wgate[:, :], a["w_gate_up"][0]).then_inc(s_par, 16)
                    sp.dma_start(wpool[:, :, :], a["w_pool"][0].rearrange("g c d -> c g d")).then_inc(s_par, 16)
                with nc.sync.Fori(0, BLOCKS) as b:
                    for t in range(TT):
                        sp.wait_ge(s_tr, ONE + b * KT)
                        sp.dma_start(xin[:, t, :], xv[:, b * TT + t, :]).then_inc(s_x[t], 16)
                    with nc.sync.Fori(0, FT // 2) as f2:
                        for i in range(2):
                            sp.wait_ge(s_wh, ONE + b * FT + f2 * 2)
                            sp.wait_ge(s_wl, ONE + b * FT + f2 * 2)
                            sp.dma_start(w_raw[i][:, :, :], wv[:, :, bass.ds(f2 * (2 * P) + i * P, P)]).then_inc(s_w[i], 16)
                sp.wait_ge(s_store, ONE + 16 * STORES * BLOCKS)
                sp.wait_ge(s_pstore, ONE + 16 * BLOCKS)

            @block.gpsimd
            def _(gp):
                nc.gpsimd.memset(eps[:, :], NORM_EPS)
                nc.gpsimd.memset(proj[:, :, TB:TB + HALO], 0.0).then_inc(s_const, 1)
                gp.wait_ge(s_const, ONE + 1)
                with nc.gpsimd.Fori(0, BLOCKS) as b:
                    with nc.gpsimd.Fori(0, FT // 2) as f2:
                        for i in range(2):
                            n = b * FT + f2 * 2 + i
                            gp.wait_ge(s_w[i], ONE + (b * (FT // 2) + f2) * 16 + 16)
                            gp.wait_ge(s_wh, ONE + n + 1)
                            nc.gpsimd.tensor_tensor(w_lo[i][:, :, :], w_raw[i][:, :, :], w_hi[i][:, :, :].bitcast(F32),
                                                    ALU.subtract).then_inc(s_wl, 1)
                    gp.wait_ge(s_prf, ONE + (b + 1) * FT)
                    gp.wait_ge(s_store, ONE + b * (16 * STORES))
                    for f in (LORA, GATE, *range(LORA)):
                        nc.gpsimd.tensor_tensor(um[:, f, :], proj[:, f, HALO - 1:HALO - 1 + TB],
                                                proj[:, f, HALO:HALO + TB], ALU.subtract).then_inc(s_diff, 1)

            @block.scalar
            def _(act):
                act.wait_ge(s_const, ONE + 1)
                with nc.scalar.Fori(0, BLOCKS) as b:
                    for t in range(TT):
                        act.wait_ge(s_x[t], ONE + b * 16 + 16)
                        if t == 0:
                            act.wait_ge(s_store, ONE + b * (16 * STORES))
                        dump = (tmp if t < 2 else einv)[:, t % 2 * 2:t % 2 * 2 + 2, :].rearrange("p a t -> p (a t)")
                        nc.scalar.activation(dump, xin[:, t, :], ACT.Square,
                                             accum_out=ss[:, t:t + 1]).then_inc(s_ss, 1)
                    act.wait_ge(s_ss, ONE + b * TT + TT)
                    nc.scalar.activation(rstd[:, :], ss[:, :], ACT.Sqrt, scale=1.0 / D_MODEL, bias=eps[:, 0:1]).then_inc(s_sq, 1)
                    act.wait_ge(s_rs, ONE + b + 1)
                    for t in range(TT):
                        nc.scalar.activation(xin[:, t, :], xin[:, t, :], ACT.Copy, scale=rstd[:, t:t + 1]).then_inc(s_xs, 1)
                    def w_high(f2, i):
                        n = b * FT + f2 * 2 + i
                        act.wait_ge(s_w[i], ONE + (b * (FT // 2) + f2) * 16 + 16)
                        nc.scalar.activation(w_hi[i][:, :, :], w_raw[i][:, :, :], ACT.Copy).then_inc(s_wh, 1)

                    def read_proj(f2, i):
                        act.wait_ge(s_pr, ONE + b * FT + f2 * 2 + i + 1)
                        nc.scalar.activation(proj[:, bass.ds(f2 * 2 + i, 1), HALO:HALO + TB],
                                             ppr[i][:, :].rearrange("p (a t) -> p a t", a=1), ACT.Copy).then_inc(s_prf, 1)

                    w_high(0, 0)
                    act.wait_ge(s_poolin, ONE + b * PAIRS)
                    act.wait_ge(s_um, ONE + b * SHIFTED)
                    nc.scalar.activation(proj[:, :, 0:HALO], proj[:, :, TB:TB + HALO], ACT.Copy).then_inc(s_halo, 1)
                    act.wait_ge(s_halo, ONE + b + 1)
                    with nc.scalar.Fori(0, FT // 2 - 1) as f2:
                        w_high(f2, 1)
                        read_proj(f2, 0)
                        w_high(f2 + 1, 0)
                        read_proj(f2, 1)
                    w_high(FT // 2 - 1, 1)
                    read_proj(FT // 2 - 1, 0)
                    read_proj(FT // 2 - 1, 1)
                    act.wait_ge(s_um, ONE + b * SHIFTED + 1)
                    nc.scalar.activation(um[0:DECAY_LORA, LORA, :], um[0:DECAY_LORA, LORA, :], ACT.Tanh).then_inc(s_lora, 1)
                    act.wait_ge(s_um, ONE + b * SHIFTED + 2)
                    nc.scalar.activation(um[:, GATE, :], um[:, GATE, :], ACT.Sigmoid).then_inc(s_lora, 1)
                    for j in range(PAIRS):
                        act.wait_ge(s_mm, ONE + b * 6 + 1)
                        last = nc.scalar.activation(dec[:, j, :], pm[:, j, :], ACT.Sigmoid, bias=par[:, W0, j:j + 1])
                    last.then_inc(s_mmr, 1)
                    act.wait_ge(s_mm, ONE + b * 6 + 2)
                    for j in range(PAIRS):
                        last = nc.scalar.activation(alpha[:, j, :], pm[:, j, :], ACT.Sigmoid, bias=par[:, A0, j:j + 1])
                    last.then_inc(s_mmr, 1)
                    act.wait_ge(s_mm, ONE + b * 6 + 3)
                    act.wait_ge(s_pstore, ONE + b * 16)
                    nc.scalar.activation(gate[:, :, :], pm[:, :, :], ACT.Copy).then_inc(s_mmr, 1)
                    act.wait_ge(s_um, ONE + b * SHIFTED + 10)
                    for j in range(PAIRS):
                        last = nc.scalar.activation(kk[:, j, :], um[:, 4 + j, :], ACT.Copy, scale=par[:, KKW, j:j + 1])
                    last.then_inc(s_kkr, 1)
                    act.wait_ge(s_kkr, ONE + b + 1)
                    nc.scalar.activation(tmp[:, :, :], kk[:, :, :], ACT.Square).then_inc(s_sqk, 1)
                    act.wait_ge(s_nmax, ONE + b + 1)
                    nc.scalar.activation(tmp[:, :, :], tmp[:, :, :], ACT.Sqrt).then_inc(s_nrt, 1)
                    act.wait_ge(s_cum, ONE + b + 1)
                    act.wait_ge(s_km, ONE + b + 1)
                    nc.scalar.activation(einv[:, :, :], cum[:, :, :], ACT.Exp, scale=-1.0).then_inc(s_exp, 1)
                    nc.scalar.activation(dec[:, :, :], dec[:, :, :], ACT.Exp).then_inc(s_exp, 1)
                    act.wait_ge(s_exp, ONE + b * 3 + 1)
                    nc.scalar.activation(cum[:, :, :], cum[:, :, :], ACT.Exp).then_inc(s_exp, 1)
                    tok = bass.ds(b * TB, TB)
                    act.wait_ge(s_um, ONE + (b + 1) * SHIFTED)
                    act.dma_start(scr["v"][:, :, tok], um[:, 8:12, :]).then_inc(s_store, 16)
                    act.wait_ge(s_mmr, ONE + b * 3 + 3)
                    act.dma_start(scr["g"][:, :, tok], gate[:, :, :]).then_inc(s_store, 16)
                    for n, (src, dst) in enumerate(((um[:, 0:4, :], scr["rt"]), (dec[:, :, :], scr["at"]),
                                                    (alpha[:, :, :], scr["bt"]), (um[:, 4:8, :], scr["kt"]),
                                                    (tmp[:, :, :], scr["bonus"]))):
                        act.wait_ge(s_out, ONE + b * 5 + n + 1)
                        act.dma_start(dst[:, :, tok], src).then_inc(s_store, 16)
                    act.wait_ge(s_mm, ONE + b * 6 + 6)
                    act.wait_ge(s_store, ONE + (b + 1) * (16 * STORES))
                    for g in range(PAIRS):
                        last = nc.scalar.activation(gate[:, g, :], pm[:, g, :], ACT.Copy, scale=par[:, PSC, g:g + 1])
                    last.then_inc(s_pout, 1)
                    last = None
                    act.wait_ge(s_pout, ONE + b + 1)
                    act.dma_start(scr["mix"][:, PAIRS:2 * PAIRS, tok], gate[:, :, :]).then_inc(s_pstore, 16)

            @block.vector
            def _(dve):
                dve.wait_ge(s_par, ONE + 16 * NPAR)
                nc.vector.tensor_scalar(par[:, ONE_KA, :], par[:, KA, :], -1.0, 1.0, ALU.mult, ALU.add).then_inc(s_dve, 1)
                dve.wait_ge(s_dve, ONE + 1)
                K = 42
                with nc.vector.Fori(0, BLOCKS) as b:
                    st = Steps(dve, s_dve, b * K + 1)
                    dve.wait_ge(s_sq, ONE + b + 1)
                    nc.vector.reciprocal(rstd[:, :], rstd[:, :]).then_inc(s_rs, 1)
                    for k in range(KT):
                        dve.wait_ge(s_tr, ONE + b * KT + k + 1)
                        st.link(nc.vector.tensor_scalar(hT_hi[:, k, :], ptr[k % 2][:, :], gain[:, k:k + 1], None, ALU.mult))
                        nc.vector.scalar_tensor_tensor(hT_lo[:, k, :], ptr[k % 2][:, :], gain[:, k:k + 1],
                                                       hT_hi[:, k, :].bitcast(F32), ALU.mult, ALU.subtract
                                                       ).then_inc(s_ht, 1)
                    for n, f in enumerate((LORA, GATE, *range(LORA))):
                        dve.wait_ge(s_diff, ONE + b * SHIFTED + n + 1)
                        nc.vector.scalar_tensor_tensor(um[:, f, :], um[:, f, :], mu[:, f:f + 1],
                                                       proj[:, f, HALO:HALO + TB], ALU.mult, ALU.add).then_inc(s_um, 1)
                    dve.wait_ge(s_mmr, ONE + b * 3 + 1)
                    st.link(nc.vector.tensor_scalar(dec[:, :, :], dec[:, :, :], -math.exp(-0.5), None, ALU.mult))
                    for j in range(PAIRS):
                        st.do(nc.vector.tensor_tensor_scan(cum[:, j, :], reset[:, :], dec[:, j, :], 0.0, ALU.mult, ALU.add))
                    st.wait()
                    nc.vector.tensor_tensor(dec[:, :, :], cum[:, :, :], dec[:, :, :], ALU.subtract).then_inc(s_cum, 1)
                    dve.wait_ge(s_mmr, ONE + b * 3 + 2)
                    for j in range(PAIRS):
                        st.do(nc.vector.tensor_scalar(einv[:, j, :], alpha[:, j, :], par[:, KA, j:j + 1],
                                                      par[:, ONE_KA, j:j + 1], ALU.mult, ALU.add))
                    st.wait()
                    dve.wait_ge(s_um, ONE + b * SHIFTED + SHIFTED)
                    dve.wait_ge(s_kkr, ONE + b + 1)
                    nc.vector.tensor_tensor(um[:, 4:8, :], um[:, 4:8, :], einv[:, :, :], ALU.mult).then_inc(s_km, 1)
                    dve.wait_ge(s_km, ONE + b + 1)
                    dve.wait_ge(s_mm, ONE + b * 6 + 4)
                    nc.vector.tensor_scalar(tmp[:, :, :], pm[:, :, :], 1e-24, None, ALU.max).then_inc(s_nmax, 1)
                    dve.wait_ge(s_nrt, ONE + b + 1)
                    st.link(nc.vector.reciprocal(tmp[:, :, :], tmp[:, :, :]))
                    st.link(nc.vector.tensor_tensor(kk[:, :, :], kk[:, :, :], tmp[:, :, :], ALU.mult))
                    for j in range(PAIRS):
                        last = nc.vector.scalar_tensor_tensor(tmp[:, j, :], um[:, j, :], par[:, RK, j:j + 1],
                                                              um[:, 4 + j, :], ALU.mult, ALU.mult)
                    last.then_inc(s_bon, 1)
                    dve.wait_ge(s_exp, ONE + b * 3 + 3)
                    dve.wait_ge(s_bon, ONE + b + 1)
                    nc.vector.tensor_tensor(um[:, 0:4, :], um[:, 0:4, :], cum[:, :, :], ALU.mult).then_inc(s_out, 1)
                    nc.vector.tensor_copy(scr["pend"][:, :, bass.ds(b * (TB // C), TB // C)],
                                          cum[:, :, :].rearrange("p j (c t) -> p j c t", t=C)[:, :, :, C - 1])
                    nc.vector.scalar_tensor_tensor(dec[:, :, :].rearrange("p j t -> p (j t)"),
                                                   kk[:, :, :].rearrange("p j t -> p (j t)"), -1.0,
                                                   dec[:, :, :].rearrange("p j t -> p (j t)"),
                                                   ALU.mult, ALU.mult).then_inc(s_out, 1)
                    st.link(nc.vector.tensor_tensor(alpha[:, :, :], alpha[:, :, :], kk[:, :, :], ALU.mult))
                    nc.vector.tensor_tensor(alpha[:, :, :], alpha[:, :, :], einv[:, :, :], ALU.mult).then_inc(s_out, 1)
                    nc.vector.tensor_tensor(um[:, 4:8, :], um[:, 4:8, :], einv[:, :, :], ALU.mult).then_inc(s_out, 1)
                    dve.wait_ge(s_mm, ONE + b * 6 + 5)
                    nc.vector.tensor_tensor(tmp[:, :, :], pm[:, :, :], um[:, 8:12, :], ALU.mult).then_inc(s_out, 1)
                    dve.wait_ge(s_store, ONE + (b + 1) * (16 * STORES))
                    for g in range(PAIRS):
                        dve.wait_ge(s_poolin, ONE + b * PAIRS + g)
                        u = proj[:, POOL0 + g, :]
                        src, dst, other = u, sA, sB
                        for l in range(g + 1):
                            w = 1 << l
                            lo = 2 * w - 1
                            st.link(nc.vector.tensor_tensor(dst[:, lo:HALO + TB], src[:, lo:HALO + TB],
                                                            src[:, lo - w:HALO + TB - w], ALU.add))
                            src, dst, other = dst, other, dst
                        s = src[:, HALO:HALO + TB]
                        st.do(nc.vector.scalar_tensor_tensor(kk[:, g, HALO:TB], s[:, HALO:TB], 1.0 / 2 ** (g + 1),
                                                             u[:, 2 * HALO:HALO + TB], ALU.mult, ALU.subtract))
                        st.link(nc.vector.tensor_tensor(s[:, 0:HALO], s[:, 0:HALO], cinv[:, g, :], ALU.mult))
                        nc.vector.tensor_tensor(kk[:, g, 0:HALO], s[:, 0:HALO], u[:, HALO:2 * HALO],
                                                ALU.subtract).then_inc(s_poolin, 1)
                    dve.wait_ge(s_poolin, ONE + (b + 1) * PAIRS)
                    for g in range(PAIRS):
                        st.do(nc.vector.memset(cinv[:, g, :], 1.0 / 2 ** (g + 1)))
                    st.wait()
                    assert st.n == K, st.n

            @block.tensor
            def _(pe):
                pe.wait_ge(s_const, ONE + 1)
                pe.wait_ge(s_par, ONE + 16 * NPAR)
                with nc.tensor.Fori(0, BLOCKS) as b:
                    for k in range(KT):
                        if k == 0:
                            pe.wait_ge(s_xs, ONE + b * TT + TT)
                        if k >= 2:
                            pe.wait_ge(s_ht, ONE + b * KT + k - 1)
                        for t in range(TT):
                            last = nc.tensor.transpose(ptr[k % 2][:, t * P:(t + 1) * P], xin[:, t, k * P:(k + 1) * P], ident[:, :])
                        last.then_inc(s_tr, 1)
                    with nc.tensor.Fori(0, FT // 2) as f2:
                        for i in range(2):
                            pe.wait_ge(s_ht, ONE + b * KT + KT)
                            n = b * FT + f2 * 2 + i
                            pe.wait_ge(s_wh, ONE + n + 1)
                            pe.wait_ge(s_wl, ONE + n + 1)
                            pe.wait_ge(s_prf, ONE + b * FT + f2 * 2)
                            for k in range(KT):
                                last = split_matmul(nc, ppr[i][:, :], w_hi[i][:, k, :], w_lo[i][:, k, :],
                                                    hT_hi[:, k, :], hT_lo[:, k, :], k == 0, k == KT - 1)
                            last.then_inc(s_pr, 1)
                    pe.wait_ge(s_lora, ONE + b * 2 + 1)
                    for j in range(PAIRS):
                        last = nc.tensor.matmul(pm[:, j, :], wlora[0:64, j * P:(j + 1) * P], um[0:64, LORA, :], start=True, stop=True)
                    last.then_inc(s_mm, 1)
                    pe.wait_ge(s_mmr, ONE + b * 3 + 1)
                    for j in range(PAIRS):
                        last = nc.tensor.matmul(pm[:, j, :], wlora[64:128, j * P:(j + 1) * P], um[64:128, LORA, :], start=True, stop=True)
                    last.then_inc(s_mm, 1)
                    pe.wait_ge(s_lora, ONE + b * 2 + 2)
                    pe.wait_ge(s_mmr, ONE + b * 3 + 2)
                    for j in range(PAIRS):
                        last = nc.tensor.matmul(pm[:, j, :], wgate[:, j * P:(j + 1) * P], um[:, GATE, :], start=True, stop=True)
                    last.then_inc(s_mm, 1)
                    pe.wait_ge(s_sqk, ONE + b + 1)
                    pe.wait_ge(s_mmr, ONE + b * 3 + 3)
                    for j in range(PAIRS):
                        last = nc.tensor.matmul(pm[:, j, :], head_ones[:, :], tmp[:, j, :], start=True, stop=True)
                    last.then_inc(s_mm, 1)
                    pe.wait_ge(s_bon, ONE + b + 1)
                    for j in range(PAIRS):
                        last = nc.tensor.matmul(pm[:, j, :], head_ones[:, :], tmp[:, j, :], start=True, stop=True)
                    last.then_inc(s_mm, 1)
                    pe.wait_ge(s_out, ONE + b * 5 + 5)
                    pe.wait_ge(s_poolin, ONE + b * PAIRS + PAIRS)
                    for g in range(PAIRS):
                        last = nc.tensor.matmul(pm[:, g, :], wpool[:, g, :], kk[:, g, :], start=True, stop=True)
                    last.then_inc(s_mm, 1)


def phase_recur(nc, a, scr):
    ctx, sems = ExitStack(), []
    with ctx:
        def sb(name, shape, dt=F32):
            return ctx.enter_context(nc.sbuf_tensor("p2_" + name, shape, dt))

        def sem(name):
            sems.append(ctx.enter_context(nc.semaphore("p2_" + name)))
            return sems[-1]

        H = HEAD_DIM
        LEVELS = 5
        N = SEQ // SC

        def two(name, shape):
            return [sb(f"{name}{i}", shape) for i in range(2)]

        ar = two("ar", [P, 2, PAIRS, SC])
        bt = sb("bt", [P, PAIRS, SC])
        kt = sb("kt", [P, PAIRS, SC])
        vt = sb("vt", [P, PAIRS, SC])
        bonus = sb("bonus", [P, PAIRS, SC])
        gate = sb("gate", [P, PAIRS, SC])
        bk = two("bk", [P, PAIRS, CH, P])
        ab = two("ab", [P, PAIRS, CH // 2, P])
        vb = two("vb", [P, PAIRS, CH // 2, P])
        wr = two("wr", [P, PAIRS, CH, P])
        aab = two("aab", [P, DBL, P])
        aak = two("aak", [P, DBL, P])
        ark = two("ark", [P, UNITS, 2 * C])
        bkt = two("bkt", [P, UNITS, P])
        uv = two("uv", [P, PAIRS, CH, H])
        z = two("zz", [P, PAIRS, CH // 2, H])
        x = sb("x", [P, DBL, C])
        xm = sb("xm", [P, DBL, C])
        xt = sb("xt", [P, DBL, P])
        t1 = sb("t1", [P, DBL, C])
        atm = sb("atm", [P, DBL, P])
        vd = sb("vd", [P, DBL, H])
        z0 = sb("z0", [P, DBL, H])
        state = sb("state", [P, PAIRS, H])
        sumst = sb("sumst", [P, PAIRS, H])
        pq = sb("pq", [P, PAIRS, CH])
        y = sb("y", [P, PAIRS, CH // 2, H])
        y2 = sb("y2", [P, DBL, H])
        yb = sb("yb", [P, DBL, 2, H])
        stat = sb("stat", [P, 4, DBL])
        mo = sb("mo", [P, PAIRS, SC])
        geps = sb("geps", [P, 1])
        zeros = sb("zeros", [P, P + 512], mybir.dt.bfloat16)
        ident = sb("ident", [P, P])
        ident2 = sb("ident2", [P, H])
        ident4 = sb("ident4", [P, C])
        strict = sb("strict", [P, C])
        causal = sb("causal", [P, C])
        levels = sb("levels", [P, LEVELS, C])
        rows = sb("rows", [P, 2 * C])
        hrow = sb("hrow", [P, 2])
        lnw = sb("lnw", [P, PAIRS])
        lnb = sb("lnb", [P, PAIRS])
        bank = ctx.enter_context(nc.psum_tensor("p2_bank", [P, 8, 512], F32))
        YB, SB, XB, GB, ROT = 0, 2, 3, 4, (6, 7)
        ybank = bank[:, YB:YB + 2, :].rearrange("p b (u v) -> p (b u) v", v=H)
        tcol = bank[:, XB, 0:DBL * C].rearrange("p (d s) -> p d s", s=C)
        xcol = bank[:, XB, DBL * C:2 * DBL * C].rearrange("p (d s) -> p d s", s=C)

        s_par = sem("params_loaded")
        s_const = sem("zeros_written")
        s_in = sem("inputs_loaded")
        s_in2 = sem("bonus_gate_loaded")
        s_bk = sem("bk_built")
        s_rb = sem("r_built")
        s_av = sem("a_v_built")
        s_gram = sem("gram_done")
        s_aab = sem("aab_masked")
        s_gr = sem("gram_read")
        s_t1 = sem("t1_done")
        s_t1r = sem("t1_read")
        s_x2 = sem("x_product")
        s_xm = sem("x_product_masked")
        s_xc = sem("x_updated")
        s_xt = sem("x_transposed")
        s_full = [sem(f"turn_bank{b}_full") for b in ROT]
        s_read = [sem(f"turn_bank{b}_read") for b in ROT]
        s_p1 = sem("state_products")
        s_u = sem("u_ready")
        s_s = sem("state_update")
        s_sum = sem("state_summed")
        s_sn = sem("state_ready")
        s_pq = sem("chunk_decay_ready")
        s_y = sem("y_done")
        s_yr = sem("y_read")
        s_gn = sem("norm_step")
        s_yc = sem("y_centred")
        s_yc2 = sem("y_normed")
        s_sq = sem("y_squared")
        s_var = sem("y_var")
        s_sd = sem("y_deviation")
        s_yb = sem("y_blocks")
        s_add = sem("bonus_added")
        s_mo = sem("mix_ready")
        s_mix = sem("mix_stored")
        s_go = sem("gpsimd_started")

        JOBS = ["v", "a0", "a1", "bk0", "bk1", "bk2", "bk3", "z0", "y", "w0", "w1", "z"]
        TURN = {name: (i % 2, i // 2) for i, name in enumerate(JOBS)}
        PER = len(JOBS) // 2

        def vrows(e):
            return slice(0, 64) if e else slice(64, 128)

        def urows(e):
            return slice(64, 128) if e else slice(0, 64)

        def by_parity(v, e):
            return v.rearrange("p j (c e) n -> p j c e n", e=2)[:, :, :, e, :]

        def iterations(eng, body):
            body(-2, 0)
            body(-1, 1)
            body(0, 0)
            with eng.Fori(0, (N - 4) // 2) as h:
                body(h * 2 + 1, 1)
                body(h * 2 + 2, 0)
            for i in range(N - 3, N + 1):
                body(i, i % 2)

        def stages(i):
            if not isinstance(i, int):
                return True, True, True, True
            return i + 2 < N, 0 <= i + 1 < N, 0 <= i < N, 0 <= i - 1 < N

        def turns(i):
            if not isinstance(i, int):
                base = [(i + 1) * PER, (i + 1) * PER]
                base[TURN["y"][0]] = (i + 1) * (PER - 1) + (i - 1)
                return base
            out = [0, 0]
            for k in range(-2, i):
                _, a2, _, c = stages(k)
                for name in JOBS:
                    if c if name == "y" else a2:
                        out[TURN[name][0]] += 1
            return out

        def job(i, name):
            _, a2, _, c = stages(i)
            t, before = TURN[name][0], 0
            for other in JOBS[:JOBS.index(name)]:
                if TURN[other][0] == t and (c if other == "y" else a2):
                    before += 1
            return t, turns(i)[t] + before

        credit(nc, sems)
        with nc.Block() as block:
            @block.sync
            def _(sp):
                with nc.allow_non_contiguous_dma(reason="per-feature parameters, once"):
                    for dst, name in ((lnw, "ln_x_w"), (lnb, "ln_x_b")):
                        sp.dma_start(dst[:, :], a[name][0].rearrange("(t p) -> p t", p=P)).then_inc(s_par, 16)
                    for dst, key in ((ident[:, :], "ident"), (ident2[:, :], "ident2"), (ident4[:, :], "ident4"),
                                     (strict[:, :], "strict"), (causal[:, :], "causal"), (levels[:, :, :], "levels"),
                                     (rows[:, :], "rows_to_tokens"), (hrow[:, :], "head_rows")):
                        sp.dma_start(dst, const_view(a, key)).then_inc(s_par, 16)

                def body(i, p):
                    a1, a2, b, c = stages(i)
                    if a1:
                        n = i + 2
                        tok = bass.ds(n * SC, SC)
                        sp.wait_ge(s_bk, ONE + n * 8)
                        sp.wait_ge(s_av, ONE + n * 8)
                        if b:
                            sp.wait_ge(s_rb, ONE + (i + 1) * 4)
                            sp.wait_ge(s_gram, ONE + i + 1)
                        for dst, key in ((bt[:, :, :], "bt"), (kt[:, :, :], "kt"), (ar[p][:, 0, :, :], "at"),
                                         (ar[p][:, 1, :, :], "rt"), (vt[:, :, :], "v")):
                            sp.dma_start(dst, scr[key][:, :, tok]).then_inc(s_in, 16)
                    if c:
                        n = i - 1
                        tok = bass.ds(n * SC, SC)
                        sp.wait_ge(s_mo, ONE + n)
                        for dst, key in ((bonus[:, :, :], "bonus"), (gate[:, :, :], "g")):
                            sp.dma_start(dst, scr[key][:, :, tok]).then_inc(s_in2, 16)
                        sp.wait_ge(s_mo, ONE + i)
                        sp.dma_start(scr["mix"][:, 0:PAIRS, tok], mo[:, :, :]).then_inc(s_mix, 16)

                iterations(nc.sync, body)
                sp.wait_ge(s_mix, ONE + 16 * N)

            @block.gpsimd
            def _(gp):
                for m in (bk, wr, ab, vb, aab, aak, ark):
                    for i in range(2):
                        nc.gpsimd.memset(m[i][:], 0.0)
                nc.gpsimd.memset(xt[:, :, :], 0.0)
                nc.gpsimd.memset(zeros[:, :], 0.0)
                nc.gpsimd.memset(geps[:, :], GN_EPS)
                nc.gpsimd.memset(state[:, :, :], 0.0).then_inc(s_const, 1)
                gp.wait_ge(s_const, ONE + 1)

                def body(i, p):
                    a1, a2, b, c = stages(i)
                    if c:
                        gp.wait_ge(s_yc, ONE + i)
                        yv = y[:].rearrange("p j c v -> p (j c) v")
                        nc.gpsimd.tensor_tensor(y2[:, :, :], yv, yv, ALU.mult).then_inc(s_sq, 1)
                    if a1:
                        n = i + 2
                        gp.wait_ge(s_in, ONE + n * 80 + 80)
                        if b:
                            t, k = job(i - 1, "bk3")
                            gp.wait_ge(s_full[t], ONE + k + 1)
                        if c:
                            gp.wait_ge(s_sq, ONE + i)
                        gp.sem_inc(s_go, 1)
                        for e in range(2):
                            for kind, src in ((e, bt), (1 - e, kt)):
                                for h in range(2):
                                    off = 64 * kind + 32 * h
                                    nc.gpsimd.tensor_copy(
                                        by_parity(bk[p][64 * h:64 * h + 64, :, :, off:off + C], e),
                                        by_parity(src[64 * h:64 * h + 64, :, :].rearrange("p j (c t) -> p j c t", t=C), e)
                                    ).then_inc(s_bk, 1)
                    if c:
                        if a1:
                            gp.wait_ge(s_bk, ONE + i * 8 + 24)
                        gp.wait_ge(s_in2, ONE + i * 32)
                        t, k = job(i, "y")
                        gp.wait_ge(s_read[t], ONE + k + 1)
                        nc.gpsimd.tensor_tensor(mo[:, :, :], mo[:, :, :], bonus[:, :, :], ALU.add).then_inc(s_add, 1)
                        gp.wait_ge(s_add, ONE + i)
                        nc.gpsimd.tensor_tensor(mo[:, :, :], mo[:, :, :], gate[:, :, :], ALU.mult).then_inc(s_mo, 1)

                iterations(nc.gpsimd, body)

            @block.scalar
            def _(act):
                act.wait_ge(s_const, ONE + 1)
                act.wait_ge(s_par, ONE + 160)

                def body(i, p):
                    a1, a2, b, c = stages(i)
                    q = 1 - p

                    def read(name, *copies):
                        t, k = job(i, name)
                        act.wait_ge(s_full[t], ONE + k + 1)
                        for out_ap, in_ap in copies:
                            last = nc.scalar.activation(out_ap, in_ap(bank[:, ROT[t], :]), ACT.Copy)
                        last.then_inc(s_read[t], 1)

                    def read_t1(l):
                        act.wait_ge(s_t1, ONE + (i + 1) * 4 + l)
                        nc.scalar.activation(t1[:, :, :], tcol, ACT.Copy).then_inc(s_t1r, 1)

                    def half(n):
                        return lambda v: v.rearrange("p (u k) -> p u k", k=n)

                    def units(lo):
                        return slice(4 * lo, 4 * lo + 4)

                    if a2:
                        read("v", (vd[:, :, :], half(H)),
                             *((by_parity(uv[q][vrows(e)], e), lambda v, e=e: v[vrows(e), :].rearrange("p (j c v) -> p j c v", j=PAIRS, v=H))
                               for e in range(2)))
                        read_t1(1)
                        for n in range(2):
                            read(f"a{n}", (atm[:, units(n), :], half(P)))
                        read_t1(2)
                        for n in range(2):
                            read(f"bk{n}", (bkt[q][:, units(n), :], half(P)))
                        read_t1(3)
                    if c:
                        act.wait_ge(s_var, ONE + i)
                        nc.scalar.activation(stat[:, 2, :], stat[:, 1, :], ACT.Sqrt, scale=1.0 / H, bias=geps[:, 0:1]).then_inc(s_sd, 1)
                    if a2:
                        for n in range(2, 4):
                            read(f"bk{n}", (bkt[q][:, units(n), :], half(P)))
                        read_t1(4)
                    if a1:
                        n = i + 2
                        act.wait_ge(s_in, ONE + n * 80 + 80)
                        for e in range(2):
                            for h in range(2):
                                off = 64 * e + 32 * h
                                nc.scalar.activation(
                                    ab[p][64 * h:64 * h + 64, :, :, off:off + C],
                                    by_parity(ar[p][64 * h:64 * h + 64, 0, :, :].rearrange("p j (c t) -> p j c t", t=C), e),
                                    ACT.Copy).then_inc(s_av, 1)
                        for e in range(2):
                            for h in range(2):
                                off = 64 * (1 - e) + 32 * h
                                nc.scalar.activation(
                                    vb[p][64 * h:64 * h + 64, :, :, off:off + C],
                                    by_parity(vt[64 * h:64 * h + 64, :, :].rearrange("p j (c t) -> p j c t", t=C), e),
                                    ACT.Copy).then_inc(s_av, 1)
                    if b:
                        act.wait_ge(s_y, ONE + i * CH + CH)
                        if c:
                            act.wait_ge(s_yb, ONE + i)
                        for e in range(2):
                            last = nc.scalar.activation(
                                y[vrows(e), :, :, :], by_parity(ybank[vrows(e)].rearrange("p (j c) v -> p j c v", c=CH), e), ACT.Copy)
                        last.then_inc(s_yr, 1)
                    if a2:
                        read("z0", (z0[:, :, :], half(H)))
                    if c:
                        t, k = job(i, "y")
                        act.wait_ge(s_full[t], ONE + k + 1)
                        act.wait_ge(s_mix, ONE + (i - 1) * 16)
                        for j in range(PAIRS):
                            last = nc.scalar.activation(mo[:, j, :], bank[:, ROT[t], j * SC:(j + 1) * SC], ACT.Identity,
                                                        scale=lnw[:, j:j + 1], bias=lnb[:, j:j + 1])
                        last.then_inc(s_read[t], 1)
                    if a2:
                        for n in range(2):
                            read(f"w{n}", *((by_parity(wr[q][:, 2 * n:2 * n + 2, :, 64 * e:64 * e + 64], e),
                                             lambda v, e=e: v.rearrange("p (j c n) -> p j c n", j=2, n=P)[:, :, :, 64 * e:64 * e + 64])
                                            for e in range(2)))
                        read("z", (z[q][:, :, :, :], lambda v: v.rearrange("p (j c v) -> p j c v", j=PAIRS, v=H)))

                iterations(nc.scalar, body)

            @block.vector
            def _(dve):
                dve.wait_ge(s_par, ONE + 160)
                dve.wait_ge(s_const, ONE + 1)
                yv = y[:].rearrange("p j c v -> p (j c) v")

                def body(i, p):
                    a1, a2, b, c = stages(i)
                    q = 1 - p

                    def inverse(l):
                        m = levels[:, l, :].unsqueeze(1).to_broadcast([P, DBL, C])
                        n = (i + 1) * LEVELS + l + 1
                        dve.wait_ge(s_x2, ONE + n)
                        nc.vector.tensor_tensor(xm[:, :, :], xcol, m, ALU.mult).then_inc(s_xm, 1)
                        base = x[:, :, :] if l else ident4[:, :].unsqueeze(1).to_broadcast([P, DBL, C])
                        dve.wait_ge(s_xm, ONE + n)
                        nc.vector.tensor_tensor(x[:, :, :], xm[:, :, :], base, ALU.add).then_inc(s_xc, 1)
                        dve.wait_ge(s_xc, ONE + n)
                        for k in range(4):
                            r = slice(32 * k, 32 * k + 32)
                            last = nc.vector.transpose(xt[r, :, 32 * k:32 * k + 32], x[r, :, :])
                        last.then_inc(s_xt, 1)

                    def solve(c4):
                        e, n = c4 % 2, i * CH + c4 + 1
                        dve.wait_ge(s_p1, ONE + n)
                        nc.vector.tensor_tensor(uv[p][urows(e), :, c4, :],
                                                ybank.rearrange("p (j c) v -> p j c v", c=CH)[urows(e), :, c4, :],
                                                z[p][urows(e), :, c4 // 2, :], ALU.add).then_inc(s_u, 1)

                    def advance(c4):
                        n = i * CH + c4 + 1
                        dve.wait_ge(s_s, ONE + n)
                        nc.vector.tensor_tensor(sumst[:, :, :], bank[:, SB, 0:PAIRS * H].rearrange("p (j v) -> p j v", v=H),
                                                state[:, :, :], ALU.add).then_inc(s_sum, 1)
                        dve.wait_ge(s_sum, ONE + n)
                        nc.vector.tensor_tensor(state[:, :, :], sumst[:, :, :],
                                                pq[:, :, c4:c4 + 1].to_broadcast([P, PAIRS, H]), ALU.mult).then_inc(s_sn, 1)
                        dve.wait_ge(s_sn, ONE + n)

                    if b:
                        nc.vector.tensor_copy(pq[:, :, :], scr["pend"][:, :, bass.ds(i * CH, CH)]).then_inc(s_pq, 1)
                        dve.wait_ge(s_pq, ONE + i + 1)
                    if a2:
                        inverse(0)
                    if b:
                        t, k = job(i - 1, "z")
                        dve.wait_ge(s_read[t], ONE + k + 1)
                        solve(0)
                    if c:
                        g = (i - 1) * 3
                        dve.wait_ge(s_yr, ONE + i)
                        nc.vector.tensor_reduce(stat[:, 0, :], yv, AX.X, ALU.add).then_inc(s_gn, 1)
                        dve.wait_ge(s_gn, ONE + g + 1)
                        nc.vector.tensor_scalar(stat[:, 0, :], stat[:, 0, :], -1.0 / H, None, ALU.mult).then_inc(s_gn, 1)
                    if b:
                        advance(0)
                    if a2:
                        inverse(1)
                    if b:
                        solve(1)
                    if c:
                        dve.wait_ge(s_gn, ONE + g + 2)
                        nc.vector.tensor_tensor(yv, yv, stat[:, 0, :].unsqueeze(2).to_broadcast([P, DBL, H]), ALU.add).then_inc(s_yc, 1)
                    if b:
                        advance(1)
                    if a2:
                        inverse(2)
                    if b:
                        solve(2)
                    if c:
                        dve.wait_ge(s_sq, ONE + i)
                        nc.vector.tensor_reduce(stat[:, 1, :], y2[:, :, :], AX.X, ALU.add).then_inc(s_var, 1)
                    if b:
                        advance(2)
                    if a2:
                        inverse(3)
                    if b:
                        solve(3)
                    if c:
                        dve.wait_ge(s_sd, ONE + i)
                        nc.vector.reciprocal(stat[:, 3, :], stat[:, 2, :]).then_inc(s_gn, 1)
                    if b:
                        advance(3)
                    if c:
                        dve.wait_ge(s_gn, ONE + g + 3)
                        nc.vector.tensor_tensor(yv, yv, stat[:, 3, :].unsqueeze(2).to_broadcast([P, DBL, H]), ALU.mult).then_inc(s_yc2, 1)
                        dve.wait_ge(s_yc2, ONE + i)
                        for h in range(2):
                            last = nc.vector.tensor_scalar(yb[:, :, h, :], yv, hrow[:, h:h + 1], None, ALU.mult)
                        last.then_inc(s_yb, 1)
                    if a2:
                        for e in range(2):
                            for h in range(2):
                                off = 64 * (1 - e) + 32 * h
                                nc.vector.tensor_copy(
                                    by_parity(wr[q][64 * h:64 * h + 64, :, :, off:off + C], e),
                                    by_parity(ar[q][64 * h:64 * h + 64, 1, :, :].rearrange("p j (c t) -> p j c t", t=C), e)
                                ).then_inc(s_rb, 1)
                        inverse(4)
                    if a1:
                        dve.wait_ge(s_gram, ONE + i + 3)
                        g = bank[:, GB:GB + 2, :].rearrange("p b (j c n) -> p (b j) c n", j=2, n=2 * C)
                        for k in range(4):
                            e, r = k // 2, slice(32 * k, 32 * k + 32)
                            m = strict[r, :].unsqueeze(1).unsqueeze(1).to_broadcast([32, PAIRS, CH // 2, C])
                            last = nc.vector.tensor_tensor(aab[p][r, :, 32 * k:32 * k + 32].rearrange("p (j c) t -> p j c t", c=CH // 2),
                                                           by_parity(g[r, :, :, 0:C], e), m, ALU.mult)
                        last.then_inc(s_aab, 1)
                        for k in range(4):
                            e, r, col = 1 - k // 2, slice(32 * k, 32 * k + 32), 32 * ((k + 2) % 4)
                            m = strict[r, :].unsqueeze(1).unsqueeze(1).to_broadcast([32, PAIRS, CH // 2, C])
                            nc.vector.tensor_tensor(aak[p][r, :, col:col + 32].rearrange("p (j c) t -> p j c t", c=CH // 2),
                                                    by_parity(g[r, :, :, 0:C], e), m, ALU.mult)
                        g2 = bank[:, GB:GB + 2, :].rearrange("p b (u n) -> p (b u) n", n=2 * C)
                        if b:
                            dve.wait_ge(s_y, ONE + i * CH + CH)
                        for k in range(4):
                            r = slice(32 * k, 32 * k + 32)
                            m = causal[r, :].unsqueeze(1).to_broadcast([32, UNITS, C])
                            last = nc.vector.tensor_tensor(ark[p][r, :, 32 * (k % 2):32 * (k % 2) + 32], g2[r, :, C:2 * C], m, ALU.mult)
                        last.then_inc(s_gr, 1)

                iterations(nc.vector, body)

            @block.tensor
            def _(pe):
                pe.wait_ge(s_const, ONE + 1)
                pe.wait_ge(s_par, ONE + 160)

                def body(i, p):
                    a1, a2, b, c = stages(i)
                    q = 1 - p

                    def turn(name, matmul, count):
                        t, k = job(i, name)
                        pe.wait_ge(s_read[t], ONE + k)
                        for n in range(count):
                            last = matmul(bank[:, ROT[t], :], n)
                        last.then_inc(s_full[t], 1)

                    def first_x():
                        pe.wait_ge(s_aab, ONE + i + 2)
                        for d in range(DBL):
                            last = nc.tensor.matmul(xcol[:, d, :], aab[q][:, d, :], ident4[:, :], start=True, stop=True)
                        last.then_inc(s_x2, 1)

                    def t1_product(l):
                        pe.wait_ge(s_xc, ONE + (i + 1) * LEVELS + l)
                        for d in range(DBL):
                            last = nc.tensor.matmul(tcol[:, d, :], aab[q][:, d, :], x[:, d, :], start=True, stop=True)
                        last.then_inc(s_t1, 1)

                    def x_product(l):
                        pe.wait_ge(s_t1r, ONE + (i + 1) * 4 + l)
                        pe.wait_ge(s_xt, ONE + (i + 1) * LEVELS + l)
                        for d in range(DBL):
                            last = nc.tensor.matmul(xcol[:, d, :], xt[:, d, :], t1[:, d, :], start=True, stop=True)
                        last.then_inc(s_x2, 1)

                    def from_state(c4):
                        pe.wait_ge(s_sn, ONE + i * CH + c4)
                        for j in range(PAIRS):
                            last = nc.tensor.matmul(ybank[:, j * CH + c4, :], wr[p][:, j, c4, :], state[:, j, :], start=False, stop=True,
                                                    skip_group_check=True)
                        last.then_inc(s_p1, 1)

                    def to_state(c4):
                        pe.wait_ge(s_u, ONE + i * CH + c4 + 1)
                        for j in range(PAIRS):
                            last = nc.tensor.matmul(bank[:, SB, j * H:(j + 1) * H], bkt[p][:, j * CH + c4, :], uv[p][:, j, c4, :],
                                                    start=True, stop=True)
                        last.then_inc(s_s, 1)
                        for j in range(PAIRS):
                            last = nc.tensor.matmul(ybank[vrows(c4 % 2), j * CH + c4, :], ark[p][:, j * CH + c4, :], uv[p][:, j, c4, :],
                                                    start=False, stop=True, skip_group_check=True)
                        last.then_inc(s_y, 1)

                    def a_transposes(n):
                        turn(f"a{n}", lambda o, d: nc.tensor.transpose(o[:, d * P:(d + 1) * P], ab[q][:, 2 * n + d // 2, d % 2, :], ident[:, :]), 4)

                    def bk_transposes(n):
                        turn(f"bk{n}", lambda o, u: nc.tensor.transpose(o[:, u * P:(u + 1) * P], bk[q][:, n, u, :], ident[:, :]), 4)

                    def grams(n):
                        if n == 0:
                            pe.wait_ge(s_bk, ONE + i * 8 + 24)
                            pe.wait_ge(s_gr, ONE + i + 2)
                        for j in range(2 * n, 2 * n + 2):
                            for u in range(CH):
                                k = (j - 2 * n) * CH + u
                                last = nc.tensor.matmul(bank[:, GB + n, k * 64:(k + 1) * 64], bk[p][:, j, u, :],
                                                        ar[p][:, :, j, u * C:(u + 1) * C], start=True, stop=True)
                        if n == 1:
                            last.then_inc(s_gram, 1)

                    if a2:
                        first_x()
                        pe.wait_ge(s_av, ONE + i * 8 + 16)
                        turn("v", lambda o, d: nc.tensor.matmul(o[:, d * H:(d + 1) * H], vb[q][:, d // 2, d % 2, :], ident2[:, :],
                                                                start=True, stop=True), DBL)
                    if b:
                        pe.wait_ge(s_yr, ONE + i)
                        pe.wait_ge(s_rb, ONE + i * 4 + 4)
                        t, k = job(i - 1, "w1")
                        pe.wait_ge(s_read[t], ONE + k + 1)
                        for n in range(2):
                            nc.tensor.matmul(bank[:, YB + n, :], zeros[:, 0:P], zeros[:, P:P + 512], start=True, stop=True)
                        from_state(0)
                    if a2:
                        t1_product(1)
                        a_transposes(0)
                    if b:
                        to_state(0)
                    if a2:
                        x_product(1)
                        a_transposes(1)
                    if b:
                        from_state(1)
                    if a2:
                        t1_product(2)
                        bk_transposes(0)
                    if b:
                        to_state(1)
                    if a2:
                        x_product(2)
                        bk_transposes(1)
                    if b:
                        from_state(2)
                    if a2:
                        t1_product(3)
                        bk_transposes(2)
                    if b:
                        to_state(2)
                    if a2:
                        x_product(3)
                        bk_transposes(3)
                    if b:
                        from_state(3)
                    if a2:
                        t1_product(4)
                    if a1:
                        grams(0)
                    if b:
                        to_state(3)
                    if a2:
                        x_product(4)
                    if a1:
                        grams(1)
                    if a2:
                        turn("z0", lambda o, d: nc.tensor.matmul(o[:, d * H:(d + 1) * H], aak[q][:, d, :], vd[:, d, :], start=True, stop=True), DBL)
                    if c:
                        pe.wait_ge(s_yb, ONE + i)
                        turn("y", lambda o, d: nc.tensor.matmul(o[:, d * 2 * C:(d + 1) * 2 * C], yb[:, d, :, :].rearrange("p h v -> p (h v)"),
                                                                rows[:, :], start=True, stop=True), DBL)
                    if a2:
                        pe.wait_ge(s_xt, ONE + (i + 2) * LEVELS)
                        for n in range(2):
                            turn(f"w{n}", lambda o, d: nc.tensor.matmul(o[:, d * P:(d + 1) * P], atm[:, 4 * n + d, :], xt[:, 4 * n + d, :],
                                                                        start=True, stop=True), 4)
                        t, k = job(i, "z0")
                        pe.wait_ge(s_read[t], ONE + k + 1)
                        turn("z", lambda o, d: nc.tensor.matmul(o[:, d * H:(d + 1) * H], xt[:, d, :], z0[:, d, :], start=True, stop=True), DBL)

                iterations(nc.tensor, body)


def phase_ffn(nc, a, scr, out):
    ctx, sems = ExitStack(), []
    with ctx:
        def sb(name, shape, dt=F32):
            return ctx.enter_context(nc.sbuf_tensor("p3_" + name, shape, dt))

        def sem(name):
            sems.append(ctx.enter_context(nc.semaphore("p3_" + name)))
            return sems[-1]

        KO = KT
        NDN = KO + FF
        HALF = D_MODEL // TB
        mraw = sb("mraw", [P, KO, TB])
        hT_hi = sb("hT_hi", [P, KT, TB], F32R)
        hT_lo = sb("hT_lo", [P, KT, TB], F32R)
        x = sb("x", [P, TT, D_MODEL])
        acc = sb("acc", [P, TT, D_MODEL])
        hs = sb("hs", [P, 2, D_MODEL])
        up_raw = [sb(f"up_raw{i}", [P, 2, KT, P]) for i in range(2)]
        up_hi = [sb(f"up_hi{i}", [P, 2, KT, P], F32R) for i in range(2)]
        up_lo = [sb(f"up_lo{i}", [P, 2, KT, P], F32R) for i in range(2)]
        dn_raw = [sb(f"dn_raw{i}", [P, D_MODEL]) for i in range(2)]
        dn_hi = [sb(f"dn_hi{i}", [P, D_MODEL], F32R) for i in range(2)]
        dn_lo = [sb(f"dn_lo{i}", [P, D_MODEL], F32R) for i in range(2)]
        ub = [sb(f"ub{i}", [P, 2, 2 + TB]) for i in range(2)]
        cv = [sb(f"cv{i}", [P, 2, TB]) for i in range(2)]
        ah = [sb(f"ah{i}", [P, TB]) for i in range(2)]
        a_hi = [sb(f"a_hi{i}", [P, TB], F32R) for i in range(2)]
        a_lo = [sb(f"a_lo{i}", [P, TB], F32R) for i in range(2)]
        cpar = [sb(f"cpar{i}", [P, 2, 4]) for i in range(2)]
        cw = sb("cw", [P, 2, FF, 4])
        tail = sb("tail", [P, 2, FF, 2])
        gpost = sb("gpost", [P, D_MODEL])
        gffn = sb("gffn", [P, D_MODEL])
        gain = sb("gain", [P, KT])
        ss = sb("ss", [P, 3, TT])
        rstd = sb("rstd", [P, 3, TT])
        eps = sb("eps", [P, 1])
        ident = sb("ident", [P, P])
        bank = ctx.enter_context(nc.psum_tensor("p3_bank", [P, 8, 512], F32))

        s_par = sem("params_loaded")
        s_const = sem("zeros_written")
        s_mix = sem("mix_loaded")
        s_x = sem("x_loaded")
        s_up = [sem(f"up_loaded{i}") for i in range(2)]
        s_dn = [sem(f"dn_loaded{i}") for i in range(2)]
        s_mh = sem("mix_hi_ready")
        s_ml = sem("mix_lo_ready")
        s_uh = sem("up_hi_ready")
        s_ul = sem("up_lo_ready")
        s_dh = sem("dn_hi_ready")
        s_dl = sem("dn_lo_ready")
        s_op = sem("out_proj_tile")
        s_sq = sem("squares_summed")
        s_rt = sem("rms_root")
        s_rc = sem("rms_recip")
        s_x2 = sem("x_updated")
        s_xs = sem("x_scaled")
        s_tr = sem("transposed")
        s_ht = sem("hT_ready")
        s_zero = sem("acc_zeroed")
        s_upd = sem("up_done")
        s_tl = sem("tail_used")
        s_ub = sem("up_read")
        s_tap = sem("tap_bias")
        s_cv = sem("conv_done")
        s_gl = sem("gelu_done")
        s_a = sem("hidden_ready")
        s_ah = sem("hidden_hi_ready")
        s_al = sem("hidden_lo_ready")
        s_db = sem("down_bank_done")
        s_acc = sem("down_bank_added")
        s_fin = sem("block_ready")
        s_out = sem("block_stored")
        s_dve = sem("dve_step")
        s_go = sem("gpsimd_started")

        upv = a["w_up"][0].rearrange("(k p) (s n) -> p s k n", p=P, s=2)
        xv = a["x"][0].rearrange("(t p) d -> p t d", p=P)
        ov = out[0].rearrange("(t p) d -> p t d", p=P)
        NPAR = 1 + 2 + 1 + 2 * (CONV_WIDTH + 1)

        with ExitStack():
            credit(nc, sems)
        with nc.Block() as block:
            @block.sync
            def _(sp):
                with nc.allow_non_contiguous_dma(reason="per-feature parameters, once"):
                    sp.dma_start(gain[:, :], a["pre_ffn_norm"][0].rearrange("(t p) -> p t", p=P)).then_inc(s_par, 16)
                    sp.dma_start(gpost[:, :], a["post_mix_norm"][0].partition_broadcast(P)).then_inc(s_par, 16)
                    sp.dma_start(gffn[:, :], a["post_ffn_norm"][0].partition_broadcast(P)).then_inc(s_par, 16)
                    sp.dma_start(ident[:, :], const_view(a, "ident")).then_inc(s_par, 16)
                    for s in range(2):
                        for tap in range(CONV_WIDTH):
                            sp.dma_start(cw[:, s, :, tap], a["conv_w"][0, tap, s * D_FF:(s + 1) * D_FF].rearrange("(f p) -> p f", p=P)
                                         ).then_inc(s_par, 16)
                        sp.dma_start(cw[:, s, :, CONV_WIDTH], a["conv_b"][0, s * D_FF:(s + 1) * D_FF].rearrange("(f p) -> p f", p=P)
                                     ).then_inc(s_par, 16)

                def load_up(b, g, s):
                    n = b * FF + g * GROUP + (0 if s == 0 else s - 1)
                    sp.wait_ge(s_uh, ONE + n)
                    sp.wait_ge(s_ul, ONE + n)
                    sp.dma_start(up_raw[s][:, 0, :, :], upv[:, 0, :, bass.ds((g * GROUP + s) * P, P)]).then_inc(s_up[s], 16)
                    sp.dma_start(up_raw[s][:, 1, :, :], upv[:, 1, :, bass.ds((g * GROUP + s) * P, P)]).then_inc(s_up[s], 16)

                def load_dn(b, n, s, src):
                    w = b * NDN + n - (0 if s == 0 else 1)
                    sp.wait_ge(s_dh, ONE + w)
                    sp.wait_ge(s_dl, ONE + w)
                    sp.dma_start(dn_raw[s][:, :], src).then_inc(s_dn[s], 16)

                with nc.sync.Fori(0, BLOCKS) as b:
                    sp.wait_ge(s_mh, ONE + b)
                    sp.wait_ge(s_ml, ONE + b)
                    sp.dma_start(mraw[:, :, :], scr["mix"][:, :, bass.ds(b * TB, TB)]).then_inc(s_mix, 16)
                    for s in range(GROUP):
                        load_up(b, 0, s)
                    for k in range(KO):
                        load_dn(b, k, k % 2, a["w_out"][0, k * P:(k + 1) * P, :])
                        if k == 1:
                            sp.wait_ge(s_out, ONE + b * 16)
                            sp.dma_start(x[:, :, :], xv[:, bass.ds(b * TT, TT), :]).then_inc(s_x, 16)
                    with nc.sync.Fori(0, GROUPS - 1) as g:
                        load_up(b, g + 1, 0)
                        for s in range(GROUP):
                            load_dn(b, KO + g * GROUP + s, s, a["w_down"][0, bass.ds((g * GROUP + s) * P, P), :])
                        load_up(b, g + 1, 1)
                    for s in range(GROUP):
                        f = (GROUPS - 1) * GROUP + s
                        load_dn(b, KO + f, s, a["w_down"][0, f * P:(f + 1) * P, :])
                    sp.wait_ge(s_fin, ONE + b * TT + TT)
                    sp.dma_start(ov[:, bass.ds(b * TT, TT), :], x[:, :, :]).then_inc(s_out, 16)
                sp.wait_ge(s_out, ONE + 16 * BLOCKS)

            @block.gpsimd
            def _(gp):
                nc.gpsimd.memset(eps[:, :], NORM_EPS)
                nc.gpsimd.memset(tail[:, :, :, :], 0.0).then_inc(s_const, 1)

                def low_up(b, g, s):
                    n = b * FF + g * GROUP + s
                    gp.wait_ge(s_uh, ONE + n + 1)
                    nc.gpsimd.tensor_tensor(up_lo[s][:, :, :, :], up_raw[s][:, :, :, :], up_hi[s][:, :, :, :].bitcast(F32),
                                            ALU.subtract).then_inc(s_ul, 1)

                def low_dn(b, n, s):
                    gp.wait_ge(s_dh, ONE + b * NDN + n + 1)
                    nc.gpsimd.tensor_tensor(dn_lo[s][:, :], dn_raw[s][:, :], dn_hi[s][:, :].bitcast(F32),
                                            ALU.subtract).then_inc(s_dl, 1)

                with nc.gpsimd.Fori(0, BLOCKS) as b:
                    for s in range(GROUP):
                        low_up(b, 0, s)
                    gp.wait_ge(s_mh, ONE + b + 1)
                    nc.gpsimd.tensor_tensor(hT_lo[:, :, :], mraw[:, :, :], hT_hi[:, :, :].bitcast(F32), ALU.subtract).then_inc(s_ml, 1)
                    for k in range(KO):
                        low_dn(b, k, k % 2)
                    gp.wait_ge(s_tr, ONE + b * KT + KT)
                    gp.sem_inc(s_go, 1)
                    nc.gpsimd.memset(acc[:, :, :], 0.0).then_inc(s_zero, 1)
                    with nc.gpsimd.Fori(0, GROUPS - 1) as g:
                        low_up(b, g + 1, 0)
                        for s in range(GROUP):
                            low_dn(b, KO + g * GROUP + s, s)
                        low_up(b, g + 1, 1)
                    for s in range(GROUP):
                        low_dn(b, KO + (GROUPS - 1) * GROUP + s, s)

            @block.scalar
            def _(act):
                act.wait_ge(s_const, ONE + 1)
                act.wait_ge(s_par, ONE + 16 * NPAR)

                def high_up(b, g, s):
                    act.wait_ge(s_up[s], ONE + (b * GROUPS + g) * 32 + 32)
                    nc.scalar.activation(up_hi[s][:, :, :, :], up_raw[s][:, :, :, :], ACT.Copy).then_inc(s_uh, 1)

                def high_dn(b, n, s):
                    act.wait_ge(s_dn[s], ONE + (b * (NDN // 2)) * 16 + (n - s) * 8 + 16)
                    nc.scalar.activation(dn_hi[s][:, :], dn_raw[s][:, :], ACT.Copy).then_inc(s_dh, 1)

                def read_up(b, g, s):
                    n = b * FF + g * GROUP + s
                    act.wait_ge(s_upd, ONE + n + 1)
                    act.wait_ge(s_a, ONE + b * FF + g * GROUP + (0 if s == 0 else s - 1))
                    nc.scalar.activation(ub[s][:, :, 2:2 + TB], bank[:, 2 * s:2 * s + 2, :], ACT.Copy).then_inc(s_ub, 1)
                    nc.scalar.activation(ub[s][:, :, 0:2], tail[:, :, bass.ds(g * GROUP + s, 1), :].rearrange("p s f t -> p s (f t)"),
                                         ACT.Copy)
                    nc.scalar.activation(cpar[s][:, :, :], cw[:, :, bass.ds(g * GROUP + s, 1), :].rearrange("p s f t -> p s (f t)"),
                                         ACT.Copy).then_inc(s_tl, 1)

                def taps(b, g, s):
                    n = b * FF + g * GROUP + s
                    act.wait_ge(s_ub, ONE + n + 1)
                    act.wait_ge(s_tl, ONE + n + 1)
                    for i in range(2):
                        last = nc.scalar.activation(cv[s][:, i, :], ub[s][:, i, 2:2 + TB], ACT.Identity,
                                                    scale=cpar[s][:, i, 2:3], bias=cpar[s][:, i, 3:4])
                    last.then_inc(s_tap, 1)
                    nc.scalar.activation(tail[:, :, bass.ds(g * GROUP + s, 1), :].rearrange("p s f t -> p s (f t)"),
                                         ub[s][:, :, TB:TB + 2], ACT.Copy)

                def gelu(b, g, s):
                    n = b * FF + g * GROUP + s
                    act.wait_ge(s_cv, ONE + n + 1)
                    nc.scalar.activation(cv[s][:, 0, :], cv[s][:, 0, :], ACT.Gelu_apprx_tanh).then_inc(s_gl, 1)

                def high_a(b, g, s):
                    n = b * FF + g * GROUP + s
                    act.wait_ge(s_a, ONE + n + 1)
                    nc.scalar.activation(a_hi[s][:, :], ah[s][:, :], ACT.Copy).then_inc(s_ah, 1)

                def group(b, g, last):
                    read_up(b, g, 0)
                    if not last:
                        high_up(b, g + 1, 0)
                    taps(b, g, 0)
                    gelu(b, g, 0)
                    act.wait_ge(s_db, ONE + (b * GROUPS + g) * 8)
                    for s in range(GROUP):
                        high_dn(b, KO + g * GROUP + s, s)
                    high_a(b, g, 0)
                    read_up(b, g, 1)
                    if not last:
                        high_up(b, g + 1, 1)
                    taps(b, g, 1)
                    gelu(b, g, 1)
                    high_a(b, g, 1)

                def root(b, i):
                    act.wait_ge(s_sq, ONE + (b * 3 + i) * TT + TT)
                    nc.scalar.activation(rstd[:, i, :], ss[:, i, :], ACT.Sqrt, scale=1.0 / D_MODEL, bias=eps[:, 0:1]).then_inc(s_rt, 1)

                with nc.scalar.Fori(0, BLOCKS) as b:
                    act.wait_ge(s_upd, ONE + b * FF)
                    for s in range(GROUP):
                        high_up(b, 0, s)
                    act.wait_ge(s_mix, ONE + b * 16 + 16)
                    nc.scalar.activation(hT_hi[:, :, :], mraw[:, :, :], ACT.Copy).then_inc(s_mh, 1)
                    act.wait_ge(s_db, ONE + b * (GROUPS * 8))
                    for k in range(KO):
                        if k >= 2:
                            act.wait_ge(s_op, ONE + b * KO + k - 1)
                        high_dn(b, k, k % 2)
                    act.wait_ge(s_op, ONE + b * KO + KO)
                    for t in range(TT):
                        if t >= 2 or True:
                            act.wait_ge(s_sq, ONE + (b * 3) * TT + (t - 1 if t else 0))
                        nc.scalar.activation(hs[:, t % 2, :], bank[:, 2 * t:2 * t + 2, :].rearrange("p h d -> p (h d)"), ACT.Square,
                                             accum_out=ss[:, 0, t:t + 1]).then_inc(s_sq, 1)
                    root(b, 0)
                    for t in range(TT):
                        act.wait_ge(s_x2, ONE + b * TT + t + 1)
                        nc.scalar.activation(acc[:, t, :], x[:, t, :], ACT.Square, accum_out=ss[:, 1, t:t + 1]).then_inc(s_sq, 1)
                    root(b, 1)
                    act.wait_ge(s_rc, ONE + b * 3 + 2)
                    for t in range(TT):
                        nc.scalar.activation(acc[:, t, :], x[:, t, :], ACT.Copy, scale=rstd[:, 1, t:t + 1]).then_inc(s_xs, 1)
                    with nc.scalar.Fori(0, GROUPS - 1) as g:
                        group(b, g, False)
                    group(b, GROUPS - 1, True)
                    act.wait_ge(s_acc, ONE + (b + 1) * (GROUPS * 8))
                    for t in range(TT):
                        act.wait_ge(s_sq, ONE + (b * 3 + 2) * TT + (t - 1 if t else 0))
                        nc.scalar.activation(hs[:, t % 2, :], acc[:, t, :], ACT.Square, accum_out=ss[:, 2, t:t + 1]).then_inc(s_sq, 1)
                    root(b, 2)

            @block.vector
            def _(dve):
                dve.wait_ge(s_par, ONE + 16 * NPAR)

                def conv(st, b, g, s):
                    n = b * FF + g * GROUP + s
                    dve.wait_ge(s_tap, ONE + n + 1)
                    for i in range(2):
                        st.do(nc.vector.scalar_tensor_tensor(cv[s][:, i, :], ub[s][:, i, 1:1 + TB], cpar[s][:, i, 1:2],
                                                             cv[s][:, i, :], ALU.mult, ALU.add))
                    st.wait()
                    for i in range(2):
                        last = nc.vector.scalar_tensor_tensor(cv[s][:, i, :], ub[s][:, i, 0:TB], cpar[s][:, i, 0:1],
                                                              cv[s][:, i, :], ALU.mult, ALU.add)
                    last.then_inc(s_cv, 1)
                    dve.wait_ge(s_gl, ONE + n + 1)
                    dve.wait_ge(s_ah, ONE + b * FF + g * GROUP + (0 if s == 0 else s - 1))
                    nc.vector.tensor_tensor(ah[s][:, :], cv[s][:, 0, :], cv[s][:, 1, :], ALU.mult).then_inc(s_a, 1)

                def low_a(b, g, s):
                    dve.wait_ge(s_ah, ONE + b * FF + g * GROUP + s + 1)
                    nc.vector.tensor_tensor(a_lo[s][:, :], ah[s][:, :], a_hi[s][:, :].bitcast(F32), ALU.subtract).then_inc(s_al, 1)

                def add_down(b, g):
                    for n in range(TT * HALF):
                        dve.wait_ge(s_db, ONE + (b * GROUPS + g) * 8 + n + 1)
                        dst = acc[:, n // HALF, (n % HALF) * TB:(n % HALF + 1) * TB]
                        nc.vector.tensor_tensor(dst, bank[:, 4 + n % 4, :], dst, ALU.add).then_inc(s_acc, 1)

                def group(st, b, g, first):
                    conv(st, b, g, 0)
                    if not first:
                        dve.wait_ge(s_acc, ONE + (b * GROUPS + g - 1) * 8)
                        add_down(b, g - 1)
                    low_a(b, g, 0)
                    conv(st, b, g, 1)
                    low_a(b, g, 1)

                def residual(b, i, sem_done, src, gain_row):
                    dve.wait_ge(s_rt, ONE + b * 3 + (0 if i == 0 else 2) + 1)
                    j = 0 if i == 0 else 2
                    nc.vector.reciprocal(rstd[:, j, :], rstd[:, j, :]).then_inc(s_rc, 1)
                    dve.wait_ge(s_rc, ONE + b * 3 + j + 1)
                    for t in range(TT):
                        if t >= 2:
                            dve.wait_ge(sem_done[0], sem_done[1] + t - 1)
                        st2 = nc.vector.scalar_tensor_tensor(hs[:, t % 2, :], src(t), rstd[:, j, t:t + 1], gain_row[:, :], ALU.mult, ALU.mult)
                        yield t, st2

                K = 2 * TT + KT + FF * 2
                with nc.vector.Fori(0, BLOCKS) as b:
                    st = Steps(dve, s_dve, b * K)
                    dve.wait_ge(s_x, ONE + b * 16 + 16)
                    base = ONE + b * TT
                    for t, ins in residual(b, 0, (s_x2, base), lambda t: bank[:, 2 * t:2 * t + 2, :].rearrange("p h d -> p (h d)"), gpost):
                        st.link(ins)
                        nc.vector.tensor_tensor(x[:, t, :], x[:, t, :], hs[:, t % 2, :], ALU.add).then_inc(s_x2, 1)
                    dve.wait_ge(s_rt, ONE + b * 3 + 2)
                    nc.vector.reciprocal(rstd[:, 1, :], rstd[:, 1, :]).then_inc(s_rc, 1)
                    for k in range(KT):
                        dve.wait_ge(s_tr, ONE + b * KT + k + 1)
                        st.link(nc.vector.tensor_scalar(hT_hi[:, k, :], bank[:, k % 2, :], gain[:, k:k + 1], None, ALU.mult))
                        nc.vector.scalar_tensor_tensor(hT_lo[:, k, :], bank[:, k % 2, :], gain[:, k:k + 1],
                                                       hT_hi[:, k, :].bitcast(F32), ALU.mult, ALU.subtract).then_inc(s_ht, 1)
                    dve.wait_ge(s_zero, ONE + b + 1)
                    group(st, b, 0, True)
                    inner = st.n
                    with nc.vector.Fori(1, GROUPS) as g:
                        sg = Steps(dve, s_dve, b * K + inner + (g - 1) * 4)
                        group(sg, b, g, False)
                        assert sg.n == 4
                    st.n = inner + (GROUPS - 1) * 4
                    add_down(b, GROUPS - 1)
                    dve.wait_ge(s_acc, ONE + (b + 1) * (GROUPS * 8))
                    for t, ins in residual(b, 1, (s_fin, ONE + b * TT), lambda t: acc[:, t, :], gffn):
                        st.link(ins)
                        nc.vector.tensor_tensor(x[:, t, :], x[:, t, :], hs[:, t % 2, :], ALU.add).then_inc(s_fin, 1)
                    assert st.n == K, (st.n, K)

            @block.tensor
            def _(pe):
                pe.wait_ge(s_par, ONE + 16 * NPAR)

                def up(b, g, s):
                    n = b * FF + g * GROUP + s
                    pe.wait_ge(s_uh, ONE + n + 1)
                    pe.wait_ge(s_ul, ONE + n + 1)
                    pe.wait_ge(s_ub, ONE + b * FF + g * GROUP + (0 if s == 0 else s - 1))
                    for i in range(2):
                        for k in range(KT):
                            last = split_matmul(nc, bank[:, 2 * s + i, :], up_hi[s][:, i, k, :], up_lo[s][:, i, k, :],
                                                hT_hi[:, k, :], hT_lo[:, k, :], k == 0, k == KT - 1)
                    last.then_inc(s_upd, 1)

                def down(b, g):
                    pe.wait_ge(s_ah, ONE + b * FF + g * GROUP + GROUP)
                    pe.wait_ge(s_al, ONE + b * FF + g * GROUP + GROUP)
                    pe.wait_ge(s_dh, ONE + b * NDN + KO + g * GROUP + GROUP)
                    pe.wait_ge(s_dl, ONE + b * NDN + KO + g * GROUP + GROUP)
                    for n in range(TT * HALF):
                        t, h = n // HALF, n % HALF
                        pe.wait_ge(s_acc, ONE + (b * GROUPS + g) * 8 + (n - 3 if n >= 4 else 0))
                        for s in range(GROUP):
                            last = split_matmul(nc, bank[:, 4 + n % 4, :], a_hi[s][:, t * P:(t + 1) * P], a_lo[s][:, t * P:(t + 1) * P],
                                                dn_hi[s][:, h * TB:(h + 1) * TB], dn_lo[s][:, h * TB:(h + 1) * TB],
                                                s == 0, s == GROUP - 1)
                        last.then_inc(s_db, 1)

                with nc.tensor.Fori(0, BLOCKS) as b:
                    pe.wait_ge(s_mh, ONE + b + 1)
                    pe.wait_ge(s_ml, ONE + b + 1)
                    pe.wait_ge(s_acc, ONE + b * (GROUPS * 8))
                    for k in range(KO):
                        pe.wait_ge(s_dh, ONE + b * NDN + k + 1)
                        pe.wait_ge(s_dl, ONE + b * NDN + k + 1)
                        for t in range(TT):
                            for h in range(HALF):
                                last = split_matmul(nc, bank[:, 2 * t + h, :], hT_hi[:, k, t * P:(t + 1) * P], hT_lo[:, k, t * P:(t + 1) * P],
                                                    dn_hi[k % 2][:, h * TB:(h + 1) * TB], dn_lo[k % 2][:, h * TB:(h + 1) * TB],
                                                    k == 0, k == KO - 1)
                        last.then_inc(s_op, 1)
                    pe.wait_ge(s_xs, ONE + b * TT + TT)
                    for k in range(KT):
                        if k >= 2:
                            pe.wait_ge(s_ht, ONE + b * KT + k - 1)
                        for t in range(TT):
                            last = nc.tensor.transpose(bank[:, k % 2, t * P:(t + 1) * P], acc[:, t, k * P:(k + 1) * P], ident[:, :])
                        last.then_inc(s_tr, 1)
                    pe.wait_ge(s_ht, ONE + b * KT + KT)
                    up(b, 0, 0)
                    up(b, 0, 1)
                    with nc.tensor.Fori(1, GROUPS) as g:
                        up(b, g, 0)
                        down(b, g - 1)
                        up(b, g, 1)
                    down(b, GROUPS - 1)


_INS = ['x', 'pre_mix_norm', 'w_in', 'mu_shift', 'w0', 'w_decay_up', 'a0', 'w_aaa_up', 'w_gate_up', 'k_k', 'k_a', 'r_k',
        'ln_x_w', 'ln_x_b', 'w_pool', 'pool_scale', 'w_out', 'post_mix_norm', 'pre_ffn_norm', 'w_up', 'conv_w', 'conv_b',
        'w_down', 'post_ffn_norm']

def build(nc, a, out):
    def scratch(name, shape):
        return nc.dram_tensor("scratch_" + name, shape, F32).ap()

    with ExitStack() as ctx:
        pend = ctx.enter_context(nc.sbuf_tensor("chunk_decay", [P, PAIRS, SEQ // C], F32))
        scr = {k: scratch(k, (P, PAIRS, SEQ)) for k in ("rt", "at", "bt", "kt", "v", "bonus", "g")}
        scr["mix"] = scratch("mix", (P, 2 * PAIRS, SEQ))
        scr["pend"] = pend
        phase_project(nc, a, scr)
        phase_recur(nc, a, scr)
        phase_ffn(nc, a, scr, out)


def kernel(**inputs):
    import concourse.bacc as bacc
    from concourse.bass_utils import run_bass_kernel_spmd

    nc = bacc.Bacc("TRN2", target_bir_lowering=False, num_devices=1)
    arrays = {"in_" + k: np.ascontiguousarray(inputs[k]) for k in _INS}
    arrays["in_consts"] = constants()
    a = {k[3:]: nc.dram_tensor(k, v.shape, mybir.dt.from_np(v.dtype), kind="ExternalInput").ap() for k, v in arrays.items()}
    out = nc.dram_tensor("out", (1, SEQ, D_MODEL), F32, kind="ExternalOutput").ap()
    build(nc, a, out)
    r = run_bass_kernel_spmd(nc, [arrays], core_ids=[0])
    return r.results[0]["out"]
```

```python
import math
from contextlib import ExitStack

import numpy as np

import concourse.bass as bass
from concourse import mybir

F32 = mybir.dt.float32
F32R = mybir.dt.float32r
ALU = mybir.AluOpType
ACT = mybir.ActivationFunctionType
AX = mybir.AxisListType

P = 128
D_MODEL, SEQ = 1024, 2048
RWKV_WIDTH, POOL_WIDTH, HEAD_DIM = 512, 512, 64
DECAY_LORA = AAA_LORA = 64
GATE_LORA = 128
IN_COLS = 3 * RWKV_WIDTH + DECAY_LORA + AAA_LORA + GATE_LORA + POOL_WIDTH
D_FF = 2816
CONV_WIDTH = 3
NORM_EPS, GN_EPS = 1e-6, 64e-5

TB = 512
BLOCKS = SEQ // TB
TT = TB // P
KT = D_MODEL // P
FT = IN_COLS // P
PAIRS = RWKV_WIDTH // P
SHIFTED = 14
LORA, GATE, R0, K0, V0, POOL0 = 0, 1, 2, 6, 10, 14
HALO = 16
C = 32
SC = P
CH = SC // C
UNITS = PAIRS * CH
DBL = UNITS // 2
FF = D_FF // P
GROUP = 2
GROUPS = FF // GROUP


CONSTS = {}


def _layout():
    at = 0
    for name, shape in (("ident", (P,)), ("head_ones", (P,)), ("head_sums", (PAIRS, 2 * PAIRS)), ("head_spread", (PAIRS, P)),
                        ("reset", (TB,)), ("cinv", (PAIRS, HALO)),
                        ("ident2", (HEAD_DIM,)), ("ident4", (C,)), ("strict", (C,)), ("causal", (C,)),
                        ("levels", (5, C)), ("rows_to_tokens", (2 * C,)), ("head_rows", (2,))):
        size = math.prod(shape)
        CONSTS[name] = (at, size, shape)
        at += size



_layout()


def constants():
    p = np.arange(P)[:, None]
    t = np.arange(C)[None, :]
    s = p % C
    parts = {
        "ident": p == np.arange(P)[None, :],
        "head_ones": p // HEAD_DIM == np.arange(P)[None, :] // HEAD_DIM,
        "head_sums": np.concatenate([2 * j + p // HEAD_DIM == np.arange(2 * PAIRS)[None, :] for j in range(PAIRS)], axis=1),
        "head_spread": np.concatenate([p == 2 * j + np.arange(P)[None, :] // HEAD_DIM for j in range(PAIRS)], axis=1),
        "reset": np.broadcast_to(np.arange(TB)[None, :] % C != 0, (P, TB)),
        "cinv": np.broadcast_to(1.0 / np.minimum(np.arange(HALO)[None, :] + 1, 2.0 ** np.arange(1, PAIRS + 1)[:, None]).reshape(1, -1),
                                (P, PAIRS * HALO)),
        "ident2": p % HEAD_DIM == np.arange(HEAD_DIM)[None, :],
        "ident4": s == t,
        "strict": s < t,
        "causal": s <= t,
        "levels": np.concatenate([(s >> (l + 1) == t >> (l + 1)) & ((s >> l) % 2 == 1) & ((t >> l) % 2 == 0)
                                  for l in range(5)], axis=1),
        "rows_to_tokens": (1 - p // HEAD_DIM) * C + s == np.arange(2 * C)[None, :],
        "head_rows": (p // C) % 2 == np.arange(2)[None, :],
    }
    return np.concatenate([np.asarray(parts[k], np.float32) for k in CONSTS], axis=1)


def const_view(a, name):
    at, size, shape = CONSTS[name]
    v = a["consts"][:, at:at + size]
    return v.rearrange("p (a b) -> p a b", b=shape[1]) if len(shape) == 2 else v


class Steps:

    def __init__(self, eng, sem, base=0):
        self.eng, self.sem, self.base, self.n = eng, sem, base, 0

    def do(self, ins):
        ins.then_inc(self.sem, 1)
        self.n += 1
        return self.n

    def wait(self, n=None):
        self.eng.wait_ge(self.sem, ONE + self.base + (self.n if n is None else n))

    def link(self, ins):
        self.do(ins)
        self.wait()


ONE = 1


def credit(nc, sems):
    with nc.Block() as block:
        @block.sync
        def _(sp):
            for s in sems:
                sp.sem_inc(s, ONE)


def split_matmul(nc, out, lhs_hi, lhs_lo, rhs_hi, rhs_lo, start, stop):
    nc.tensor.matmul(out, lhs_hi, rhs_hi, start=start, stop=False)
    nc.tensor.matmul(out, lhs_hi, rhs_lo, start=False, stop=False)
    return nc.tensor.matmul(out, lhs_lo, rhs_hi, start=False, stop=stop)


def phase_project(nc, a, scr):
    ctx, sems = ExitStack(), []
    with ctx:
        def sb(name, shape, dt=F32):
            return ctx.enter_context(nc.sbuf_tensor("p1_" + name, shape, dt))

        def sem(name):
            sems.append(ctx.enter_context(nc.semaphore("p1_" + name)))
            return sems[-1]

        xin = sb("xin", [P, TT, D_MODEL])
        hT_hi = sb("hT_hi", [P, KT, TB], F32R)
        hT_lo = sb("hT_lo", [P, KT, TB], F32R)
        w_raw = [sb(f"w_raw{i}", [P, KT, P]) for i in range(2)]
        w_hi = [sb(f"w_hi{i}", [P, KT, P], F32R) for i in range(2)]
        w_lo = [sb(f"w_lo{i}", [P, KT, P], F32R) for i in range(2)]
        proj = sb("proj", [P, FT, HALO + TB])
        um = sb("um", [P, SHIFTED, TB])
        dec = sb("dec", [P, PAIRS, TB])
        alpha = sb("alpha", [P, PAIRS, TB])
        cum = sb("cum", [P, PAIRS, TB])
        einv = sb("einv", [P, PAIRS, TB])
        kk = sb("kk", [P, PAIRS, TB])
        tmp = sb("tmp", [P, PAIRS, TB])
        gate = sb("gate", [P, PAIRS, TB])
        ident = sb("ident", [P, P])
        head_ones = sb("head_ones", [P, P])
        head_sums = sb("head_sums", [P, PAIRS, 2 * PAIRS])
        head_spread = sb("head_spread", [2 * PAIRS, PAIRS, P])
        norm = sb("norm", [2 * PAIRS, TB])
        reset = sb("reset", [P, TB])
        cinv = sb("cinv", [P, PAIRS, HALO])
        wlora = sb("wlora", [P, RWKV_WIDTH])
        wgate = sb("wgate", [P, RWKV_WIDTH])
        wpool = sb("wpool", [P, PAIRS, P])
        gain = sb("gain", [P, KT])
        mu = sb("mu", [P, SHIFTED])
        par = sb("par", [P, 7, PAIRS])
        W0, A0, KKW, KA, RK, PSC, ONE_KA = range(7)
        ss = sb("ss", [P, TT])
        rstd = sb("rstd", [P, TT])
        eps = sb("eps", [P, 1])
        sA = tmp[:, 0:2, :].rearrange("p a t -> p (a t)")[:, 0:HALO + TB]
        sB = tmp[:, 2:4, :].rearrange("p a t -> p (a t)")[:, 0:HALO + TB]

        ptr = ctx.enter_context(nc.psum_tensor("p1_ptr", [P, 2, TB], F32))
        ppr = [ctx.enter_context(nc.psum_tensor(f"p1_ppr{i}", [P, TB], F32)) for i in range(2)]
        pm = ctx.enter_context(nc.psum_tensor("p1_pm", [P, 4, TB], F32))

        s_par = sem("params_loaded")
        s_const = sem("constants_built")
        s_x = [sem(f"x_loaded{i}") for i in range(2)]
        s_xs = sem("x_scaled")
        s_ss = sem("sum_squares")
        s_sq = sem("rms_root")
        s_rs = sem("rms_recip")
        s_tr = sem("transposed")
        s_hh = sem("hT_hi_ready")
        s_ht = sem("hT_ready")
        s_w = [sem(f"w_loaded{i}") for i in range(2)]
        s_wh = sem("w_hi_ready")
        s_wl = sem("w_lo_ready")
        s_pr = sem("proj_done")
        s_prf = sem("proj_read")
        s_halo = sem("halo_moved")
        s_diff = sem("shift_diff")
        s_um = sem("shifted")
        s_lora = sem("lora_act")
        s_mm = sem("small_matmul")
        s_mmr = sem("small_matmul_read")
        s_kkr = sem("kk_raw")
        s_sqk = sem("kk_squared")
        s_nmax = sem("kk_norm_max")
        s_nrt = sem("kk_norm_root")
        s_nrc = sem("kk_norm_recip")
        s_kn = sem("kk_normed")
        s_km = sem("k_modified")
        s_cum = sem("decay_sums")
        s_exp = sem("exps_ready")
        s_bon = sem("bonus_terms")
        s_rt = sem("r_ready")
        s_kt = sem("k_ready")
        s_bo = sem("bonus_ready")
        s_at = sem("a_ready")
        s_bt = sem("b_ready")
        s_store = sem("stored")
        s_gst = sem("gate_stored")
        s_poolin = sem("pool_in")
        s_pout = sem("pool_out_ready")
        s_pstore = sem("pool_stored")
        s_dve = sem("dve_step")

        xv = a["x"][0].rearrange("(t p) d -> p t d", p=P)
        wv = a["w_in"][0].rearrange("(k p) n -> p k n", p=P)
        NPAR = 9 + 10
        STORES = 6
        DECAY = -math.exp(-0.5)
        MM = 7

        def iterations(eng, body):
            body(0)
            with eng.Fori(1, BLOCKS - 1) as i:
                body(i)
            body(BLOCKS - 1)
            body(BLOCKS)

        def stages(i):
            if not isinstance(i, int):
                return True, True, True
            return i < BLOCKS, i > 0, i + 1 < BLOCKS

        def column(f):
            return (f + 12 if f < R0 else f - R0 if f < POOL0 else f) * P

        credit(nc, sems)
        with nc.Block() as block:
            @block.sync
            def _(sp):
                def load_x(i):
                    for half in range(2):
                        t = half * (TT // 2)
                        sp.dma_start(xin[:, t:t + TT // 2, :], xv[:, bass.ds(i * TT + t, TT // 2), :]).then_inc(s_x[half], 16)

                def load_w(n, f):
                    if not isinstance(n, int) or n >= 2:
                        sp.wait_ge(s_wh, ONE + n - 1)
                        sp.wait_ge(s_wl, ONE + n - 1)
                    sp.dma_start(w_raw[f % 2][:, :, :], wv[:, :, column(f):column(f) + P]).then_inc(s_w[f % 2], 16)

                load_x(0)
                load_w(0, 0)
                load_w(1, 1)
                with nc.allow_non_contiguous_dma(reason="per-feature parameters, once"):
                    sp.dma_start(gain[:, :], a["pre_mix_norm"][0].rearrange("(t p) -> p t", p=P)).then_inc(s_par, 16)
                    for slot, start, tiles in ((LORA, 12 * P, 2), (R0, 0, 12)):
                        sp.dma_start(mu[:, slot:slot + tiles], a["mu_shift"][0, start:start + tiles * P].rearrange("(t p) -> p t", p=P)
                                     ).then_inc(s_par, 16)
                    for i, name in ((W0, "w0"), (A0, "a0"), (KKW, "k_k"), (KA, "k_a"), (PSC, "pool_scale")):
                        sp.dma_start(par[:, i, :], a[name][0].rearrange("(t p) -> p t", p=P)).then_inc(s_par, 16)
                    sp.dma_start(par[:, RK, :], a["r_k"][0].rearrange("h d -> (h d)").rearrange("(t p) -> p t", p=P)
                                 ).then_inc(s_par, 16)
                    for dst, key in ((ident[:, :], "ident"), (head_ones[:, :], "head_ones"), (reset[:, :], "reset"),
                                     (cinv[:, :, :], "cinv"), (head_sums[:, :, :], "head_sums")):
                        sp.dma_start(dst, const_view(a, key)).then_inc(s_par, 16)
                    sp.dma_start(head_spread[:, :, :], const_view(a, "head_spread")[0:2 * PAIRS]).then_inc(s_par, 16)
                    sp.dma_start(wlora[0:DECAY_LORA, :], a["w_decay_up"][0]).then_inc(s_par, 16)
                    sp.dma_start(wlora[DECAY_LORA:P, :], a["w_aaa_up"][0]).then_inc(s_par, 16)
                    sp.dma_start(wgate[:, :], a["w_gate_up"][0]).then_inc(s_par, 16)
                    sp.dma_start(wpool[:, :, :], a["w_pool"][0].rearrange("g c d -> c g d")).then_inc(s_par, 16)

                def body(i):
                    project, finish, more = stages(i)
                    if not project:
                        return
                    for f in range(2, FT):
                        load_w(i * FT + f, f)
                        if more and f == 3:
                            sp.wait_ge(s_tr, ONE + (i + 1) * KT)
                            load_x(i + 1)
                    if more:
                        load_w(i * FT + FT, 0)
                        load_w(i * FT + FT + 1, 1)

                iterations(nc.sync, body)
                sp.wait_ge(s_store, ONE + 16 * STORES * BLOCKS)
                sp.wait_ge(s_gst, ONE + 16 * BLOCKS)
                sp.wait_ge(s_pstore, ONE + 16 * BLOCKS)

            @block.gpsimd
            def _(gp):
                nc.gpsimd.memset(eps[:, :], NORM_EPS)
                nc.gpsimd.memset(proj[:, :, TB:TB + HALO], 0.0).then_inc(s_const, 1)
                gp.wait_ge(s_const, ONE + 1)

                def low_w(n, f):
                    gp.wait_ge(s_wh, ONE + n + 1)
                    nc.gpsimd.tensor_tensor(w_lo[f % 2][:, :, :], w_raw[f % 2][:, :, :], w_hi[f % 2][:, :, :].bitcast(F32),
                                            ALU.subtract).then_inc(s_wl, 1)

                def diff(b, f):
                    if f == 0:
                        gp.wait_ge(s_store, ONE + b * (16 * STORES))
                    gp.wait_ge(s_prf, ONE + b * FT + f + 1)
                    nc.gpsimd.tensor_tensor(um[:, f, :], proj[:, f, HALO - 1:HALO - 1 + TB],
                                            proj[:, f, HALO:HALO + TB], ALU.subtract).then_inc(s_diff, 1)

                low_w(0, 0)
                low_w(1, 1)

                def body(i):
                    project, finish, more = stages(i)
                    done = 4
                    if finish:
                        for f in range(done):
                            diff(i - 1, f)
                    for f in range(2, FT + 2):
                        if project and (f < FT or more):
                            low_w(i * FT + f, f % FT)
                        if finish:
                            for d in range(done, min(done + 3, SHIFTED)):
                                diff(i - 1, d)
                            done = min(done + 3, SHIFTED)

                iterations(nc.gpsimd, body)

            @block.scalar
            def _(act):
                act.wait_ge(s_const, ONE + 1)

                def norm_squares(i):
                    if not isinstance(i, int) or i > 0:
                        act.wait_ge(s_ht, ONE + i * KT)
                    for t in range(TT):
                        act.wait_ge(s_x[t // (TT // 2)], ONE + i * 16 + 16)
                        if t or not isinstance(i, int) or i > 0:
                            act.wait_ge(s_ss, ONE + i * TT + t)
                        nc.scalar.activation(ptr[:, :, :].rearrange("p a t -> p (a t)"), xin[:, t, :], ACT.Square,
                                             accum_out=ss[:, t:t + 1]).then_inc(s_ss, 1)

                def norm_root(i):
                    act.wait_ge(s_ss, ONE + i * TT + TT)
                    nc.scalar.activation(rstd[:, :], ss[:, :], ACT.Sqrt, scale=1.0 / D_MODEL, bias=eps[:, 0:1]).then_inc(s_sq, 1)

                def norm_scale(i):
                    act.wait_ge(s_rs, ONE + i + 1)
                    for t in range(TT):
                        nc.scalar.activation(xin[:, t, :], xin[:, t, :], ACT.Copy, scale=rstd[:, t:t + 1]).then_inc(s_xs, 1)

                def high_w(n, f, blocks):
                    act.wait_ge(s_w[f % 2], ONE + blocks * (FT // 2 * 16) + (f // 2 + 1) * 16)
                    nc.scalar.activation(w_hi[f % 2][:, :, :], w_raw[f % 2][:, :, :], ACT.Copy).then_inc(s_wh, 1)

                def read_proj(i, f):
                    n = i * FT + f
                    act.wait_ge(s_pr, ONE + n + 1)
                    if not isinstance(i, int) or i > 0:
                        if f < SHIFTED:
                            act.wait_ge(s_um, ONE + (i - 1) * SHIFTED + f + 1)
                        else:
                            act.wait_ge(s_poolin, ONE + (i - 1) * PAIRS + f - POOL0 + 1)
                    nc.scalar.activation(proj[:, f, 0:HALO], proj[:, f, TB:TB + HALO], ACT.Copy).then_inc(s_halo, 1)
                    act.wait_ge(s_halo, ONE + n + 1)
                    nc.scalar.activation(proj[:, f, HALO:HALO + TB], ppr[f % 2][:, :], ACT.Copy).then_inc(s_prf, 1)

                def store(dst, src, b, done):
                    act.dma_start(scr[dst][:, :, bass.ds(b * TB, TB)], src).then_inc(done, 16)

                def loras(b):
                    act.wait_ge(s_um, ONE + b * SHIFTED + 1)
                    nc.scalar.activation(um[0:DECAY_LORA, LORA, :], um[0:DECAY_LORA, LORA, :], ACT.Tanh).then_inc(s_lora, 1)
                    act.wait_ge(s_um, ONE + b * SHIFTED + 2)
                    nc.scalar.activation(um[:, GATE, :], um[:, GATE, :], ACT.Sigmoid).then_inc(s_lora, 1)

                def decays(b):
                    act.wait_ge(s_mm, ONE + b * MM + 1)
                    act.wait_ge(s_store, ONE + b * (16 * STORES))
                    for j in range(PAIRS):
                        last = nc.scalar.activation(dec[:, j, :], pm[:, j, :], ACT.Sigmoid, bias=par[:, W0, j:j + 1])
                    last.then_inc(s_mmr, 1)

                def alphas(b):
                    act.wait_ge(s_mm, ONE + b * MM + 2)
                    for j in range(PAIRS):
                        last = nc.scalar.activation(alpha[:, j, :], pm[:, j, :], ACT.Sigmoid, bias=par[:, A0, j:j + 1])
                    last.then_inc(s_mmr, 1)

                def gates(b):
                    act.wait_ge(s_mm, ONE + b * MM + 3)
                    act.wait_ge(s_pstore, ONE + b * 16)
                    nc.scalar.activation(gate[:, :, :], pm[:, :, :], ACT.Copy).then_inc(s_mmr, 1)
                    act.wait_ge(s_mmr, ONE + b * 3 + 3)
                    store("g", gate[:, :, :], b, s_gst)
                    act.wait_ge(s_um, ONE + (b + 1) * SHIFTED)
                    store("v", um[:, V0:V0 + PAIRS, :], b, s_store)

                def pool_out(b):
                    act.wait_ge(s_mm, ONE + b * MM + 4)
                    act.wait_ge(s_gst, ONE + b * 16 + 16)
                    for g in range(PAIRS):
                        last = nc.scalar.activation(gate[:, g, :], pm[:, g, :], ACT.Copy, scale=par[:, PSC, g:g + 1])
                    last.then_inc(s_pout, 1)
                    act.wait_ge(s_pout, ONE + b + 1)
                    act.dma_start(scr["mix"][:, PAIRS:2 * PAIRS, bass.ds(b * TB, TB)], gate[:, :, :]).then_inc(s_pstore, 16)

                def kk_squares(b):
                    for j in range(PAIRS):
                        last = nc.scalar.activation(kk[:, j, :], um[:, K0 + j, :], ACT.Copy, scale=par[:, KKW, j:j + 1])
                    last.then_inc(s_kkr, 1)
                    act.wait_ge(s_kkr, ONE + b + 1)
                    nc.scalar.activation(tmp[:, :, :], kk[:, :, :], ACT.Square).then_inc(s_sqk, 1)

                def exps(b):
                    act.wait_ge(s_cum, ONE + b + 1)
                    act.wait_ge(s_km, ONE + b + 1)
                    nc.scalar.activation(einv[:, :, :], cum[:, :, :], ACT.Exp, scale=-DECAY).then_inc(s_exp, 1)
                    nc.scalar.activation(dec[:, :, :], dec[:, :, :], ACT.Exp, scale=DECAY).then_inc(s_exp, 1)
                    act.wait_ge(s_exp, ONE + b * 3 + 1)
                    nc.scalar.activation(cum[:, :, :], cum[:, :, :], ACT.Exp, scale=DECAY).then_inc(s_exp, 1)

                def kk_root(b):
                    act.wait_ge(s_nmax, ONE + b + 1)
                    nc.scalar.activation(norm[:, :], norm[:, :], ACT.Sqrt).then_inc(s_nrt, 1)

                norm_squares(0)
                norm_root(0)
                norm_scale(0)
                high_w(0, 0, 0)
                high_w(1, 1, 0)
                act.wait_ge(s_par, ONE + 16 * NPAR)

                def body(i):
                    project, finish, more = stages(i)
                    b = i - 1
                    if project:
                        if not isinstance(i, int) or i > 0:
                            act.wait_ge(s_pr, ONE + i * FT)
                        for k in range(KT):
                            act.wait_ge(s_tr, ONE + i * KT + k + 1)
                            nc.scalar.activation(hT_hi[:, k, :], ptr[:, k % 2, :], ACT.Copy, scale=gain[:, k:k + 1]).then_inc(s_hh, 1)
                    if finish:
                        loras(b)
                    for pair in range(FT // 2):
                        for f in (2 * pair, 2 * pair + 1):
                            if project:
                                read_proj(i, f)
                                if f + 2 < FT:
                                    high_w(i * FT + f + 2, f + 2, i)
                                elif more:
                                    high_w(i * FT + f + 2, f + 2 - FT, i + 1)
                        if finish and pair == 0:
                            decays(b)
                        if finish and pair == 1:
                            alphas(b)
                        if finish and pair == 2:
                            gates(b)
                        if finish and pair == 4:
                            pool_out(b)
                            kk_squares(b)
                        if finish and pair == 5:
                            exps(b)
                        if more and pair == 5:
                            norm_squares(i + 1)
                        if finish and pair == 6:
                            kk_root(b)
                        if more and pair == 6:
                            norm_root(i + 1)
                        if more and pair == 7:
                            norm_scale(i + 1)
                        if finish and pair == 7:
                            act.wait_ge(s_rt, ONE + b + 1)
                            store("rt", um[:, R0:R0 + PAIRS, :], b, s_store)
                            act.wait_ge(s_kt, ONE + b + 1)
                            store("kt", um[:, K0:K0 + PAIRS, :], b, s_store)
                            act.wait_ge(s_bo, ONE + b + 1)
                            store("bonus", tmp[:, :, :], b, s_store)
                    if finish:
                        act.wait_ge(s_at, ONE + b + 1)
                        store("at", dec[:, :, :], b, s_store)
                        act.wait_ge(s_bt, ONE + b + 1)
                        store("bt", alpha[:, :, :], b, s_store)

                iterations(nc.scalar, body)

            @block.vector
            def _(dve):
                K = 31

                def norm_reciprocal(i):
                    dve.wait_ge(s_sq, ONE + i + 1)
                    nc.vector.reciprocal(rstd[:, :], rstd[:, :]).then_inc(s_rs, 1)

                norm_reciprocal(0)
                dve.wait_ge(s_par, ONE + 16 * NPAR)
                nc.vector.tensor_scalar(par[:, ONE_KA, :], par[:, KA, :], -1.0, 1.0, ALU.mult, ALU.add).then_inc(s_dve, 1)
                dve.wait_ge(s_dve, ONE + 1)

                def low_hT(i):
                    for k in range(KT):
                        dve.wait_ge(s_hh, ONE + i * KT + k + 1)
                        nc.vector.scalar_tensor_tensor(hT_lo[:, k, :], ptr[:, k % 2, :], gain[:, k:k + 1],
                                                       hT_hi[:, k, :].bitcast(F32), ALU.mult, ALU.subtract).then_inc(s_ht, 1)

                def pool(b, st):
                    dve.wait_ge(s_store, ONE + b * (16 * STORES))
                    dve.wait_ge(s_at, ONE + b)
                    for g in range(PAIRS):
                        dve.wait_ge(s_prf, ONE + b * FT + POOL0 + g + 1)
                        dve.wait_ge(s_poolin, ONE + b * PAIRS + g)
                        u = proj[:, POOL0 + g, :]
                        src, dst, other = u, sA, sB
                        for l in range(g + 1):
                            w = 1 << l
                            lo = 2 * w - 1
                            st.link(nc.vector.tensor_tensor(dst[:, lo:HALO + TB], src[:, lo:HALO + TB],
                                                            src[:, lo - w:HALO + TB - w], ALU.add))
                            src, dst, other = dst, other, dst
                        s = src[:, HALO:HALO + TB]
                        st.do(nc.vector.scalar_tensor_tensor(kk[:, g, HALO:TB], s[:, HALO:TB], 1.0 / 2 ** (g + 1),
                                                             u[:, 2 * HALO:HALO + TB], ALU.mult, ALU.subtract))
                        st.link(nc.vector.tensor_tensor(s[:, 0:HALO], s[:, 0:HALO], cinv[:, g, :], ALU.mult))
                        nc.vector.tensor_tensor(kk[:, g, 0:HALO], s[:, 0:HALO], u[:, HALO:2 * HALO],
                                                ALU.subtract).then_inc(s_poolin, 1)
                    dve.wait_ge(s_poolin, ONE + (b + 1) * PAIRS)
                    for g in range(PAIRS):
                        st.do(nc.vector.memset(cinv[:, g, :], 1.0 / 2 ** (g + 1)))
                    st.wait()

                def body(i):
                    project, finish, more = stages(i)
                    b = i - 1
                    st = Steps(dve, s_dve, b * K + 1)
                    if project:
                        low_hT(i)
                    if finish:
                        for f in range(SHIFTED):
                            dve.wait_ge(s_diff, ONE + b * SHIFTED + f + 1)
                            nc.vector.scalar_tensor_tensor(um[:, f, :], um[:, f, :], mu[:, f:f + 1],
                                                           proj[:, f, HALO:HALO + TB], ALU.mult, ALU.add).then_inc(s_um, 1)
                            if f == 3:
                                pool(b, st)
                        dve.wait_ge(s_mmr, ONE + b * 3 + 1)
                        for j in range(PAIRS):
                            st.do(nc.vector.tensor_tensor_scan(cum[:, j, :], reset[:, :], dec[:, j, :], 0.0, ALU.mult, ALU.add))
                        st.wait()
                        nc.vector.tensor_tensor(dec[:, :, :], cum[:, :, :], dec[:, :, :], ALU.subtract).then_inc(s_cum, 1)
                        dve.wait_ge(s_mmr, ONE + b * 3 + 2)
                        for j in range(PAIRS):
                            st.do(nc.vector.tensor_scalar(einv[:, j, :], alpha[:, j, :], par[:, KA, j:j + 1],
                                                          par[:, ONE_KA, j:j + 1], ALU.mult, ALU.add))
                        st.wait()
                        dve.wait_ge(s_um, ONE + (b + 1) * SHIFTED)
                        dve.wait_ge(s_kkr, ONE + b + 1)
                        nc.vector.tensor_tensor(um[:, K0:K0 + PAIRS, :], um[:, K0:K0 + PAIRS, :], einv[:, :, :], ALU.mult).then_inc(s_km, 1)
                        dve.wait_ge(s_km, ONE + b + 1)
                        dve.wait_ge(s_mm, ONE + b * MM + 5)
                        nc.vector.tensor_scalar(norm[:, :], pm[0:2 * PAIRS, 0, :], 1e-24, None, ALU.max).then_inc(s_nmax, 1)
                        for j in range(PAIRS):
                            last = nc.vector.scalar_tensor_tensor(tmp[:, j, :], um[:, R0 + j, :], par[:, RK, j:j + 1],
                                                                  um[:, K0 + j, :], ALU.mult, ALU.mult)
                        last.then_inc(s_bon, 1)
                        dve.wait_ge(s_exp, ONE + b * 3 + 3)
                        dve.wait_ge(s_bon, ONE + b + 1)
                        nc.vector.tensor_tensor(um[:, R0:R0 + PAIRS, :], um[:, R0:R0 + PAIRS, :], cum[:, :, :], ALU.mult).then_inc(s_rt, 1)
                        nc.vector.tensor_tensor(um[:, K0:K0 + PAIRS, :], um[:, K0:K0 + PAIRS, :], einv[:, :, :], ALU.mult).then_inc(s_kt, 1)
                        nc.vector.tensor_copy(scr["pend"][:, :, bass.ds(b * (TB // C), TB // C)],
                                              cum[:, :, :].rearrange("p j (c t) -> p j c t", t=C)[:, :, :, C - 1])
                        dve.wait_ge(s_nrt, ONE + b + 1)
                        nc.vector.reciprocal(norm[:, :], norm[:, :]).then_inc(s_nrc, 1)
                    if more:
                        norm_reciprocal(i + 1)
                    if finish:
                        dve.wait_ge(s_mm, ONE + b * MM + 6)
                        nc.vector.tensor_tensor(tmp[:, :, :], pm[:, :, :], um[:, V0:V0 + PAIRS, :], ALU.mult).then_inc(s_bo, 1)
                        dve.wait_ge(s_mm, ONE + b * MM + 7)
                        nc.vector.tensor_tensor(kk[:, :, :], kk[:, :, :], pm[:, :, :], ALU.mult).then_inc(s_kn, 1)
                        dve.wait_ge(s_kn, ONE + b + 1)
                        st.link(nc.vector.tensor_tensor(alpha[:, :, :], alpha[:, :, :], kk[:, :, :], ALU.mult))
                        nc.vector.tensor_tensor(alpha[:, :, :], alpha[:, :, :], einv[:, :, :], ALU.mult).then_inc(s_bt, 1)
                        nc.vector.scalar_tensor_tensor(dec[:, :, :].rearrange("p j t -> p (j t)"),
                                                       kk[:, :, :].rearrange("p j t -> p (j t)"), -1.0,
                                                       dec[:, :, :].rearrange("p j t -> p (j t)"),
                                                       ALU.mult, ALU.mult).then_inc(s_at, 1)
                        assert st.n == K, st.n

                iterations(nc.vector, body)

            @block.tensor
            def _(pe):
                pe.wait_ge(s_const, ONE + 1)
                pe.wait_ge(s_par, ONE + 16 * NPAR)

                def products(lhs, rhs):
                    for j in range(PAIRS):
                        last = nc.tensor.matmul(pm[:, j, :], lhs(j), rhs(j), start=True, stop=True)
                    last.then_inc(s_mm, 1)

                def small(b, pair):
                    if pair == 0:
                        pe.wait_ge(s_lora, ONE + b * 2 + 1)
                        pe.wait_ge(s_kn, ONE + b)
                        products(lambda j: wlora[0:64, j * P:(j + 1) * P], lambda j: um[0:64, LORA, :])
                    if pair == 1:
                        pe.wait_ge(s_um, ONE + b * SHIFTED + 1)
                        pe.wait_ge(s_mmr, ONE + b * 3 + 1)
                        products(lambda j: wlora[64:128, j * P:(j + 1) * P], lambda j: um[64:128, LORA, :])
                    if pair == 2:
                        pe.wait_ge(s_lora, ONE + b * 2 + 2)
                        pe.wait_ge(s_mmr, ONE + b * 3 + 2)
                        products(lambda j: wgate[:, j * P:(j + 1) * P], lambda j: um[:, GATE, :])
                    if pair == 3:
                        pe.wait_ge(s_poolin, ONE + b * PAIRS + PAIRS)
                        pe.wait_ge(s_mmr, ONE + b * 3 + 3)
                        products(lambda g: wpool[:, g, :], lambda g: kk[:, g, :])
                    if pair == 5:
                        pe.wait_ge(s_sqk, ONE + b + 1)
                        pe.wait_ge(s_pout, ONE + b + 1)
                        for j in range(PAIRS):
                            last = nc.tensor.matmul(pm[0:2 * PAIRS, 0, :], head_sums[:, j, :], tmp[:, j, :], start=j == 0, stop=j == PAIRS - 1)
                        last.then_inc(s_mm, 1)
                    if pair == 6:
                        pe.wait_ge(s_bon, ONE + b + 1)
                        pe.wait_ge(s_nmax, ONE + b + 1)
                        products(lambda j: head_ones[:, :], lambda j: tmp[:, j, :])
                    if pair == 7:
                        pe.wait_ge(s_nrc, ONE + b + 1)
                        pe.wait_ge(s_bo, ONE + b + 1)
                        products(lambda j: head_spread[:, j, :], lambda j: norm[:, :])

                def body(i):
                    project, finish, more = stages(i)
                    if project:
                        pe.wait_ge(s_xs, ONE + i * TT + TT)
                        for k in range(KT):
                            if k >= 2 or not isinstance(i, int) or i > 0:
                                pe.wait_ge(s_ht, ONE + i * KT + (k - 1 if k >= 2 else 0))
                            for t in range(TT):
                                last = nc.tensor.transpose(ptr[:, k % 2, t * P:(t + 1) * P], xin[:, t, k * P:(k + 1) * P], ident[:, :])
                            last.then_inc(s_tr, 1)
                    for pair in range(FT // 2):
                        for f in (2 * pair, 2 * pair + 1):
                            if not project:
                                continue
                            n = i * FT + f
                            pe.wait_ge(s_wh, ONE + n + 1)
                            pe.wait_ge(s_wl, ONE + n + 1)
                            if not isinstance(n, int) or n >= 2:
                                pe.wait_ge(s_prf, ONE + n - 1)
                            for k in range(KT):
                                if f == 0:
                                    pe.wait_ge(s_ht, ONE + i * KT + k + 1)
                                last = split_matmul(nc, ppr[f % 2][:, :], w_hi[f % 2][:, k, :], w_lo[f % 2][:, k, :],
                                                    hT_hi[:, k, :], hT_lo[:, k, :], k == 0, k == KT - 1)
                            last.then_inc(s_pr, 1)
                        if finish:
                            small(i - 1, pair)

                iterations(nc.tensor, body)


def phase_recur(nc, a, scr):
    ctx, sems = ExitStack(), []
    with ctx:
        def sb(name, shape, dt=F32):
            return ctx.enter_context(nc.sbuf_tensor("p2_" + name, shape, dt))

        def sem(name):
            sems.append(ctx.enter_context(nc.semaphore("p2_" + name)))
            return sems[-1]

        H = HEAD_DIM
        LEVELS = 5
        N = SEQ // SC

        def two(name, shape):
            return [sb(f"{name}{i}", shape) for i in range(2)]

        ar = two("ar", [P, 2, PAIRS, SC])
        bt = sb("bt", [P, PAIRS, SC])
        kt = sb("kt", [P, PAIRS, SC])
        vt = sb("vt", [P, PAIRS, SC])
        bonus = sb("bonus", [P, PAIRS, SC])
        gate = sb("gate", [P, PAIRS, SC])
        bk = two("bk", [P, PAIRS, CH, P])
        ab = two("ab", [P, PAIRS, CH // 2, P])
        vb = two("vb", [P, PAIRS, CH // 2, P])
        wr = two("wr", [P, PAIRS, CH, P])
        aab = two("aab", [P, DBL, P])
        aak = two("aak", [P, DBL, P])
        ark = two("ark", [P, UNITS, 2 * C])
        bkt = two("bkt", [P, UNITS, P])
        uv = two("uv", [P, PAIRS, CH, H])
        z = two("zz", [P, PAIRS, CH // 2, H])
        x = sb("x", [P, DBL, C])
        xm = sb("xm", [P, DBL, C])
        at = sb("at", [P, DBL, C])
        xt = sb("xt", [P, DBL, P])
        t1 = sb("t1", [P, DBL, C])
        atm = sb("atm", [P, DBL, P])
        vd = sb("vd", [P, DBL, H])
        z0 = sb("z0", [P, DBL, H])
        state = sb("state", [P, PAIRS, H])
        sumst = sb("sumst", [P, PAIRS, H])
        pq = sb("pq", [P, PAIRS, CH])
        y = sb("y", [P, PAIRS, CH // 2, H])
        y2 = sb("y2", [P, DBL, H])
        yb = sb("yb", [P, DBL, 2, H])
        stat = sb("stat", [P, 4, DBL])
        mo = sb("mo", [P, PAIRS, SC])
        geps = sb("geps", [P, 1])
        zeros = sb("zeros", [P, P + 512], mybir.dt.bfloat16)
        ident = sb("ident", [P, P])
        ident2 = sb("ident2", [P, H])
        ident4 = sb("ident4", [P, C])
        strict = sb("strict", [P, C])
        causal = sb("causal", [P, C])
        levels = sb("levels", [P, LEVELS, C])
        rows = sb("rows", [P, 2 * C])
        hrow = sb("hrow", [P, 2])
        lnw = sb("lnw", [P, PAIRS])
        lnb = sb("lnb", [P, PAIRS])
        bank = ctx.enter_context(nc.psum_tensor("p2_bank", [P, 8, 512], F32))
        YB, SB, XB, GB, ROT = 0, 2, 3, 4, (6, 7)
        ybank = bank[:, YB:YB + 2, :].rearrange("p b (u v) -> p (b u) v", v=H)
        tcol = bank[:, XB, 0:DBL * C].rearrange("p (d s) -> p d s", s=C)
        xcol = bank[:, XB, DBL * C:2 * DBL * C].rearrange("p (d s) -> p d s", s=C)

        s_par = sem("params_loaded")
        s_const = sem("zeros_written")
        s_zb = sem("blocks_zeroed")
        s_in = sem("inputs_loaded")
        s_in2 = sem("bonus_gate_loaded")
        s_bk = sem("bk_built")
        s_rb = sem("r_built")
        s_av = sem("a_v_built")
        s_gram = sem("gram_done")
        s_aab = sem("aab_masked")
        s_gr = sem("gram_read")
        s_t1 = sem("t1_done")
        s_t1r = sem("t1_read")
        s_at = sem("aab_turned")
        s_x2 = sem("x_product")
        s_xm = sem("x_product_masked")
        s_xc = sem("x_updated")
        s_xt = sem("x_transposed")
        s_full = [sem(f"turn_bank{b}_full") for b in ROT]
        s_read = [sem(f"turn_bank{b}_read") for b in ROT]
        s_p1 = sem("state_products")
        s_u = sem("u_ready")
        s_s = sem("state_update")
        s_sum = sem("state_summed")
        s_sn = sem("state_ready")
        s_pq = sem("chunk_decay_ready")
        s_y = sem("y_done")
        s_yr = sem("y_read")
        s_gn = sem("norm_step")
        s_yc = sem("y_centred")
        s_yc2 = sem("y_normed")
        s_sq = sem("y_squared")
        s_var = sem("y_var")
        s_sd = sem("y_deviation")
        s_yb = sem("y_blocks")
        s_add = sem("bonus_added")
        s_mo = sem("mix_ready")
        s_mix = sem("mix_stored")
        s_go = sem("gpsimd_started")

        JOBS = ["v", "a0", "a1", "bk0", "bk1", "bk2", "bk3", "y", "z0", "w0", "w1", "z"]
        TURN = {name: (i % 2, i // 2) for i, name in enumerate(JOBS)}
        PER = len(JOBS) // 2

        def vrows(e):
            return slice(0, 64) if e else slice(64, 128)

        def urows(e):
            return slice(64, 128) if e else slice(0, 64)

        def by_parity(v, e):
            return v.rearrange("p j (c e) n -> p j c e n", e=2)[:, :, :, e, :]

        def iterations(eng, body):
            body(-2, 0)
            body(-1, 1)
            body(0, 0)
            with eng.Fori(0, (N - 4) // 2) as h:
                body(h * 2 + 1, 1)
                body(h * 2 + 2, 0)
            for i in range(N - 3, N + 1):
                body(i, i % 2)

        def stages(i):
            if not isinstance(i, int):
                return True, True, True, True
            return i + 2 < N, 0 <= i + 1 < N, 0 <= i < N, 0 <= i - 1 < N

        def turns(i):
            if not isinstance(i, int):
                base = [(i + 1) * PER, (i + 1) * PER]
                base[TURN["y"][0]] = (i + 1) * (PER - 1) + (i - 1)
                return base
            out = [0, 0]
            for k in range(-2, i):
                _, a2, _, c = stages(k)
                for name in JOBS:
                    if c if name == "y" else a2:
                        out[TURN[name][0]] += 1
            return out

        def job(i, name):
            _, a2, _, c = stages(i)
            t, before = TURN[name][0], 0
            for other in JOBS[:JOBS.index(name)]:
                if TURN[other][0] == t and (c if other == "y" else a2):
                    before += 1
            return t, turns(i)[t] + before

        credit(nc, sems)
        with nc.Block() as block:
            @block.sync
            def _(sp):
                def body(i, p):
                    a1, a2, b, c = stages(i)
                    if a1:
                        n = i + 2
                        tok = bass.ds(n * SC, SC)
                        sp.wait_ge(s_bk, ONE + n * 8)
                        sp.wait_ge(s_av, ONE + n * 8)
                        if b:
                            sp.wait_ge(s_rb, ONE + (i + 1) * 4)
                            sp.wait_ge(s_gram, ONE + i + 1)
                        for dst, key in ((bt[:, :, :], "bt"), (kt[:, :, :], "kt"), (ar[p][:, 0, :, :], "at"),
                                         (ar[p][:, 1, :, :], "rt"), (vt[:, :, :], "v")):
                            sp.dma_start(dst, scr[key][:, :, tok]).then_inc(s_in, 16)
                    if isinstance(i, int) and i == -2:
                        with nc.allow_non_contiguous_dma(reason="per-feature parameters, once"):
                            for dst, name in ((lnw, "ln_x_w"), (lnb, "ln_x_b")):
                                sp.dma_start(dst[:, :], a[name][0].rearrange("(t p) -> p t", p=P)).then_inc(s_par, 16)
                            for dst, key in ((ident[:, :], "ident"), (ident2[:, :], "ident2"), (ident4[:, :], "ident4"),
                                             (strict[:, :], "strict"), (causal[:, :], "causal"), (levels[:, :, :], "levels"),
                                             (rows[:, :], "rows_to_tokens"), (hrow[:, :], "head_rows")):
                                sp.dma_start(dst, const_view(a, key)).then_inc(s_par, 16)
                    if c:
                        n = i - 1
                        tok = bass.ds(n * SC, SC)
                        sp.wait_ge(s_mo, ONE + n)
                        for dst, key in ((bonus[:, :, :], "bonus"), (gate[:, :, :], "g")):
                            sp.dma_start(dst, scr[key][:, :, tok]).then_inc(s_in2, 16)
                        sp.wait_ge(s_mo, ONE + i)
                        sp.dma_start(scr["mix"][:, 0:PAIRS, tok], mo[:, :, :]).then_inc(s_mix, 16)

                iterations(nc.sync, body)
                sp.wait_ge(s_mix, ONE + 16 * N)

            @block.gpsimd
            def _(gp):
                for i in range(2):
                    nc.gpsimd.memset(bk[i][:], 0.0)
                nc.gpsimd.memset(zeros[:, :], 0.0)
                nc.gpsimd.memset(geps[:, :], GN_EPS)
                nc.gpsimd.memset(state[:, :, :], 0.0).then_inc(s_const, 1)
                gp.wait_ge(s_const, ONE + 1)

                def body(i, p):
                    a1, a2, b, c = stages(i)
                    if c:
                        gp.wait_ge(s_yc, ONE + i)
                        yv = y[:].rearrange("p j c v -> p (j c) v")
                        nc.gpsimd.tensor_tensor(y2[:, :, :], yv, yv, ALU.mult).then_inc(s_sq, 1)
                    if a1:
                        n = i + 2
                        gp.wait_ge(s_in, ONE + n * 80 + 80)
                        if b:
                            t, k = job(i - 1, "bk3")
                            gp.wait_ge(s_full[t], ONE + k + 1)
                        if c:
                            gp.wait_ge(s_sq, ONE + i)
                        gp.sem_inc(s_go, 1)
                        for e in range(2):
                            for kind, src in ((e, bt), (1 - e, kt)):
                                for h in range(2):
                                    off = 64 * kind + 32 * h
                                    nc.gpsimd.tensor_copy(
                                        by_parity(bk[p][64 * h:64 * h + 64, :, :, off:off + C], e),
                                        by_parity(src[64 * h:64 * h + 64, :, :].rearrange("p j (c t) -> p j c t", t=C), e)
                                    ).then_inc(s_bk, 1)
                    if c:
                        if a1:
                            gp.wait_ge(s_bk, ONE + i * 8 + 24)
                        gp.wait_ge(s_in2, ONE + i * 32)
                        t, k = job(i, "y")
                        gp.wait_ge(s_read[t], ONE + k + 1)
                        nc.gpsimd.tensor_tensor(mo[:, :, :], mo[:, :, :], bonus[:, :, :], ALU.add).then_inc(s_add, 1)
                        gp.wait_ge(s_add, ONE + i)
                        nc.gpsimd.tensor_tensor(mo[:, :, :], mo[:, :, :], gate[:, :, :], ALU.mult).then_inc(s_mo, 1)

                iterations(nc.gpsimd, body)

            @block.scalar
            def _(act):
                act.wait_ge(s_const, ONE + 1)
                act.wait_ge(s_zb, ONE + 1)
                act.wait_ge(s_par, ONE + 160)

                def body(i, p):
                    a1, a2, b, c = stages(i)
                    q = 1 - p

                    def read(name, *copies):
                        t, k = job(i, name)
                        act.wait_ge(s_full[t], ONE + k + 1)
                        for out_ap, in_ap in copies:
                            last = nc.scalar.activation(out_ap, in_ap(bank[:, ROT[t], :]), ACT.Copy)
                        last.then_inc(s_read[t], 1)

                    def read_t1(l):
                        act.wait_ge(s_t1, ONE + (i + 1) * 4 + l)
                        nc.scalar.activation(t1[:, :, :], tcol, ACT.Copy).then_inc(s_t1r, 1)

                    def half(n):
                        return lambda v: v.rearrange("p (u k) -> p u k", k=n)

                    def units(lo):
                        return slice(4 * lo, 4 * lo + 4)

                    if a2:
                        read("v", (vd[:, :, :], half(H)),
                             *((by_parity(uv[q][vrows(e)], e), lambda v, e=e: v[vrows(e), :].rearrange("p (j c v) -> p j c v", j=PAIRS, v=H))
                               for e in range(2)))
                        read_t1(1)
                        for n in range(2):
                            read(f"a{n}", (atm[:, units(n), :], half(P)))
                        read_t1(2)
                        for n in range(2):
                            read(f"bk{n}", (bkt[q][:, units(n), :], half(P)))
                        read_t1(3)
                    if c:
                        act.wait_ge(s_var, ONE + i)
                        nc.scalar.activation(stat[:, 2, :], stat[:, 1, :], ACT.Sqrt, scale=1.0 / H, bias=geps[:, 0:1]).then_inc(s_sd, 1)
                    if a2:
                        for n in range(2, 4):
                            read(f"bk{n}", (bkt[q][:, units(n), :], half(P)))
                        read_t1(4)
                    if a1:
                        n = i + 2
                        act.wait_ge(s_in, ONE + n * 80 + 80)
                        for e in range(2):
                            for h in range(2):
                                off = 64 * e + 32 * h
                                nc.scalar.activation(
                                    ab[p][64 * h:64 * h + 64, :, :, off:off + C],
                                    by_parity(ar[p][64 * h:64 * h + 64, 0, :, :].rearrange("p j (c t) -> p j c t", t=C), e),
                                    ACT.Copy).then_inc(s_av, 1)
                        for e in range(2):
                            for h in range(2):
                                off = 64 * (1 - e) + 32 * h
                                nc.scalar.activation(
                                    vb[p][64 * h:64 * h + 64, :, :, off:off + C],
                                    by_parity(vt[64 * h:64 * h + 64, :, :].rearrange("p j (c t) -> p j c t", t=C), e),
                                    ACT.Copy).then_inc(s_av, 1)
                    if b:
                        act.wait_ge(s_y, ONE + i * CH + CH)
                        if c:
                            act.wait_ge(s_yb, ONE + i)
                        for e in range(2):
                            last = nc.scalar.activation(
                                y[vrows(e), :, :, :], by_parity(ybank[vrows(e)].rearrange("p (j c) v -> p j c v", c=CH), e), ACT.Copy)
                        last.then_inc(s_yr, 1)
                    if c:
                        t, k = job(i, "y")
                        act.wait_ge(s_full[t], ONE + k + 1)
                        act.wait_ge(s_mix, ONE + (i - 1) * 16)
                        for j in range(PAIRS):
                            last = nc.scalar.activation(mo[:, j, :], bank[:, ROT[t], j * SC:(j + 1) * SC], ACT.Identity,
                                                        scale=lnw[:, j:j + 1], bias=lnb[:, j:j + 1])
                        last.then_inc(s_read[t], 1)
                    if a2:
                        read("z0", (z0[:, :, :], half(H)))
                        for n in range(2):
                            read(f"w{n}", *((by_parity(wr[q][:, 2 * n:2 * n + 2, :, 64 * e:64 * e + 64], e),
                                             lambda v, e=e: v.rearrange("p (j c n) -> p j c n", j=2, n=P)[:, :, :, 64 * e:64 * e + 64])
                                            for e in range(2)))
                        read("z", (z[q][:, :, :, :], lambda v: v.rearrange("p (j c v) -> p j c v", j=PAIRS, v=H)))

                iterations(nc.scalar, body)

            @block.vector
            def _(dve):
                for m in (ab, vb):
                    for i in range(2):
                        last = nc.vector.memset(m[i][:], 0.0)
                last.then_inc(s_zb, 1)
                for m in (aab, aak, ark, wr):
                    for i in range(2):
                        nc.vector.memset(m[i][:], 0.0)
                nc.vector.memset(xt[:, :, :], 0.0).then_inc(s_zb, 1)
                dve.wait_ge(s_zb, ONE + 2)
                dve.wait_ge(s_par, ONE + 160)
                dve.wait_ge(s_const, ONE + 1)
                yv = y[:].rearrange("p j c v -> p (j c) v")

                def body(i, p):
                    a1, a2, b, c = stages(i)
                    q = 1 - p

                    def inverse(l):
                        m = levels[:, l, :].unsqueeze(1).to_broadcast([P, DBL, C])
                        n = (i + 1) * LEVELS + l + 1
                        if l == 0:
                            dve.wait_ge(s_aab, ONE + i + 2)
                            for k in range(4):
                                r = slice(32 * k, 32 * k + 32)
                                last = nc.vector.transpose(at[r, :, :], aab[q][r, :, 32 * k:32 * k + 32])
                            last.then_inc(s_at, 1)
                            dve.wait_ge(s_at, ONE + i + 2)
                            nc.vector.tensor_tensor(xm[:, :, :], at[:, :, :], m, ALU.mult).then_inc(s_xm, 1)
                        else:
                            dve.wait_ge(s_x2, ONE + (i + 1) * (LEVELS - 1) + l)
                            nc.vector.tensor_tensor(xm[:, :, :], xcol, m, ALU.mult).then_inc(s_xm, 1)
                        base = x[:, :, :] if l else ident4[:, :].unsqueeze(1).to_broadcast([P, DBL, C])
                        dve.wait_ge(s_xm, ONE + n)
                        nc.vector.tensor_tensor(x[:, :, :], xm[:, :, :], base, ALU.add).then_inc(s_xc, 1)
                        dve.wait_ge(s_xc, ONE + n)
                        if l == 0 and b:
                            t, k = job(i - 1, "z")
                            dve.wait_ge(s_full[t], ONE + k + 1)
                        for k in range(4):
                            r = slice(32 * k, 32 * k + 32)
                            last = nc.vector.transpose(xt[r, :, 32 * k:32 * k + 32], x[r, :, :])
                        last.then_inc(s_xt, 1)

                    def solve(c4):
                        e, n = c4 % 2, i * CH + c4 + 1
                        dve.wait_ge(s_p1, ONE + n)
                        nc.vector.tensor_tensor(uv[p][urows(e), :, c4, :],
                                                ybank.rearrange("p (j c) v -> p j c v", c=CH)[urows(e), :, c4, :],
                                                z[p][urows(e), :, c4 // 2, :], ALU.add).then_inc(s_u, 1)

                    def advance(c4):
                        n = i * CH + c4 + 1
                        dve.wait_ge(s_s, ONE + n)
                        nc.vector.tensor_tensor(sumst[:, :, :], bank[:, SB, 0:PAIRS * H].rearrange("p (j v) -> p j v", v=H),
                                                state[:, :, :], ALU.add).then_inc(s_sum, 1)
                        dve.wait_ge(s_sum, ONE + n)
                        nc.vector.tensor_tensor(state[:, :, :], sumst[:, :, :],
                                                pq[:, :, c4:c4 + 1].to_broadcast([P, PAIRS, H]), ALU.mult).then_inc(s_sn, 1)
                        dve.wait_ge(s_sn, ONE + n)

                    if b:
                        nc.vector.tensor_copy(pq[:, :, :], scr["pend"][:, :, bass.ds(i * CH, CH)]).then_inc(s_pq, 1)
                        dve.wait_ge(s_pq, ONE + i + 1)
                    if a2:
                        inverse(0)
                    if b:
                        t, k = job(i - 1, "z")
                        dve.wait_ge(s_read[t], ONE + k + 1)
                        solve(0)
                    if c:
                        g = (i - 1) * 3
                        dve.wait_ge(s_yr, ONE + i)
                        nc.vector.tensor_reduce(stat[:, 0, :], yv, AX.X, ALU.add).then_inc(s_gn, 1)
                        dve.wait_ge(s_gn, ONE + g + 1)
                        nc.vector.tensor_scalar(stat[:, 0, :], stat[:, 0, :], -1.0 / H, None, ALU.mult).then_inc(s_gn, 1)
                    if b:
                        advance(0)
                    if a2:
                        inverse(1)
                    if b:
                        solve(1)
                    if c:
                        dve.wait_ge(s_gn, ONE + g + 2)
                        nc.vector.tensor_tensor(yv, yv, stat[:, 0, :].unsqueeze(2).to_broadcast([P, DBL, H]), ALU.add).then_inc(s_yc, 1)
                    if b:
                        advance(1)
                    if a2:
                        inverse(2)
                    if b:
                        solve(2)
                    if c:
                        dve.wait_ge(s_sq, ONE + i)
                        nc.vector.tensor_reduce(stat[:, 1, :], y2[:, :, :], AX.X, ALU.add).then_inc(s_var, 1)
                    if b:
                        advance(2)
                    if a2:
                        inverse(3)
                    if b:
                        solve(3)
                    if c:
                        dve.wait_ge(s_sd, ONE + i)
                        nc.vector.reciprocal(stat[:, 3, :], stat[:, 2, :]).then_inc(s_gn, 1)
                    if b:
                        advance(3)
                    if c:
                        dve.wait_ge(s_gn, ONE + g + 3)
                        nc.vector.tensor_tensor(yv, yv, stat[:, 3, :].unsqueeze(2).to_broadcast([P, DBL, H]), ALU.mult).then_inc(s_yc2, 1)
                        dve.wait_ge(s_yc2, ONE + i)
                        for h in range(2):
                            last = nc.vector.tensor_scalar(yb[:, :, h, :], yv, hrow[:, h:h + 1], None, ALU.mult)
                        last.then_inc(s_yb, 1)
                    if a2:
                        for e in range(2):
                            for h in range(2):
                                off = 64 * (1 - e) + 32 * h
                                nc.vector.tensor_copy(
                                    by_parity(wr[q][64 * h:64 * h + 64, :, :, off:off + C], e),
                                    by_parity(ar[q][64 * h:64 * h + 64, 1, :, :].rearrange("p j (c t) -> p j c t", t=C), e)
                                ).then_inc(s_rb, 1)
                        inverse(4)
                    if a1:
                        dve.wait_ge(s_gram, ONE + i + 3)
                        g = bank[:, GB:GB + 2, :].rearrange("p b (j c n) -> p (b j) c n", j=2, n=2 * C)
                        for k in range(4):
                            e, r = k // 2, slice(32 * k, 32 * k + 32)
                            m = strict[r, :].unsqueeze(1).unsqueeze(1).to_broadcast([32, PAIRS, CH // 2, C])
                            last = nc.vector.tensor_tensor(aab[p][r, :, 32 * k:32 * k + 32].rearrange("p (j c) t -> p j c t", c=CH // 2),
                                                           by_parity(g[r, :, :, 0:C], e), m, ALU.mult)
                        last.then_inc(s_aab, 1)
                        for k in range(4):
                            e, r, col = 1 - k // 2, slice(32 * k, 32 * k + 32), 32 * ((k + 2) % 4)
                            m = strict[r, :].unsqueeze(1).unsqueeze(1).to_broadcast([32, PAIRS, CH // 2, C])
                            nc.vector.tensor_tensor(aak[p][r, :, col:col + 32].rearrange("p (j c) t -> p j c t", c=CH // 2),
                                                    by_parity(g[r, :, :, 0:C], e), m, ALU.mult)
                        g2 = bank[:, GB:GB + 2, :].rearrange("p b (u n) -> p (b u) n", n=2 * C)
                        if b:
                            dve.wait_ge(s_y, ONE + i * CH + CH)
                        for k in range(4):
                            r = slice(32 * k, 32 * k + 32)
                            m = causal[r, :].unsqueeze(1).to_broadcast([32, UNITS, C])
                            last = nc.vector.tensor_tensor(ark[p][r, :, 32 * (k % 2):32 * (k % 2) + 32], g2[r, :, C:2 * C], m, ALU.mult)
                        last.then_inc(s_gr, 1)

                iterations(nc.vector, body)

            @block.tensor
            def _(pe):
                pe.wait_ge(s_const, ONE + 1)
                pe.wait_ge(s_zb, ONE + 2)
                pe.wait_ge(s_par, ONE + 160)

                def body(i, p):
                    a1, a2, b, c = stages(i)
                    q = 1 - p

                    def turn(name, matmul, count):
                        t, k = job(i, name)
                        pe.wait_ge(s_read[t], ONE + k)
                        for n in range(count):
                            last = matmul(bank[:, ROT[t], :], n)
                        last.then_inc(s_full[t], 1)

                    def t1_product(l):
                        pe.wait_ge(s_xc, ONE + (i + 1) * LEVELS + l)
                        for d in range(DBL):
                            last = nc.tensor.matmul(tcol[:, d, :], aab[q][:, d, :], x[:, d, :], start=True, stop=True)
                        last.then_inc(s_t1, 1)

                    def x_product(l):
                        pe.wait_ge(s_t1r, ONE + (i + 1) * 4 + l)
                        pe.wait_ge(s_xt, ONE + (i + 1) * LEVELS + l)
                        for d in range(DBL):
                            last = nc.tensor.matmul(xcol[:, d, :], xt[:, d, :], t1[:, d, :], start=True, stop=True)
                        last.then_inc(s_x2, 1)

                    def from_state(c4):
                        pe.wait_ge(s_sn, ONE + i * CH + c4)
                        for j in range(PAIRS):
                            last = nc.tensor.matmul(ybank[:, j * CH + c4, :], wr[p][:, j, c4, :], state[:, j, :], start=False, stop=True,
                                                    skip_group_check=True)
                        last.then_inc(s_p1, 1)

                    def to_state(c4):
                        pe.wait_ge(s_u, ONE + i * CH + c4 + 1)
                        for j in range(PAIRS):
                            last = nc.tensor.matmul(bank[:, SB, j * H:(j + 1) * H], bkt[p][:, j * CH + c4, :], uv[p][:, j, c4, :],
                                                    start=True, stop=True)
                        last.then_inc(s_s, 1)
                        for j in range(PAIRS):
                            last = nc.tensor.matmul(ybank[vrows(c4 % 2), j * CH + c4, :], ark[p][:, j * CH + c4, :], uv[p][:, j, c4, :],
                                                    start=False, stop=True, skip_group_check=True)
                        last.then_inc(s_y, 1)

                    def a_transposes(n):
                        turn(f"a{n}", lambda o, d: nc.tensor.transpose(o[:, d * P:(d + 1) * P], ab[q][:, 2 * n + d // 2, d % 2, :], ident[:, :]), 4)

                    def bk_transposes(n):
                        turn(f"bk{n}", lambda o, u: nc.tensor.transpose(o[:, u * P:(u + 1) * P], bk[q][:, n, u, :], ident[:, :]), 4)

                    def grams(n):
                        if n == 0:
                            pe.wait_ge(s_bk, ONE + i * 8 + 24)
                            pe.wait_ge(s_gr, ONE + i + 2)
                        for j in range(2 * n, 2 * n + 2):
                            for u in range(CH):
                                k = (j - 2 * n) * CH + u
                                last = nc.tensor.matmul(bank[:, GB + n, k * 64:(k + 1) * 64], bk[p][:, j, u, :],
                                                        ar[p][:, :, j, u * C:(u + 1) * C], start=True, stop=True)
                        if n == 1:
                            last.then_inc(s_gram, 1)

                    if b:
                        pe.wait_ge(s_yr, ONE + i)
                        for n in range(2):
                            nc.tensor.matmul(bank[:, YB + n, :], zeros[:, 0:P], zeros[:, P:P + 512], start=True, stop=True)
                    if a2:
                        pe.wait_ge(s_av, ONE + i * 8 + 16)
                        turn("v", lambda o, d: nc.tensor.matmul(o[:, d * H:(d + 1) * H], vb[q][:, d // 2, d % 2, :], ident2[:, :],
                                                                start=True, stop=True), DBL)
                    if b:
                        pe.wait_ge(s_rb, ONE + i * 4 + 4)
                        t, k = job(i - 1, "w1")
                        pe.wait_ge(s_read[t], ONE + k + 1)
                        from_state(0)
                    if a2:
                        t1_product(1)
                        a_transposes(0)
                    if b:
                        to_state(0)
                    if a2:
                        x_product(1)
                        a_transposes(1)
                    if b:
                        from_state(1)
                    if a2:
                        t1_product(2)
                        bk_transposes(0)
                    if b:
                        to_state(1)
                    if a2:
                        x_product(2)
                        bk_transposes(1)
                    if b:
                        from_state(2)
                    if a2:
                        t1_product(3)
                        bk_transposes(2)
                    if b:
                        to_state(2)
                    if a2:
                        x_product(3)
                        bk_transposes(3)
                    if b:
                        from_state(3)
                    if a2:
                        t1_product(4)
                    if a1:
                        grams(0)
                    if b:
                        to_state(3)
                    if a2:
                        x_product(4)
                    if a1:
                        grams(1)
                    if c:
                        pe.wait_ge(s_yb, ONE + i)
                        turn("y", lambda o, d: nc.tensor.matmul(o[:, d * 2 * C:(d + 1) * 2 * C], yb[:, d, :, :].rearrange("p h v -> p (h v)"),
                                                                rows[:, :], start=True, stop=True), DBL)
                    if a2:
                        turn("z0", lambda o, d: nc.tensor.matmul(o[:, d * H:(d + 1) * H], aak[q][:, d, :], vd[:, d, :], start=True, stop=True), DBL)
                        pe.wait_ge(s_xt, ONE + (i + 2) * LEVELS)
                        for n in range(2):
                            turn(f"w{n}", lambda o, d: nc.tensor.matmul(o[:, d * P:(d + 1) * P], atm[:, 4 * n + d, :], xt[:, 4 * n + d, :],
                                                                        start=True, stop=True), 4)
                        t, k = job(i, "z0")
                        pe.wait_ge(s_read[t], ONE + k + 1)
                        turn("z", lambda o, d: nc.tensor.matmul(o[:, d * H:(d + 1) * H], xt[:, d, :], z0[:, d, :], start=True, stop=True), DBL)

                iterations(nc.tensor, body)


def phase_mix_out(nc, a, scr):
    ctx, sems = ExitStack(), []
    with ctx:
        def sb(name, shape, dt=F32):
            return ctx.enter_context(nc.sbuf_tensor("p3_" + name, shape, dt))

        def two(name, shape, dt=F32):
            return [sb(f"{name}{i}", shape, dt) for i in range(2)]

        def sem(name):
            sems.append(ctx.enter_context(nc.semaphore("p3_" + name)))
            return sems[-1]

        N = SEQ // P
        HALF = D_MODEL // TB
        w_raw = sb("w_raw", [P, KT, D_MODEL])
        w_hi = sb("w_hi", [P, KT, D_MODEL], F32R)
        w_lo = sb("w_lo", [P, KT, D_MODEL], F32R)
        m_raw = two("m_raw", [P, KT, P])
        m_hi = two("m_hi", [P, KT, P], F32R)
        m_lo = two("m_lo", [P, KT, P], F32R)
        x = two("x", [P, D_MODEL])
        hs = two("hs", [P, D_MODEL])
        xs = two("xs", [P, D_MODEL])
        sq = two("sq", [P, D_MODEL])
        h = two("h", [P, KT, P])
        h_hi = two("h_hi", [P, KT, P], F32R)
        h_lo = two("h_lo", [P, KT, P], F32R)
        gpost = sb("gpost", [P, D_MODEL])
        gain = sb("gain", [P, KT])
        ss = two("ss", [P, 2])
        rt = two("rt", [P, 4])
        eps = sb("eps", [P, 1])
        ident = sb("ident", [P, P])
        bank = ctx.enter_context(nc.psum_tensor("p3_bank", [P, 8, 512], F32))

        s_par = sem("params_loaded")
        s_const = sem("eps_written")
        s_w = [sem(f"w_loaded{k}") for k in range(KT)]
        s_wh = sem("w_hi_ready")
        s_wl = sem("w_lo_even_ready")
        s_wo = sem("w_lo_odd_ready")
        s_m = [sem(f"mix_loaded{i}") for i in range(2)]
        s_x = [sem(f"x_loaded{i}") for i in range(2)]
        s_mh = sem("mix_hi_ready")
        s_ml = sem("mix_lo_ready")
        s_op = sem("out_proj_done")
        s_sq = sem("squares_summed")
        s_rt = sem("rms_root")
        s_rc = sem("rms_recip")
        s_nm = sem("mixed_normed")
        s_x2 = sem("x_updated")
        s_xs = sem("x_scaled")
        s_tr = sem("transposed")
        s_h = sem("h_ready")
        s_sx = [sem(f"x_stored{i}") for i in range(2)]
        s_hh = sem("h_hi_ready")
        s_hl = sem("h_lo_ready")
        s_sh = [sem(f"h_hi_stored{i}") for i in range(2)]
        s_sl = [sem(f"h_lo_stored{i}") for i in range(2)]

        xv = a["x"][0].rearrange("(t p) d -> t p d", p=P)

        def tiles(eng, body):
            body(0, 0)
            body(1, 1)
            with eng.Fori(1, N // 2 - 1) as t2:
                body(t2 * 2, 0)
                body(t2 * 2 + 1, 1)
            body(N - 2, 0)
            body(N - 1, 1)

        def later(t):
            return not isinstance(t, int) or t > 1

        credit(nc, sems)
        with nc.Block() as block:
            @block.sync
            def _(sp):
                for k in range(KT):
                    sp.dma_start(w_raw[:, k, :], a["w_out"][0, k * P:(k + 1) * P, :]).then_inc(s_w[k], 16)
                    if k < 2:
                        sp.dma_start(m_raw[k][:, :, :], scr["mix"][:, :, k * P:(k + 1) * P]).then_inc(s_m[k], 16)
                    if k == 0:
                        with nc.allow_non_contiguous_dma(reason="per-feature parameters, once"):
                            sp.dma_start(gain[:, :], a["pre_ffn_norm"][0].rearrange("(t p) -> p t", p=P)).then_inc(s_par, 16)
                        sp.dma_start(gpost[:, :], a["post_mix_norm"][0].partition_broadcast(P)).then_inc(s_par, 16)
                        sp.dma_start(ident[:, :], const_view(a, "ident")).then_inc(s_par, 16)

                def body(t, p):
                    if not isinstance(t, int) or t < N - 2:
                        sp.wait_ge(s_mh, ONE + t + 1)
                        sp.wait_ge(s_ml, ONE + t + 1)
                        sp.dma_start(m_raw[p][:, :, :], scr["mix"][:, :, bass.ds(t * P + 2 * P, P)]).then_inc(s_m[p], 16)
                    if later(t):
                        sp.wait_ge(s_xs, ONE + t - 1)
                        sp.wait_ge(s_sx[p], ONE + (t - p) * 8)
                    sp.dma_start(x[p][:, :], xv[bass.ds(t, 1), :, :].rearrange("t p d -> p (t d)")).then_inc(s_x[p], 16)

                tiles(nc.sync, body)
                for p in range(2):
                    sp.wait_ge(s_sx[p], ONE + N * 8)
                    sp.wait_ge(s_sh[p], ONE + N * 8)
                    sp.wait_ge(s_sl[p], ONE + N * 8)

            @block.gpsimd
            def _(gp):
                nc.gpsimd.memset(eps[:, :], NORM_EPS).then_inc(s_const, 1)
                for k in range(KT):
                    if k % 2 == 0:
                        gp.wait_ge(s_wh, ONE + k + 1)
                        nc.gpsimd.tensor_tensor(w_lo[:, k, :], w_raw[:, k, :], w_hi[:, k, :].bitcast(F32), ALU.subtract).then_inc(s_wl, 1)
                    if k < 2:
                        gp.wait_ge(s_mh, ONE + k + 1)
                        nc.gpsimd.tensor_tensor(m_lo[k][:, :, :], m_raw[k][:, :, :], m_hi[k][:, :, :].bitcast(F32), ALU.subtract).then_inc(s_ml, 1)

                def low_h(t, p):
                    gp.wait_ge(s_hh, ONE + t + 1)
                    if later(t):
                        gp.wait_ge(s_sl[p], ONE + (t - p) * 8)
                    nc.gpsimd.tensor_tensor(h_lo[p][:, :, :], h[p][:, :, :], h_hi[p][:, :, :].bitcast(F32), ALU.subtract).then_inc(s_hl, 1)

                def body(t, p):
                    if not isinstance(t, int) or t < N - 2:
                        gp.wait_ge(s_mh, ONE + t + 3)
                        nc.gpsimd.tensor_tensor(m_lo[p][:, :, :], m_raw[p][:, :, :], m_hi[p][:, :, :].bitcast(F32), ALU.subtract).then_inc(s_ml, 1)
                    if not isinstance(t, int) or t > 0:
                        low_h(t - 1, 1 - p)

                tiles(nc.gpsimd, body)
                low_h(N - 1, 1)

            @block.scalar
            def _(act):
                def high_m(t, p):
                    act.wait_ge(s_m[p], ONE + (t - p) * 8 + 16)
                    if later(t):
                        act.wait_ge(s_op, ONE + t - 1)
                    nc.scalar.activation(m_hi[p][:, :, :], m_raw[p][:, :, :], ACT.Copy).then_inc(s_mh, 1)

                def high_h(t, p):
                    act.wait_ge(s_h, ONE + t + 1)
                    if later(t):
                        act.wait_ge(s_sh[p], ONE + (t - p) * 8)
                    nc.scalar.activation(h_hi[p][:, :, :], h[p][:, :, :], ACT.Copy).then_inc(s_hh, 1)
                    act.wait_ge(s_hh, ONE + t + 1)
                    act.dma_start(scr["h_hi"][:, :, bass.ds(t * P, P)], h_hi[p][:, :, :].bitcast(F32)).then_inc(s_sh[p], 16)

                def store_low(t, p):
                    act.wait_ge(s_hl, ONE + t + 1)
                    act.dma_start(scr["h_lo"][:, :, bass.ds(t * P, P)], h_lo[p][:, :, :].bitcast(F32)).then_inc(s_sl[p], 16)

                for k in range(KT):
                    act.wait_ge(s_w[k], ONE + 16)
                    nc.scalar.activation(w_hi[:, k, :], w_raw[:, k, :], ACT.Copy).then_inc(s_wh, 1)
                    if k < 2:
                        high_m(k, k)
                act.wait_ge(s_const, ONE + 1)

                def body(t, p):
                    act.wait_ge(s_op, ONE + t + 1)
                    if later(t):
                        act.wait_ge(s_rt, ONE + t * 2 - 2)
                    nc.scalar.activation(sq[p][:, :], bank[:, 2 * p:2 * p + 2, :].rearrange("p b d -> p (b d)"), ACT.Square,
                                         accum_out=ss[p][:, 0:1]).then_inc(s_sq, 1)
                    act.wait_ge(s_sq, ONE + t * 2 + 1)
                    nc.scalar.activation(rt[p][:, 0:1], ss[p][:, 0:1], ACT.Sqrt, scale=1.0 / D_MODEL, bias=eps[:, 0:1]).then_inc(s_rt, 1)
                    if not isinstance(t, int) or t < N - 2:
                        high_m(t + 2, p)
                    act.wait_ge(s_x2, ONE + t + 1)
                    nc.scalar.activation(sq[p][:, :], x[p][:, :], ACT.Square, accum_out=ss[p][:, 1:2]).then_inc(s_sq, 1)
                    act.wait_ge(s_sq, ONE + t * 2 + 2)
                    nc.scalar.activation(rt[p][:, 1:2], ss[p][:, 1:2], ACT.Sqrt, scale=1.0 / D_MODEL, bias=eps[:, 0:1]).then_inc(s_rt, 1)
                    act.wait_ge(s_rc, ONE + t * 2 + 2)
                    if later(t):
                        act.wait_ge(s_tr, ONE + t - 1)
                    nc.scalar.activation(xs[p][:, :], x[p][:, :], ACT.Copy, scale=rt[p][:, 3:4]).then_inc(s_xs, 1)
                    act.dma_start(scr["x2"][:, bass.ds(t, 1), :], x[p][:, :].rearrange("p (t d) -> p t d", t=1)).then_inc(s_sx[p], 16)
                    if later(t):
                        store_low(t - 2, p)
                    if not isinstance(t, int) or t > 0:
                        high_h(t - 1, 1 - p)

                tiles(nc.scalar, body)
                high_h(N - 1, 1)
                store_low(N - 2, 0)
                store_low(N - 1, 1)

            @block.vector
            def _(dve):
                for k in range(1, KT, 2):
                    dve.wait_ge(s_wh, ONE + k + 1)
                    nc.vector.tensor_tensor(w_lo[:, k, :], w_raw[:, k, :], w_hi[:, k, :].bitcast(F32), ALU.subtract).then_inc(s_wo, 1)
                dve.wait_ge(s_par, ONE + 48)

                def turn(t, p):
                    dve.wait_ge(s_tr, ONE + t + 1)
                    if later(t):
                        dve.wait_ge(s_hh, ONE + t - 1)
                        dve.wait_ge(s_hl, ONE + t - 1)
                    nc.vector.tensor_tensor(h[p][:, :, :], bank[:, 4 + 2 * p:6 + 2 * p, :].rearrange("p b (k t) -> p (b k) t", t=P),
                                            gain[:, :].unsqueeze(2).to_broadcast([P, KT, P]), ALU.mult).then_inc(s_h, 1)

                def body(t, p):
                    dve.wait_ge(s_rt, ONE + t * 2 + 1)
                    nc.vector.reciprocal(rt[p][:, 2:3], rt[p][:, 0:1]).then_inc(s_rc, 1)
                    dve.wait_ge(s_rc, ONE + t * 2 + 1)
                    nc.vector.scalar_tensor_tensor(hs[p][:, :], bank[:, 2 * p:2 * p + 2, :].rearrange("p b d -> p (b d)"), rt[p][:, 2:3],
                                                   gpost[:, :], ALU.mult, ALU.mult).then_inc(s_nm, 1)
                    dve.wait_ge(s_nm, ONE + t + 1)
                    dve.wait_ge(s_x[p], ONE + (t - p) * 8 + 16)
                    nc.vector.tensor_tensor(x[p][:, :], x[p][:, :], hs[p][:, :], ALU.add).then_inc(s_x2, 1)
                    if not isinstance(t, int) or t > 0:
                        turn(t - 1, 1 - p)
                    dve.wait_ge(s_rt, ONE + t * 2 + 2)
                    nc.vector.reciprocal(rt[p][:, 3:4], rt[p][:, 1:2]).then_inc(s_rc, 1)

                tiles(nc.vector, body)
                turn(N - 1, 1)

            @block.tensor
            def _(pe):
                pe.wait_ge(s_par, ONE + 48)

                def transposes(t, p):
                    pe.wait_ge(s_xs, ONE + t + 1)
                    if later(t):
                        pe.wait_ge(s_h, ONE + t - 1)
                    for k in range(KT):
                        last = nc.tensor.transpose(bank[:, 4 + 2 * p + k // 4, (k % 4) * P:(k % 4 + 1) * P], xs[p][:, k * P:(k + 1) * P], ident[:, :])
                    last.then_inc(s_tr, 1)

                def body(t, p):
                    pe.wait_ge(s_mh, ONE + t + 1)
                    pe.wait_ge(s_ml, ONE + t + 1)
                    if later(t):
                        pe.wait_ge(s_nm, ONE + t - 1)
                    for k in range(KT):
                        if isinstance(t, int) and t == 0:
                            pe.wait_ge(s_wh, ONE + k + 1)
                            pe.wait_ge(s_wo if k % 2 else s_wl, ONE + k // 2 + 1)
                        for n in range(HALF):
                            last = split_matmul(nc, bank[:, 2 * p + n, :], m_hi[p][:, k, :], m_lo[p][:, k, :],
                                                w_hi[:, k, n * TB:(n + 1) * TB], w_lo[:, k, n * TB:(n + 1) * TB], k == 0, k == KT - 1)
                    last.then_inc(s_op, 1)
                    if not isinstance(t, int) or t > 0:
                        transposes(t - 1, 1 - p)

                tiles(nc.tensor, body)
                transposes(N - 1, 1)


def phase_ffn(nc, a, scr, out):
    ctx, sems = ExitStack(), []
    with ctx:
        def sb(name, shape, dt=F32):
            return ctx.enter_context(nc.sbuf_tensor("p4_" + name, shape, dt))

        def two(name, shape, dt=F32):
            return [sb(f"{name}{i}", shape, dt) for i in range(2)]

        def sem(name):
            sems.append(ctx.enter_context(nc.semaphore("p4_" + name)))
            return sems[-1]

        HALF = D_MODEL // TB
        BANKS = TT * HALF
        TAPS = CONV_WIDTH + 1
        hT_hi = two("hT_hi", [P, KT, TB], F32R)
        hT_lo = two("hT_lo", [P, KT, TB], F32R)
        x = sb("x", [P, TT, D_MODEL])
        acc = sb("acc", [P, TT, D_MODEL])
        dump = sb("dump", [P, D_MODEL], mybir.dt.bfloat16)
        up_raw = two("up_raw", [P, 2, KT, P])
        up_hi = two("up_hi", [P, 2, KT, P], F32R)
        up_lo = two("up_lo", [P, 2, KT, P], F32R)
        dn_raw = two("dn_raw", [P, D_MODEL])
        dn_hi = two("dn_hi", [P, D_MODEL], F32R)
        dn_lo = two("dn_lo", [P, D_MODEL], F32R)
        ub = two("ub", [P, 2, 2 + TB])
        cv = two("cv", [P, 2, TB])
        ah = two("ah", [P, TB])
        a_hi = two("a_hi", [P, TB], F32R)
        a_lo = two("a_lo", [P, TB], F32R)
        cpar = two("cpar", [P, 2, TAPS])
        cw = sb("cw", [P, 2, FF, TAPS])
        tail = sb("tail", [P, 2, FF, 2])
        gffn = sb("gffn", [P, D_MODEL])
        ss = sb("ss", [P, TT])
        rstd = sb("rstd", [P, TT])
        eps = sb("eps", [P, 1])
        cw_rows = acc[0:2 * FF, 0, 0:TAPS * P].rearrange("q (t p) -> q t p", p=P)
        ident = acc[:, 1, 0:P]
        bank = ctx.enter_context(nc.psum_tensor("p4_bank", [P, 8, 512], F32))
        cw_bank = bank[:, 4, 0:TAPS * 2 * FF].rearrange("p (t s f) -> p s f t", s=2, f=FF)

        s_par = sem("params_loaded")
        s_const = sem("zeros_written")
        s_cwt = sem("taps_transposed")
        s_cw = sem("taps_ready")
        s_h = [[sem(f"h_loaded{i}{half}") for half in range(2)] for i in range(2)]
        s_x = sem("x_loaded")
        s_up = [sem(f"up_loaded{i}") for i in range(2)]
        s_dn = [sem(f"dn_loaded{i}") for i in range(2)]
        s_uh = sem("up_hi_ready")
        s_ul = sem("up_lo_ready")
        s_dh = sem("dn_hi_ready")
        s_dl = sem("dn_lo_ready")
        s_sq = sem("squares_summed")
        s_rt = sem("rms_root")
        s_rc = sem("rms_recip")
        s_upd = sem("up_done")
        s_tl = sem("tail_used")
        s_ub = sem("up_read")
        s_tap = sem("tap_bias")
        s_cv1 = sem("conv_tap")
        s_cv = sem("conv_done")
        s_gl = sem("gelu_done")
        s_a = sem("hidden_ready")
        s_ah = sem("hidden_hi_ready")
        s_al = sem("hidden_lo_ready")
        s_db = sem("down_bank_done")
        s_acc = sem("down_bank_added")
        s_nm = sem("output_normed")
        s_fin = sem("tile_ready")
        s_out = sem("block_stored")

        upv = a["w_up"][0].rearrange("(k p) (s n) -> p s k n", p=P, s=2)
        ov = out[0].rearrange("(t p) d -> p t d", p=P)
        NPAR = TAPS + 2

        def stream(eng, body):
            for b in range(BLOCKS):
                body(b, 0)
                body(b, 1)
                with eng.Fori(2, GROUPS - 1) as g:
                    body(b, g)
                body(b, GROUPS - 1)

        def at(b, g, s):
            return g * GROUP + (b * FF + s)

        def following(b, g):
            if isinstance(g, int) and g == GROUPS - 1:
                return (b + 1, 0) if b < BLOCKS - 1 else None
            return b, g + 1

        def preceding(b, g):
            if isinstance(g, int) and g == 0:
                return (b - 1, GROUPS - 1) if b > 0 else None
            return b, g - 1

        def slot_free(eng, n, *sems):
            if not isinstance(n, int) or n >= 2:
                for s in sems:
                    eng.wait_ge(s, ONE + n - 1)

        credit(nc, sems)
        with nc.Block() as block:
            @block.sync
            def _(sp):
                def load_up(b, g, s):
                    slot_free(sp, at(b, g, s), s_uh, s_ul)
                    for i in range(2):
                        sp.dma_start(up_raw[s][:, i, :, :], upv[:, i, :, bass.ds(g * (GROUP * P) + s * P, P)]).then_inc(s_up[s], 16)

                def load_dn(b, g, s):
                    slot_free(sp, at(b, g, s), s_dh, s_dl)
                    sp.dma_start(dn_raw[s][:, :], a["w_down"][0, bass.ds(g * (GROUP * P) + s * P, P), :]).then_inc(s_dn[s], 16)

                def load_h(b, half):
                    if b >= 2:
                        sp.wait_ge(s_upd, ONE + (b - 1) * FF)
                    k = slice(half * KT // 2, (half + 1) * KT // 2)
                    for dst, key in ((hT_hi, "h_hi"), (hT_lo, "h_lo")):
                        sp.dma_start(dst[b % 2][:, k, :].bitcast(F32), scr[key][:, k, b * TB:(b + 1) * TB]).then_inc(s_h[b % 2][half], 16)

                def store(b):
                    for t in range(0, TT, 2):
                        sp.wait_ge(s_fin, ONE + b * TT + t + 2)
                        sp.dma_start(ov[:, b * TT + t:b * TT + t + 2, :], x[:, t:t + 2, :]).then_inc(s_out, 16)

                load_up(0, 0, 0)
                load_h(0, 0)
                load_h(0, 1)
                load_up(0, 0, 1)
                for tap in range(CONV_WIDTH):
                    sp.dma_start(cw_rows[:, tap, :], a["conv_w"][0, tap].rearrange("(q p) -> q p", p=P)).then_inc(s_par, 16)
                sp.dma_start(cw_rows[:, CONV_WIDTH, :], a["conv_b"][0].rearrange("(q p) -> q p", p=P)).then_inc(s_par, 16)
                sp.dma_start(ident, const_view(a, "ident")).then_inc(s_par, 16)
                sp.dma_start(gffn[:, :], a["post_ffn_norm"][0].partition_broadcast(P)).then_inc(s_par, 16)

                def group(b, g):
                    after = following(b, g)
                    if after:
                        load_up(*after, 0)
                    for s in range(GROUP):
                        load_dn(b, g, s)
                    if after:
                        load_up(*after, 1)
                    if isinstance(g, int) and g == 0 and b < BLOCKS - 1:
                        load_h(b + 1, 0)
                    if isinstance(g, int) and g == 1 and b > 0:
                        store(b - 1)
                    if isinstance(g, int) and g == GROUPS - 1:
                        if b < BLOCKS - 1:
                            load_h(b + 1, 1)
                        if b > 0:
                            sp.wait_ge(s_out, ONE + b * (TT // 2 * 16))
                        sp.dma_start(x[:, :, :], scr["x2"][:, b * TT:(b + 1) * TT, :]).then_inc(s_x, 16)

                stream(nc.sync, group)
                store(BLOCKS - 1)
                sp.wait_ge(s_out, ONE + TT // 2 * 16 * BLOCKS)

            @block.gpsimd
            def _(gp):
                nc.gpsimd.memset(eps[:, :], NORM_EPS)
                nc.gpsimd.memset(tail[:, :, :, :], 0.0).then_inc(s_const, 1)

                def low_up(b, g, s):
                    gp.wait_ge(s_uh, ONE + at(b, g, s) + 1)
                    nc.gpsimd.tensor_tensor(up_lo[s][:, :, :, :], up_raw[s][:, :, :, :], up_hi[s][:, :, :, :].bitcast(F32),
                                            ALU.subtract).then_inc(s_ul, 1)

                def low_dn(b, g, s):
                    gp.wait_ge(s_dh, ONE + at(b, g, s) + 1)
                    nc.gpsimd.tensor_tensor(dn_lo[s][:, :], dn_raw[s][:, :], dn_hi[s][:, :].bitcast(F32),
                                            ALU.subtract).then_inc(s_dl, 1)

                def group(b, g):
                    after = following(b, g)
                    if after:
                        low_up(*after, 0)
                    for s in range(GROUP):
                        low_dn(b, g, s)
                    if after:
                        low_up(*after, 1)

                for s in range(GROUP):
                    low_up(0, 0, s)
                stream(nc.gpsimd, group)

            @block.scalar
            def _(act):
                def high_up(b, g, s):
                    act.wait_ge(s_up[s], ONE + g * 32 + (b * GROUPS * 32 + 32))
                    nc.scalar.activation(up_hi[s][:, :, :, :], up_raw[s][:, :, :, :], ACT.Copy).then_inc(s_uh, 1)

                def high_dn(b, g, s):
                    act.wait_ge(s_dn[s], ONE + g * 16 + (b * GROUPS * 16 + 16))
                    nc.scalar.activation(dn_hi[s][:, :], dn_raw[s][:, :], ACT.Copy).then_inc(s_dh, 1)

                def read_up(b, g, s):
                    n, f = at(b, g, s), g * GROUP + s
                    act.wait_ge(s_upd, ONE + n + 1)
                    slot_free(act, n, s_a)
                    nc.scalar.activation(ub[s][:, :, 2:2 + TB], bank[:, 2 * s:2 * s + 2, :], ACT.Copy).then_inc(s_ub, 1)
                    nc.scalar.activation(ub[s][:, :, 0:2], tail[:, :, bass.ds(f, 1), :].rearrange("p s f t -> p s (f t)"), ACT.Copy)
                    nc.scalar.activation(cpar[s][:, :, :], cw[:, :, bass.ds(f, 1), :].rearrange("p s f t -> p s (f t)"),
                                         ACT.Copy).then_inc(s_tl, 1)

                def taps(b, g, s):
                    n, f = at(b, g, s), g * GROUP + s
                    act.wait_ge(s_ub, ONE + n + 1)
                    act.wait_ge(s_tl, ONE + n + 1)
                    for i in range(2):
                        last = nc.scalar.activation(cv[s][:, i, :], ub[s][:, i, 2:2 + TB], ACT.Identity,
                                                    scale=cpar[s][:, i, 2:3], bias=cpar[s][:, i, 3:4])
                    last.then_inc(s_tap, 1)
                    nc.scalar.activation(tail[:, :, bass.ds(f, 1), :].rearrange("p s f t -> p s (f t)"), ub[s][:, :, TB:TB + 2], ACT.Copy)

                def gelu(b, g, s):
                    act.wait_ge(s_cv, ONE + at(b, g, s) + 1)
                    nc.scalar.activation(cv[s][:, 0, :], cv[s][:, 0, :], ACT.Gelu_apprx_tanh).then_inc(s_gl, 1)

                def high_a(b, g, s):
                    act.wait_ge(s_a, ONE + at(b, g, s) + 1)
                    nc.scalar.activation(a_hi[s][:, :], ah[s][:, :], ACT.Copy).then_inc(s_ah, 1)

                def norm(b):
                    for t in range(TT):
                        act.wait_ge(s_acc, ONE + (b + 1) * GROUPS * BANKS - BANKS + (t + 1) * HALF)
                        if b * TT + t:
                            act.wait_ge(s_sq, ONE + b * TT + t)
                        nc.scalar.activation(dump[:, :], acc[:, t, :], ACT.Square, accum_out=ss[:, t:t + 1]).then_inc(s_sq, 1)
                    act.wait_ge(s_sq, ONE + b * TT + TT)
                    nc.scalar.activation(rstd[:, :], ss[:, :], ACT.Sqrt, scale=1.0 / D_MODEL, bias=eps[:, 0:1]).then_inc(s_rt, 1)

                def group(b, g):
                    after, before = following(b, g), preceding(b, g)
                    read_up(b, g, 0)
                    taps(b, g, 0)
                    if after:
                        high_up(*after, 0)
                    gelu(b, g, 0)
                    if before:
                        act.wait_ge(s_db, ONE + g * BANKS + b * (GROUPS * BANKS))
                    for s in range(GROUP):
                        high_dn(b, g, s)
                    high_a(b, g, 0)
                    if isinstance(g, int) and g == 0 and b > 0:
                        norm(b - 1)
                    read_up(b, g, 1)
                    taps(b, g, 1)
                    if after:
                        high_up(*after, 1)
                    gelu(b, g, 1)
                    high_a(b, g, 1)

                for s in range(GROUP):
                    high_up(0, 0, s)
                act.wait_ge(s_const, ONE + 1)
                act.wait_ge(s_cw, ONE + 1)
                stream(nc.scalar, group)
                norm(BLOCKS - 1)

            @block.vector
            def _(dve):
                dve.wait_ge(s_cwt, ONE + 1)
                nc.vector.tensor_copy(cw[:, :, :, :], cw_bank).then_inc(s_cw, 1)
                dve.wait_ge(s_par, ONE + 16 * NPAR)

                def conv(b, g, s):
                    n = at(b, g, s)
                    dve.wait_ge(s_tap, ONE + n + 1)
                    for i in range(2):
                        nc.vector.scalar_tensor_tensor(cv[s][:, i, :], ub[s][:, i, 1:1 + TB], cpar[s][:, i, 1:2],
                                                       cv[s][:, i, :], ALU.mult, ALU.add).then_inc(s_cv1, 1)
                    for i in range(2):
                        dve.wait_ge(s_cv1, ONE + n * 2 + i + 1)
                        last = nc.vector.scalar_tensor_tensor(cv[s][:, i, :], ub[s][:, i, 0:TB], cpar[s][:, i, 0:1],
                                                              cv[s][:, i, :], ALU.mult, ALU.add)
                    last.then_inc(s_cv, 1)

                def hidden(b, g, s):
                    n = at(b, g, s)
                    dve.wait_ge(s_gl, ONE + n + 1)
                    slot_free(dve, n, s_al)
                    nc.vector.tensor_tensor(ah[s][:, :], cv[s][:, 0, :], cv[s][:, 1, :], ALU.mult).then_inc(s_a, 1)

                def low_a(b, g, s):
                    n = at(b, g, s)
                    dve.wait_ge(s_ah, ONE + n + 1)
                    nc.vector.tensor_tensor(a_lo[s][:, :], ah[s][:, :], a_hi[s][:, :].bitcast(F32), ALU.subtract).then_inc(s_al, 1)

                def add_down(bg, banks):
                    if bg is None:
                        return
                    b, g = bg
                    start = isinstance(g, int) and g == 0
                    for n in banks:
                        c = g * BANKS + (b * GROUPS * BANKS + n)
                        dve.wait_ge(s_db, ONE + c + 1)
                        dst = acc[:, n // HALF, (n % HALF) * TB:(n % HALF + 1) * TB]
                        if start:
                            nc.vector.tensor_copy(dst, bank[:, 4 + n % 4, :]).then_inc(s_acc, 1)
                        else:
                            dve.wait_ge(s_acc, ONE + c - (BANKS - 1))
                            nc.vector.tensor_tensor(dst, bank[:, 4 + n % 4, :], dst, ALU.add).then_inc(s_acc, 1)

                def scale(b):
                    dve.wait_ge(s_rt, ONE + b + 1)
                    dve.wait_ge(s_x, ONE + b * 16 + 16)
                    nc.vector.reciprocal(rstd[:, :], rstd[:, :]).then_inc(s_rc, 1)
                    dve.wait_ge(s_rc, ONE + b + 1)

                def output(b, tiles):
                    for t in tiles:
                        nc.vector.scalar_tensor_tensor(acc[:, t, :], acc[:, t, :], rstd[:, t:t + 1], gffn[:, :],
                                                       ALU.mult, ALU.mult).then_inc(s_nm, 1)
                        dve.wait_ge(s_nm, ONE + b * TT + t + 1)
                        nc.vector.tensor_tensor(x[:, t, :], x[:, t, :], acc[:, t, :], ALU.add).then_inc(s_fin, 1)

                def group(b, g):
                    before = preceding(b, g)
                    last = isinstance(g, int) and g == 0 and b > 0
                    if isinstance(g, int) and g == 1 and b > 0:
                        dve.wait_ge(s_fin, ONE + b * TT)
                    add_down(before, (0, 1))
                    conv(b, g, 0)
                    add_down(before, (2, 3))
                    hidden(b, g, 0)
                    add_down(before, (4, 5, 6, 7))
                    low_a(b, g, 0)
                    if last:
                        scale(b - 1)
                        output(b - 1, (0, 1))
                    conv(b, g, 1)
                    hidden(b, g, 1)
                    low_a(b, g, 1)
                    if last:
                        output(b - 1, (2, 3))

                stream(nc.vector, group)
                add_down((BLOCKS - 1, GROUPS - 1), range(BANKS))
                dve.wait_ge(s_acc, ONE + BLOCKS * GROUPS * BANKS)
                scale(BLOCKS - 1)
                output(BLOCKS - 1, range(TT))

            @block.tensor
            def _(pe):
                def up(b, g, s):
                    n = at(b, g, s)
                    pe.wait_ge(s_uh, ONE + n + 1)
                    pe.wait_ge(s_ul, ONE + n + 1)
                    slot_free(pe, n, s_ub)
                    for i in range(2):
                        for k in range(KT):
                            if isinstance(g, int) and g == 0 and s == 0 and i == 0 and k % (KT // 2) == 0:
                                pe.wait_ge(s_h[b % 2][k // (KT // 2)], ONE + b // 2 * 32 + 32)
                            last = split_matmul(nc, bank[:, 2 * s + i, :], up_hi[s][:, i, k, :], up_lo[s][:, i, k, :],
                                                hT_hi[b % 2][:, k, :], hT_lo[b % 2][:, k, :], k == 0, k == KT - 1)
                    last.then_inc(s_upd, 1)

                def down(bg):
                    if bg is None:
                        return
                    b, g = bg
                    ready = at(b, g, 0) + GROUP
                    pe.wait_ge(s_dh, ONE + ready)
                    pe.wait_ge(s_dl, ONE + ready)
                    pe.wait_ge(s_al, ONE + ready)
                    for n in range(BANKS):
                        t, h = n // HALF, n % HALF
                        c = g * BANKS + (b * GROUPS * BANKS + n)
                        if not isinstance(c, int) or c >= 4:
                            pe.wait_ge(s_acc, ONE + c - 3)
                        for s in range(GROUP):
                            last = split_matmul(nc, bank[:, 4 + n % 4, :], a_hi[s][:, t * P:(t + 1) * P], a_lo[s][:, t * P:(t + 1) * P],
                                                dn_hi[s][:, h * TB:(h + 1) * TB], dn_lo[s][:, h * TB:(h + 1) * TB],
                                                s == 0, s == GROUP - 1)
                        last.then_inc(s_db, 1)

                def group(b, g):
                    up(b, g, 0)
                    if isinstance(g, int) and g == 0 and b == 0:
                        pe.wait_ge(s_par, ONE + 16 * NPAR)
                        for tap in range(TAPS):
                            last = nc.tensor.transpose(bank[:, 4, tap * 2 * FF:(tap + 1) * 2 * FF], cw_rows[:, tap, :], ident[0:2 * FF, 0:2 * FF])
                        last.then_inc(s_cwt, 1)
                    down(preceding(b, g))
                    up(b, g, 1)

                stream(nc.tensor, group)
                down((BLOCKS - 1, GROUPS - 1))


_INS = ['x', 'pre_mix_norm', 'w_in', 'mu_shift', 'w0', 'w_decay_up', 'a0', 'w_aaa_up', 'w_gate_up', 'k_k', 'k_a', 'r_k',
        'ln_x_w', 'ln_x_b', 'w_pool', 'pool_scale', 'w_out', 'post_mix_norm', 'pre_ffn_norm', 'w_up', 'conv_w', 'conv_b',
        'w_down', 'post_ffn_norm']

def build(nc, a, out):
    def scratch(name, shape):
        return nc.dram_tensor("scratch_" + name, shape, F32).ap()

    with ExitStack() as ctx:
        pend = ctx.enter_context(nc.sbuf_tensor("chunk_decay", [P, PAIRS, SEQ // C], F32))
        scr = {k: scratch(k, (P, PAIRS, SEQ)) for k in ("rt", "at", "bt", "kt", "v", "bonus", "g")}
        scr["mix"] = scratch("mix", (P, 2 * PAIRS, SEQ))
        scr["h_hi"] = scratch("h_hi", (P, KT, SEQ))
        scr["h_lo"] = scratch("h_lo", (P, KT, SEQ))
        scr["x2"] = scratch("x2", (P, SEQ // P, D_MODEL))
        scr["pend"] = pend
        phase_project(nc, a, scr)
        phase_recur(nc, a, scr)
        phase_mix_out(nc, a, scr)
        phase_ffn(nc, a, scr, out)


def kernel(**inputs):
    import concourse.bacc as bacc
    from concourse.bass_utils import run_bass_kernel_spmd

    nc = bacc.Bacc("TRN2", target_bir_lowering=False, num_devices=1)
    arrays = {"in_" + k: np.ascontiguousarray(inputs[k]) for k in _INS}
    arrays["in_consts"] = constants()
    a = {k[3:]: nc.dram_tensor(k, v.shape, mybir.dt.from_np(v.dtype), kind="ExternalInput").ap() for k, v in arrays.items()}
    out = nc.dram_tensor("out", (1, SEQ, D_MODEL), F32, kind="ExternalOutput").ap()
    build(nc, a, out)
    r = run_bass_kernel_spmd(nc, [arrays], core_ids=[0])
    return r.results[0]["out"]
```
